# Optimizing a Trainium2 kernel written in Bass

```python
import math
import jax
import jax.numpy as jnp
from jax import lax
import numpy as np

D_MODEL = 1024
BATCH = 1
SEQ = 512
DEPTH = 1

CTX_LEN = 256
GRID_W = 64
A_HEADS = 8
A_DH = 64
A_DV = 2 * A_DH
A_WIDTH = A_HEADS * A_DV
H_HEADS = 8
H_DK = 128
H_DV = 128
H_WIDTH = H_HEADS * H_DV
CHUNK = 64
Q_BLOCK = 128
ROPE_BASE = 10000.0
EPS = 1e-6

IN_COLS = (
    ("attn_k", A_HEADS * 2 * A_DH),
    ("attn_v", A_WIDTH),
    ("hgrn_i", H_WIDTH),
    ("hgrn_f_fwd", H_HEADS * H_DK),
    ("hgrn_f_bwd", H_HEADS * H_DK),
    ("attn_q", A_HEADS * 2 * A_DH),
    ("hgrn_q", H_HEADS * H_DK),
    ("attn_z", A_WIDTH),
    ("hgrn_z", H_WIDTH),
    ("merge_gate", 2 * D_MODEL),
)
IN_WIDTH = (4 * A_HEADS * A_DH + A_WIDTH + H_WIDTH + 3 * H_HEADS * H_DK
            + A_WIDTH + H_WIDTH + 2 * D_MODEL)

kernel_name = "hybrid_diffattn_hgrn2_dit_layer"

def _rms(u, gain):
    uf = u.astype(jnp.float32)
    y = uf * lax.rsqrt(jnp.mean(uf * uf, axis=-1, keepdims=True) + EPS)
    return (y * gain.astype(jnp.float32)).astype(u.dtype)

def _cols(w, name):
    start = 0
    for n, width in IN_COLS:
        if n == name:
            return w[:, start:start + width]
        start += width
    raise KeyError(name)

def _axial_rope(n_tok):
    rows = n_tok // GRID_W
    row = jnp.repeat(jnp.arange(rows, dtype=jnp.float32), GRID_W)
    col = jnp.tile(jnp.arange(GRID_W, dtype=jnp.float32), rows)
    half = A_DH // 2
    inv = ROPE_BASE ** (-jnp.arange(0, half, 2, dtype=jnp.float32) / half)
    ar = row[:, None] * inv[None, :]
    ac = col[:, None] * inv[None, :]
    ang = jnp.concatenate([ar, ar, ac, ac], axis=-1)
    return jnp.cos(ang), jnp.sin(ang)

def _rotate_half_axial(u):
    ur, uc = jnp.split(u, 2, axis=-1)
    r1, r2 = jnp.split(ur, 2, axis=-1)
    c1, c2 = jnp.split(uc, 2, axis=-1)
    return jnp.concatenate([-r2, r1, -c2, c1], axis=-1)

def _apply_rope(u, cos, sin):
    return (u * cos + _rotate_half_axial(u) * sin).astype(u.dtype)

def _qk_heads(p, gain):
    B, T, _ = p.shape
    u = _rms(p.reshape(B, T, A_HEADS, 2, A_DH), gain)
    return u.transpose(0, 2, 3, 1, 4)

def _v_heads(p):
    B, T, _ = p.shape
    return p.reshape(B, T, A_HEADS, A_DV).transpose(0, 2, 1, 3)

def _diff_attention(q, k, v, lam):
    B, H, _, T, dh = q.shape
    nb = T // Q_BLOCK
    qb = q.reshape(B, H, 2, nb, Q_BLOCK, dh).transpose(3, 0, 1, 2, 4, 5)

    def block(qblk):
        s = jnp.einsum("bhmqd,bhmkd->bhmqk", qblk, k).astype(jnp.float32)
        p = jax.nn.softmax(s, axis=-1)
        w = p[:, :, 0] - lam * p[:, :, 1]
        return jnp.einsum("bhqk,bhkd->bhqd", w.astype(v.dtype), v)

    o = lax.map(block, qb)
    return o.transpose(1, 0, 3, 2, 4).reshape(B, T, H, A_DV)

def _lower_bound(p, l):
    return jnp.cumsum(jax.nn.softmax(p.astype(jnp.float32), axis=0), axis=0)[l]

def _log_forget(a, lb):
    B, T, _ = a.shape
    f = lb + (1.0 - lb) * jax.nn.sigmoid(a.astype(jnp.float32))
    return jnp.log(f).reshape(B, T, H_HEADS, H_DK)

def _hgrn2_scan(q, log_f, v, s0):
    B, T, H, _ = log_f.shape
    n = T // CHUNK

    def chunks(u):
        return u.astype(jnp.float32).reshape(B, n, CHUNK, H, u.shape[-1]).transpose(1, 0, 3, 2, 4)

    k = -jnp.expm1(log_f.astype(jnp.float32))
    xs = (chunks(log_f), chunks(k), chunks(v))
    if q is not None:
        xs = xs + (chunks(q),)
    mask = jnp.tril(jnp.ones((CHUNK, CHUNK), dtype=bool))[:, :, None]

    def step(S, inp):
        g, kk, vv = inp[:3]
        b = jnp.cumsum(g, axis=2)
        b_end = b[:, :, -1:, :]
        S_new = (jnp.exp(b_end[:, :, 0, :])[..., None] * S
                 + jnp.einsum("bhsk,bhsv->bhkv", kk * jnp.exp(b_end - b), vv))
        if q is None:
            return S_new, None
        qq = inp[3]
        decay = jnp.exp(jnp.where(mask, b[:, :, :, None, :] - b[:, :, None, :, :], -jnp.inf))
        scores = jnp.einsum("bhtk,bhtsk,bhsk->bhts", qq, decay, kk)
        o = (jnp.einsum("bhts,bhsv->bhtv", scores, vv)
             + jnp.einsum("bhtk,bhkv->bhtv", qq * jnp.exp(b), S))
        return S_new, o

    S_fin, o = lax.scan(step, s0, xs)
    if q is None:
        return None, S_fin
    return o.transpose(1, 0, 3, 2, 4).reshape(B, T, H, H_DV), S_fin

def _hgrn2_bidir(q_lat, f_lat, b_lat, v_lat, q_ctx, f_ctx, b_ctx, v_ctx):
    B = v_lat.shape[0]
    s0 = jnp.zeros((B, H_HEADS, H_DK, H_DV), jnp.float32)
    flip = lambda u: jnp.flip(u, axis=1)
    o_cf, s_f = _hgrn2_scan(q_ctx, f_ctx, v_ctx, s0)
    o_cb, s_b = _hgrn2_scan(None if q_ctx is None else flip(q_ctx), flip(b_ctx), flip(v_ctx), s0)
    o_lf, _ = _hgrn2_scan(q_lat, f_lat, v_lat, s_f)
    o_lb, _ = _hgrn2_scan(flip(q_lat), flip(b_lat), flip(v_lat), s_b)
    o_ctx = None if q_ctx is None else o_cf + flip(o_cb)
    return o_lf + flip(o_lb), o_ctx

def _merge(h, W, o_attn, o_hgrn, lam_init, subln_g, hgrn_g, w_ba, w_bh, w_o):
    B, T, _ = h.shape
    ya = (_rms(o_attn, subln_g) * (1.0 - lam_init)).reshape(B, T, A_WIDTH) * jax.nn.silu(h @ _cols(W, "attn_z"))
    yh = _rms(o_hgrn.astype(h.dtype), hgrn_g).reshape(B, T, H_WIDTH) * jax.nn.silu(h @ _cols(W, "hgrn_z"))
    g_a, g_h = jnp.split(jax.nn.sigmoid(h @ _cols(W, "merge_gate")), 2, axis=-1)
    return (g_a * (ya @ w_ba) + g_h * (yh @ w_bh)) @ w_o

def setup_inputs(seed: int = 0) -> dict:
    key = jax.random.key(seed)
    ks = jax.random.split(key, 24)
    D = D_MODEL

    def nrm(k, shape, s):
        return jax.random.normal(k, shape, jnp.float32) * s

    return {
        "x": nrm(ks[0], (BATCH, SEQ, D), 1.0),
        "c": nrm(ks[1], (BATCH, D), 1.0),
        "ctx": nrm(ks[2], (BATCH, CTX_LEN, D), 1.0),
        "c_ctx": nrm(ks[3], (D,), 1.0),
        "w_mod": nrm(ks[4], (DEPTH, D, 3 * D), D ** -0.5),
        "b_mod": nrm(ks[5], (DEPTH, 3 * D), 0.02),
        "norm_gain": 1.0 + nrm(ks[6], (DEPTH, D), 0.02),
        "w_in": nrm(ks[7], (DEPTH, D, IN_WIDTH), D ** -0.5),
        "q_norm_gain": 1.0 + nrm(ks[8], (DEPTH, A_DH), 0.02),
        "k_norm_gain": 1.0 + nrm(ks[9], (DEPTH, A_DH), 0.02),
        "lambda_q1": nrm(ks[10], (DEPTH, A_DH), 0.1),
        "lambda_k1": nrm(ks[11], (DEPTH, A_DH), 0.1),
        "lambda_q2": nrm(ks[12], (DEPTH, A_DH), 0.1),
        "lambda_k2": nrm(ks[13], (DEPTH, A_DH), 0.1),
        "subln_gain": 1.0 + nrm(ks[14], (DEPTH, A_DV), 0.02),
        "hgrn_lb_fwd": nrm(ks[15], (DEPTH + 1, H_HEADS * H_DK), 0.5),
        "hgrn_lb_bwd": nrm(ks[16], (DEPTH + 1, H_HEADS * H_DK), 0.5),
        "hgrn_norm_gain": 1.0 + nrm(ks[17], (DEPTH, H_DV), 0.02),
        "w_br_attn": nrm(ks[18], (DEPTH, A_WIDTH, D), A_WIDTH ** -0.5),
        "w_br_hgrn": nrm(ks[19], (DEPTH, H_WIDTH, D), H_WIDTH ** -0.5),
        "w_out": nrm(ks[20], (DEPTH, D, D), D ** -0.5),
    }

def reference(x, c, ctx, c_ctx, w_mod, b_mod, norm_gain, w_in, q_norm_gain, k_norm_gain,
              lambda_q1, lambda_k1, lambda_q2, lambda_k2, subln_gain, hgrn_lb_fwd, hgrn_lb_bwd,
              hgrn_norm_gain, w_br_attn, w_br_hgrn, w_out):
    B, T, _ = x.shape
    Lc = ctx.shape[1]
    cos, sin = _axial_rope(T)
    q_scale = A_DH ** -0.5
    f32 = jnp.float32
    for l in range(DEPTH):
        last = l == DEPTH - 1
        W = w_in[l]
        lam_init = 0.8 - 0.6 * math.exp(-0.3 * l)
        mod = jax.nn.silu(c) @ w_mod[l] + b_mod[l]
        shift, scale, gate = jnp.split(mod[:, None, :], 3, axis=-1)
        mod_c = jax.nn.silu(c_ctx) @ w_mod[l] + b_mod[l]
        shift_c, scale_c, gate_c = jnp.split(mod_c, 3, axis=-1)
        h = _rms(x, norm_gain[l]) * (1.0 + scale) + shift
        hc = _rms(ctx, norm_gain[l]) * (1.0 + scale_c) + shift_c

        lam = (jnp.exp(jnp.sum(lambda_q1[l].astype(f32) * lambda_k1[l].astype(f32)))
               - jnp.exp(jnp.sum(lambda_q2[l].astype(f32) * lambda_k2[l].astype(f32))) + lam_init)
        k_c = _qk_heads(hc @ _cols(W, "attn_k"), k_norm_gain[l])
        v_c = _v_heads(hc @ _cols(W, "attn_v"))
        q_l = _apply_rope(_qk_heads(h @ _cols(W, "attn_q"), q_norm_gain[l]), cos, sin) * q_scale
        k_l = _apply_rope(_qk_heads(h @ _cols(W, "attn_k"), k_norm_gain[l]), cos, sin)
        v_l = _v_heads(h @ _cols(W, "attn_v"))
        o_a = _diff_attention(q_l, jnp.concatenate([k_c, k_l], axis=3),
                              jnp.concatenate([v_c, v_l], axis=2), lam)

        lb_f = _lower_bound(hgrn_lb_fwd, l)
        lb_b = _lower_bound(hgrn_lb_bwd, l)
        q_h = jax.nn.silu(h @ _cols(W, "hgrn_q")).reshape(B, T, H_HEADS, H_DK)
        f_l = _log_forget(h @ _cols(W, "hgrn_f_fwd"), lb_f)
        b_l = _log_forget(h @ _cols(W, "hgrn_f_bwd"), lb_b)
        v_hl = (h @ _cols(W, "hgrn_i")).reshape(B, T, H_HEADS, H_DV)
        f_c = _log_forget(hc @ _cols(W, "hgrn_f_fwd"), lb_f)
        b_c = _log_forget(hc @ _cols(W, "hgrn_f_bwd"), lb_b)
        v_hc = (hc @ _cols(W, "hgrn_i")).reshape(B, Lc, H_HEADS, H_DV)
        q_hc = None if last else jax.nn.silu(hc @ _cols(W, "hgrn_q")).reshape(B, Lc, H_HEADS, H_DK)
        o_h, o_hc = _hgrn2_bidir(q_h, f_l, b_l, v_hl, q_hc, f_c, b_c, v_hc)

        y = _merge(h, W, o_a, o_h, lam_init, subln_gain[l], hgrn_norm_gain[l],
                   w_br_attn[l], w_br_hgrn[l], w_out[l])
        if not last:
            q_c = _qk_heads(hc @ _cols(W, "attn_q"), q_norm_gain[l]) * q_scale
            o_ac = _diff_attention(q_c, k_c, v_c, lam)
            ctx = ctx + gate_c * _merge(hc, W, o_ac, o_hc, lam_init, subln_gain[l], hgrn_norm_gain[l],
                                        w_br_attn[l], w_br_hgrn[l], w_out[l])
        x = x + gate * y
    return x


_drawn_inputs = setup_inputs


def setup_inputs(seed=0):
    import zlib

    import numpy as np

    out = dict(_drawn_inputs(seed))
    spreads = {}
    factors = {'b_mod': 3.099,
     'norm_gain': 7.153,
     'q_norm_gain': 8.0,
     'k_norm_gain': 8.0,
     'lambda_q1': 8.0,
     'lambda_q2': 4.428,
     'subln_gain': 8.0,
     'hgrn_lb_fwd': 8.0,
     'hgrn_lb_bwd': 8.0,
     'hgrn_norm_gain': 8.0}
    for name, (base, spread) in spreads.items():
        noise = np.random.default_rng([zlib.crc32(name.encode()), seed]).standard_normal(out[name].shape)
        drawn = base * np.exp(spread * noise) if base else spread * noise
        out[name] = jnp.asarray(drawn.astype(out[name].dtype))
    for name, factor in factors.items():
        out[name] = (out[name] * factor).astype(out[name].dtype)
    return out
```

```python
from contextlib import ExitStack

import concourse.bass as bass
from concourse import mybir

F32 = mybir.dt.float32
F32R = mybir.dt.float32r
I32 = mybir.dt.int32
ALU = mybir.AluOpType
ACT = mybir.ActivationFunctionType
AX = mybir.AxisListType

P = 128
D = 1024
KB = D // P
TC = 256
TL = 512
T = TC + TL
HEADS = 8
PAIRS = HEADS // 2
DH = 64
CH = 128
LEVELS = 7
NCH = TL // CH
UC = 256
EPS = 1e-6
GRID_W = 64
LAM_INIT = 0.8 - 0.6

COL = {"attn_k": 0, "attn_v": 1024, "hgrn_i": 2048, "hgrn_f": 3072, "hgrn_b": 4096, "attn_q": 5120,
       "hgrn_q": 6144, "attn_z": 7168, "hgrn_z": 8192, "gate_a": 9216, "gate_h": 10240}
LAT = slice(TC, T)
CTX = slice(0, TC)

A_UNIT = 4 * PAIRS + 4
M_UNIT = A_UNIT + 4 * PAIRS + 4
O_UNIT = M_UNIT + 12
N_UNIT = O_UNIT + 4
MOD_UNITS = 8
GATE_UNITS = 4


def unit(base, p, j):
    return (base + j) % 2, 2 * p + (base + j) // 2, 4 * p + (base + j)


def hblock(p, s):
    if isinstance(p, int) and p == 0:
        return s % 2, (s - 3) // 2 if s % 2 else (s - 4) // 2
    return s % 2, (5 * p - 1 + (s - 1) // 2 if s % 2 else 6 * p - 2 + s // 2)


A_BANK0 = 6 * PAIRS + 4
A_BANK1 = 5 * PAIRS + 4


def ablock(p, s):
    if isinstance(p, int) and p == 0:
        return s % 2, (A_BANK1 + (s - 3) // 2 if s % 2 else A_BANK0 + (s - 4) // 2)
    return s % 2, (A_BANK1 + 4 + 5 * (p - 1) + s // 2 if s % 2 else A_BANK0 + 3 + 5 * (p - 1) + s // 2)


M_BANK0 = A_BANK0 + 3 + 5 * PAIRS + 1
M_BANK1 = A_BANK1 + 4 + 5 * PAIRS


def mblock(n):
    return 1 - n % 2, (M_BANK0 if n % 2 else M_BANK1) + n // 2


M_ORDER = ["gh0", "gh1", "ba0", "bh0", "gh2", "ba1", "bh1", "gh3", "ba2", "bh2", "ba3", "bh3"]
GATE_BLOCK = 2 * len(M_ORDER)
OUT_BLOCK = GATE_BLOCK + 2


class Chain:

    def __init__(self, eng, sem):
        self.eng, self.sem, self.n = eng, sem, 0

    def __call__(self, ins):
        self.n += 1
        ins.then_inc(self.sem, 1)
        self.eng.wait_ge(self.sem, self.n)


def hybrid_layer(nc, a, out):
    with ExitStack() as ctx:
        block = None

        def sem(name):
            return ctx.enter_context(nc.semaphore(name))

        base = (nc.sbuf_base + 63) // 64 * 64
        at = [base]

        def place(name, shape, dt=F32, offset=None):
            size = 1
            for d in shape[1:]:
                size *= d
            size *= 4
            if offset is None:
                offset = at[0]
                at[0] += (size + 31) // 32 * 32
            return nc.alloc_sbuf_tensor_at(name, shape, dt, offset=offset)

        hTh = place("hTh", [P, KB, T], F32R)
        hTl = place("hTl", [P, KB, T], F32R)
        wraw = [place(f"wraw{i}", [P, KB, UC]) for i in range(2)]
        wh = [place(f"wh{i}", [P, KB, UC], F32R) for i in range(2)]
        wl = [place(f"wl{i}", [P, KB, UC], F32R) for i in range(2)]
        ident = place("ident", [P, P])
        gate = place("gate", [P, D])
        mhalf = place("mhalf", [P, 16])
        scT = place("scT", [P, KB, 2])
        bmT = place("bmT", [P, 16])
        modT = place("modT", [P, 16, 2])
        ngT = place("ngT", [P, KB])
        lbraw = place("lbraw", [P, 2, 2, HEADS])
        lb = place("lb", [P, 2, HEADS])
        om = place("om", [P, 2, HEADS])
        nom = place("nom", [P, 2, HEADS])
        gH = place("gH", [P, 1])
        gA = place("gA", [P, 1])
        ssx = place("ssx", [P, 6])
        rrx = place("rrx", [P, 6])
        ssH = place("ssH", [P, 2, NCH])
        rrH = place("rrH", [P, 2, NCH])
        lamv = place("lamv", [P, 1])
        lame = place("lame", [P, 2])
        nmax = place("nmax", [P, 8, 2])
        esum = place("esum", [P, 8, 2])
        coef = place("coef", [P, 8, 2])
        ssA = place("ssA", [P, 8])
        eA = place("eA", [P, 8])
        rrA = place("rrA", [P, 8])
        ssn = place("ssn", [P, 8])
        rrn = place("rrn", [P, 8])
        R = (at[0] + 63) // 64 * 64
        K16 = 16384
        oTH = place("oTH", [P, HEADS, TL], offset=R)
        xt = place("xt", [P, 6, D], offset=R + K16)
        htmp = place("htmp", [P, 2, TL], offset=R + 3 * K16)
        sqx = place("sqx", [P, D], offset=R + 3 * K16 + 4096)
        o = R + K16
        qs = place("qs", [P, 2, TL], offset=o)
        sig = place("sig", [P, 2, 2, T], offset=o + 4096)
        zh = place("zh", [P, HEADS, TL], offset=o)
        o += K16
        K_ = place("K_", [P, 2, 2, T], offset=o); o += 12288
        Q_ = place("Q_", [P, 2, 2, TL], offset=o); o += 8192
        totE = place("totE", [P, 2, 2, T], offset=o); o += 12288
        totO = place("totO", [P, 2, 2, T // 2], offset=o); o += 6144
        mixQ = place("mixQ", [P, 2, TL], offset=o); o += 4096
        mixK = place("mixK", [P, 2, TL], offset=o); o += 4096
        V = place("V", [P, 6, UC], offset=o); o += 6144
        AT = place("AT", [P, 2, TL], offset=o); o += 4096
        S_ = place("S_", [P, 2, 2, NCH, P], offset=o); o += 8192
        masks = place("masks", [P, LEVELS + 1, CH], I32, offset=R + 6 * K16)
        oTA = place("oTA", [P, HEADS, TL], offset=R + K16)
        zA = place("zA", [P, HEADS, TL], offset=R + 2 * K16)
        ga = place("ga", [P, KB, TL], offset=R + 3 * K16)
        o2 = R + 3 * K16
        qn = place("qn", [P, 10, UC], offset=o2); o2 += 10240
        cosg = place("cosg", [P, 2, 4, DH], offset=o2); o2 += 2048
        sing = place("sing", [P, 2, 4, DH], offset=o2); o2 += 2048
        gqk = place("gqk", [P, 2, DH], offset=o2); o2 += 512
        rtmp = place("rtmp", [P, 4, 2 * UC], offset=o2); o2 += 8192
        rtmp_lam = place("rtmp_lam", [P, 4, DH], offset=o2 - 8192)
        o2 = (o2 + 63) // 64 * 64
        VA = place("VA", [P, 6, UC], offset=o2); o2 += 6144
        qT = place("qT", [P, 2, TL], offset=o2); o2 += 4096
        kT = place("kT", [P, 2, T], offset=o2); o2 += 6144
        E_ = place("E_", [P, 2, T], offset=o2); o2 += 6144
        W_ = place("W_", [P, T], offset=o2); o2 += 3072
        WT = place("WT", [P, T], offset=o2); o2 += 3072
        on = place("on", [P, P], offset=o2); o2 += 512
        junk = place("junk", [P, P], offset=o2); o2 += 512
        yHh = place("yHh", [P, KB, TL], F32R, offset=R + 4 * K16)
        yHl = place("yHl", [P, KB, TL], F32R, offset=R)
        yAh = place("yAh", [P, KB, TL], F32R, offset=R + 5 * K16)
        ysig = place("ysig", [P, KB, TL], offset=R + 5 * K16)
        yAl = place("yAl", [P, KB, TL], F32R, offset=R + K16)
        mTh = place("mTh", [P, KB, TL], F32R, offset=R + 2 * K16)
        mTl = place("mTl", [P, KB, TL], F32R, offset=R + 3 * K16)
        gh = place("gh", [P, 2, 2, TL], offset=R + 6 * K16)
        scb = place("scb", [P, KB, P], offset=R)
        xb = place("xb", [P, 4, D], offset=R + 4 * K16)
        ytmp = place("ytmp", [P, 2, 2, UC], offset=R + 6 * K16)

        PB = [ctx.enter_context(nc.psum_tensor(f"PB{i}", [P, 512], F32)) for i in range(2)]
        PX = ctx.enter_context(nc.psum_tensor("PX", [P, 6, 512], F32))
        LV = [PX[:, i, :] for i in range(2)]
        X = [PX[:, 2:4, :].rearrange("p a b -> p (a b)"),
             PX[:, 4:6, :].rearrange("p a b -> p (a b)")]
        SB = PX[:, 0:4, :]
        WB = PX[:, 4:6, :].rearrange("p a b -> p (a b)")

        const_in = sem("const_in")
        x_in = sem("x_in")
        xb_in = sem("xb_in")
        raw_ready = [sem(f"raw_ready{i}") for i in range(2)]
        hi_ready = sem("hi_ready")
        lo_ready = sem("lo_ready")
        mod_used = sem("mod_used")
        gate_used = sem("gate_used")
        blk_ready = [sem(f"blk_ready{i}") for i in range(2)]
        blk_free = [sem(f"blk_free{i}") for i in range(2)]
        dve_chain = sem("dve_chain")
        act_chain = sem("act_chain")
        pool_chain = sem("pool_chain")
        sig_c = sem("sig_c")
        sc_ready = sem("sc_ready")
        mod_ready = sem("mod_ready")
        mod_final = sem("mod_final")
        ssx_ready = sem("ssx_ready")
        rrx_ready = sem("rrx_ready")
        xn_ready = sem("xn_ready")
        xT_ready = sem("xT_ready")
        xT_used = sem("xT_used")
        h_split = sem("h_split")
        lbd_ready = sem("lbd_ready")
        lb_ready = sem("lb_ready")
        qsig_ready = sem("qsig_ready")
        q_ready = sem("q_ready")
        sig_used = sem("sig_used")
        v_ready = sem("v_ready")
        diag_ready = sem("diag_ready")
        levels_ready = sem("levels_ready")
        mix_ready = sem("mix_ready")
        scores_ready = sem("scores_ready")
        scores_used = sem("scores_used")
        kT_ready = sem("kT_ready")
        kT_copied = sem("kT_copied")
        kv_ready = sem("kv_ready")
        kv_used = sem("kv_used")
        out_ready = sem("out_ready")
        sqH_ready = sem("sqH_ready")
        rrH_ready = sem("rrH_ready")
        onH_ready = sem("onH_ready")
        oT_ready = sem("oT_ready")
        oT_done = sem("oT_done")
        zsig_ready = sem("zsig_ready")
        zh_ready = sem("zh_ready")
        oTH_final = sem("oTH_final")
        lamd_ready = sem("lamd_ready")
        lame_ready = sem("lame_ready")
        tab_ready = sem("tab_ready")
        z_ready = sem("z_ready")
        va_ready = sem("va_ready")
        raw_copied = sem("raw_copied")
        ssn_ready = sem("ssn_ready")
        rrn_ready = sem("rrn_ready")
        u_ready = sem("u_ready")
        t1_ready = sem("t1_ready")
        qn_ready = sem("qn_ready")
        qkT_ready = sem("qkT_ready")
        qkT_copied = sem("qkT_copied")
        s_ready = sem("s_ready")
        max_ready = sem("max_ready")
        exp_ready = sem("exp_ready")
        w_ready = sem("w_ready")
        wT_ready = sem("wT_ready")
        wT_copied = sem("wT_copied")
        pv_ready = sem("pv_ready")
        sqA_ready = sem("sqA_ready")
        rrA_ready = sem("rrA_ready")
        onA_ready = sem("onA_ready")
        oTA_ready = sem("oTA_ready")
        oTA_done = sem("oTA_done")
        ga_ready = sem("ga_ready")
        gasig_ready = sem("gasig_ready")
        ysig_ready = sem("ysig_ready")
        yH_ready = sem("yH_ready")
        yA_ready = sem("yA_ready")
        gh_ready = sem("gh_ready")
        m_ready = sem("m_ready")
        scb_ready = sem("scb_ready")
        gate_ready = sem("gate_ready")
        o_ready = sem("o_ready")
        out_done = sem("out_done")

        w_in = a["w_in"][0]
        w_mod = a["w_mod"][0]

        def unit_source(n):
            def cols(m, c0):
                return m[:, c0:c0 + UC].rearrange("(k p) c -> p k c", p=P)
            if n < A_UNIT:
                p, j = divmod(n, 4)
                if n >= 4 * PAIRS:
                    return cols(w_in, COL["hgrn_z"] + UC * (n - 4 * PAIRS))
                return cols(w_in, COL[("hgrn_f", "hgrn_b", "hgrn_q", "hgrn_i")[j]] + UC * p)
            if n < M_UNIT:
                n -= A_UNIT
                p, j = divmod(n, 4)
                if n >= 4 * PAIRS:
                    return cols(w_in, COL["gate_a"] + UC * (n - 4 * PAIRS))
                return cols(w_in, COL[("attn_z", "attn_q", "attn_k", "attn_v")[j]] + UC * p)
            if n < O_UNIT:
                kind, j = M_ORDER[n - M_UNIT][:2], int(M_ORDER[n - M_UNIT][2])
                if kind == "gh":
                    return cols(w_in, COL["gate_h"] + UC * j)
                return cols(a["w_br_attn"][0] if kind == "ba" else a["w_br_hgrn"][0], UC * j)
            return cols(a["w_out"][0], UC * (n - O_UNIT))

        block = ctx.enter_context(nc.Block())

        @block.sync
        def _(sp):
            small = [(ident[:], a["ident"]), (masks[:], a["masks"]),
                     (scT[:, :, 0], a["c"][0].rearrange("(k p) -> p k", p=P)),
                     (scT[:, :, 1], a["c_ctx"].rearrange("(k p) -> p k", p=P))]
            for dst, src in small:
                sp.dma_start(dst, src, allow_slow_non_contiguous=True).then_inc(const_in, 16)
            sp.dma_start(xt[:, 0:2, :], a["ctx"][0].rearrange("(t p) d -> p t d", p=P)).then_inc(x_in, 16)
            sp.dma_start(xt[:, 2:6, :], a["x"][0].rearrange("(t p) d -> p t d", p=P)).then_inc(x_in, 16)
            for u in range(MOD_UNITS):
                if u >= 2:
                    sp.wait_ge(mod_used, u - 1)
                sp.dma_start(wraw[u % 2][:], w_mod[:, u * UC:(u + 1) * UC].rearrange("(k p) c -> p k c", p=P)
                             ).then_inc(raw_ready[u % 2], 16)
            for n in range(N_UNIT):
                if n == O_UNIT:
                    for u in range(GATE_UNITS):
                        if u < 2:
                            sp.wait_ge(lo_ready, O_UNIT - 1 + u)
                        else:
                            sp.wait_ge(gate_used, u - 1)
                        c0 = 2 * D + u * UC
                        sp.dma_start(wraw[u % 2][:], w_mod[:, c0:c0 + UC].rearrange("(k p) c -> p k c", p=P)
                                     ).then_inc(raw_ready[u % 2], 16)
                if n < 2:
                    sp.wait_ge(mod_used, MOD_UNITS - 1 + n)
                elif O_UNIT <= n < O_UNIT + 2:
                    sp.wait_ge(gate_used, GATE_UNITS - 1 + n - O_UNIT)
                else:
                    sp.wait_ge(lo_ready, n - 1)
                sp.dma_start(wraw[n % 2][:], unit_source(n)).then_inc(raw_ready[n % 2], 16)
            sp.wait_ge(m_ready, 8)
            sp.dma_start(xb[:], a["x"][0].rearrange("(t p) d -> p t d", p=P)).then_inc(xb_in, 16)
            ov = out[0].rearrange("(t p) d -> p t d", p=P)
            for n in range(8):
                sp.wait_ge(o_ready, n + 1)
                u, h = divmod(n, 2)
                sp.dma_start(ov[:, 2 * h:2 * h + 2, u * UC:(u + 1) * UC],
                             xb[:, 2 * h:2 * h + 2, u * UC:(u + 1) * UC]).then_inc(out_done, 16)
            sp.wait_ge(out_done, 16 * 8)

        @block.tensor
        def _(pe):
            def mm3(dst, xh, xl, yh, yl, first, last):
                nc.tensor.matmul(dst, xh, yh, start=first, stop=False)
                nc.tensor.matmul(dst, xh, yl, start=False, stop=False)
                return nc.tensor.matmul(dst, xl, yh, start=False, stop=last)

            def feature_block(dst, s, cb, cols, ks=range(KB), yh=hTh, yl=hTl):
                c = slice(cb * P, cb * P + P)
                for k in ks:
                    last = mm3(dst, wh[s][:, k, c], wl[s][:, k, c], yh[:, k, cols], yl[:, k, cols],
                               k == 0, k == KB - 1)
                return last

            def token_tile(dst, s, t, ks=range(KB), yh=hTh, yl=hTl):
                c = slice(t * P, t * P + P)
                for k in ks:
                    last = mm3(dst, yh[:, k, c], yl[:, k, c], wh[s][:, k, :], wl[s][:, k, :],
                               k == 0, k == KB - 1)
                return last

            def open_block(b, n):
                if not (isinstance(n, int) and n == 0):
                    pe.wait_ge(blk_free[b], n)

            pe.wait_ge(sc_ready, 1)
            for u in range(MOD_UNITS):
                pe.wait_ge(raw_ready[u % 2], 16 * (u // 2 + 1))
                for cb in range(2):
                    j = 2 * u + cb
                    for k in range(KB):
                        last = nc.tensor.matmul(X[0][:, 2 * j:2 * j + 2], wraw[u % 2][:, k, cb * P:cb * P + P],
                                                scT[:, k, :], start=(k == 0), stop=(k == KB - 1))
                last.then_inc(mod_used, 1)
            pe.wait_ge(const_in, 16 * 4)
            pe.wait_ge(xn_ready, 6)
            for g in range(2 * KB):
                k, c = divmod(g, 2)
                if g >= 2:
                    pe.wait_ge(xT_used, g - 1)
                tiles = range(2) if c else range(2, 6)
                for i, t in enumerate(tiles):
                    last = nc.tensor.transpose(PB[g % 2][:, i * P:i * P + P], xt[:, t, k * P:k * P + P], ident[:])
                last.then_inc(xT_ready, 1)

            def h_proj(p, s):
                b, n = hblock(p, s)
                j = -1 if s < 3 else (s - 3) // 3
                ws, _, wn = unit(0, p, j)
                if s in (0, 3, 6, 9):
                    pe.wait_ge(lo_ready, wn + 1)
                if isinstance(p, int) and p == 0 and s < 5:
                    pe.wait_ge(xT_used, 2 * KB)
                open_block(b, n)
                if s < 3:
                    for i in range(2):
                        last = token_tile(PB[b][:, i * UC:(i + 1) * UC], ws, 2 * s + i)
                elif s in (5, 8):
                    for cb in range(2):
                        last = feature_block(PB[b][:, cb * UC:(cb + 1) * UC], ws, cb, CTX)
                else:
                    cb = (s - 3) % 3 if s < 9 else s - 9
                    last = feature_block(PB[b][:, :], ws, cb, LAT)
                last.then_inc(blk_ready[b], 1)

            def h_scores(c, st):
                for h in range(2):
                    if st == 0:
                        pe.wait_ge(diag_ready, 2 * c + h + 1)
                        if not (isinstance(c, int) and c == 0):
                            pe.wait_ge(onH_ready, 2 * c + h - 1)
                    else:
                        pe.wait_ge(mix_ready, 14 * c + 2 * (st - 1) + h + 1)
                        pe.wait_ge(scores_used, 16 * c + 2 * (st - 1) + h + 1)
                    for ch in range(NCH):
                        t = slice(ch * CH, ch * CH + CH)
                        last = nc.tensor.matmul(LV[h][:, t], mixK[:, h, t], mixQ[:, h, t], start=True, stop=True)
                    last.then_inc(scores_ready, 1)

            ORDER = [(0, 1, 2, 3, 4), (1, 0, 5, 4, 3)]

            def h_keysT(c, u):
                h, d = divmod(u, 2)
                pe.wait_ge(levels_ready, 16 * c + 14 + h + 1)
                if u >= 2:
                    pe.wait_ge(kv_used, 4 * c + u - 1)
                elif not (isinstance(c, int) and c == 0):
                    pe.wait_ge(oT_done, 2 * c)
                for i, ch in enumerate(ORDER[d]):
                    last = nc.tensor.transpose(X[u % 2][:, i * P:i * P + P], K_[:, h, d, ch * CH:ch * CH + CH],
                                               ident[:])
                last.then_inc(kT_ready, 1)

            def h_kv(c, u):
                h, d = divmod(u, 2)
                pe.wait_ge(kT_copied, 4 * c + u + 1)
                pe.wait_ge(v_ready, 3 * c + 3)
                for i, ch in enumerate(ORDER[d]):
                    last = nc.tensor.matmul(X[u % 2][:, i * P:i * P + P], totE[:, h, d, i * CH:i * CH + CH],
                                            V[:, ch, h * P:h * P + P], start=True, stop=True)
                last.then_inc(kv_ready, 1)

            def h_out(c, h):
                pe.wait_ge(kv_used, 4 * c + 2 * h + 2)
                pe.wait_ge(scores_used, 16 * c + 14 + h + 1)
                for ch in range(NCH):
                    t = slice(ch * CH, ch * CH + CH)
                    dst = LV[h][:, t]
                    nc.tensor.matmul(dst, AT[:, h, t], V[:, 2 + ch, h * P:h * P + P], start=True, stop=False)
                    nc.tensor.matmul(dst, Q_[:, h, 0, t], S_[:, h, 0, ch, :], start=False, stop=False)
                    last = nc.tensor.matmul(dst, Q_[:, h, 1, t], S_[:, h, 1, ch, :], start=False, stop=True)
                last.then_inc(out_ready, 1)

            def h_outT(c, h):
                pe.wait_ge(onH_ready, 2 * c + h + 1)
                pe.wait_ge(kv_used, 4 * c + 4)
                for ch in range(NCH):
                    t = slice(ch * CH, ch * CH + CH)
                    last = nc.tensor.transpose(X[h][:, t], AT[:, h, t], ident[:])
                last.then_inc(oT_ready, 1)

            def h_core(c, s):
                if s < 8:
                    h_scores(c, s)
                elif s == 8:
                    h_keysT(c, 0)
                    h_keysT(c, 1)
                elif s == 9:
                    h_kv(c, 0)
                    h_kv(c, 1)
                    h_keysT(c, 2)
                    h_keysT(c, 3)
                else:
                    h_kv(c, 2)
                    h_kv(c, 3)
                    h_out(c, 0)
                    h_out(c, 1)

            pe.wait_ge(h_split, 2 * KB)
            for s in range(3, 11):
                h_proj(0, s)
            for p in range(1, PAIRS):
                for s in range(11):
                    h_proj(p, s)
                    if s == 0 and p > 1:
                        h_outT(p - 2, 0)
                        h_outT(p - 2, 1)
                    h_core(p - 1, s)
            for s in range(11):
                if s < 3:
                    h_proj(PAIRS, s)
                else:
                    b, n = hblock(PAIRS, s)
                    u, cb = divmod(s - 3, 2)
                    if cb == 0:
                        pe.wait_ge(lo_ready, 4 * PAIRS + u + 1)
                    open_block(b, n)
                    feature_block(PB[b][:, :], u % 2, cb, LAT).then_inc(blk_ready[b], 1)
                if s == 0:
                    h_outT(PAIRS - 2, 0)
                    h_outT(PAIRS - 2, 1)
                h_core(PAIRS - 1, s)

            def a_proj(p, s, ks):
                b, n = ablock(p, s)
                j = -1 if s < 3 else 0 if s < 5 else 1 if s < 7 else 2
                ws, _, wn = unit(A_UNIT, p, j)
                if ks == 0:
                    if s in (0, 3, 5, 7):
                        pe.wait_ge(lo_ready, wn + 1)
                    open_block(b, n)
                if 3 <= s < 5:
                    last = feature_block(PB[b][:, :], ws, s - 3, LAT, range(4 * ks, 4 * ks + 4))
                else:
                    t = (2 * s if s < 3 else 2 + 2 * (s - 5) if s < 7 else 2 * (s - 7)) + ks
                    last = token_tile(PB[b][:, ks * UC:(ks + 1) * UC], ws, t)
                if ks == 1:
                    last.then_inc(blk_ready[b], 1)

            def ga_proj(s, ks):
                b, n = ablock(PAIRS, s)
                u, cb = divmod(s - 3, 2)
                if ks == 0:
                    if cb == 0:
                        pe.wait_ge(lo_ready, A_UNIT + 4 * PAIRS + u + 1)
                    open_block(b, n)
                last = feature_block(PB[b][:, :], u % 2, cb, LAT, range(4 * ks, 4 * ks + 4))
                if ks == 1:
                    last.then_inc(blk_ready[b], 1)

            def a_qkT(c, h):
                pe.wait_ge(qn_ready, 5 * (c + 1))
                if h == 0:
                    if not (isinstance(c, int) and c == 0):
                        pe.wait_ge(exp_ready, 16 * c)
                    else:
                        pe.wait_ge(oT_done, 2 * PAIRS)
                        pe.wait_ge(kv_used, 4 * PAIRS)
                else:
                    pe.wait_ge(qkT_copied, 2 * c + 1)
                for i in range(4):
                    nc.tensor.transpose(SB[:, 0, i * P:i * P + P], qn[:, i, h * P:h * P + P], ident[:])
                for i in range(6):
                    last = nc.tensor.transpose(SB[:, 1 + i // 4, (i % 4) * P:(i % 4 + 1) * P],
                                               qn[:, 4 + i, h * P:h * P + P], ident[:])
                last.then_inc(qkT_ready, 1)

            def a_scores(c, j):
                h, qt = divmod(j, 4)
                if j == 0:
                    pe.wait_ge(qkT_copied, 2 * c + 2)
                if not (isinstance(c, int) and c == 0 and j == 0):
                    pe.wait_ge(exp_ready, 16 * c + 2 * j)
                for kh in range(2):
                    for m in range(2):
                        r = slice(m * DH, m * DH + DH)
                        last = nc.tensor.matmul(SB[:, 2 * m + kh, 0:384], qT[r, h, qt * P:qt * P + P],
                                                kT[r, h, kh * 384:kh * 384 + 384], start=True, stop=True)
                last.then_inc(s_ready, 1)

            def a_wT(c, j):
                pe.wait_ge(w_ready, 8 * c + j + 1)
                if not (isinstance(c, int) and c == 0 and j == 0):
                    pe.wait_ge(oTA_done, 8 * c + j)
                for i in range(6):
                    last = nc.tensor.transpose(WB[:, i * P:i * P + P], W_[:, i * P:i * P + P], ident[:])
                last.then_inc(wT_ready, 1)

            def a_pv(c, j):
                h = j // 4
                pe.wait_ge(wT_copied, 8 * c + j + 1)
                pe.wait_ge(va_ready, 3 * c + 3)
                for i in range(6):
                    last = nc.tensor.matmul(WB[:, 768:896], WT[:, i * P:i * P + P], VA[:, i, h * P:h * P + P],
                                            start=(i == 0), stop=(i == 5))
                last.then_inc(pv_ready, 1)

            def a_outT(c, j):
                pe.wait_ge(onA_ready, 8 * c + j + 1)
                nc.tensor.transpose(WB[:, 896:1024], on[:], ident[:]).then_inc(oTA_ready, 1)

            def a_slot(c, s, proj):
                proj(0)
                if s == 0:
                    proj(1)
                    a_qkT(c, 0)
                    a_qkT(c, 1)
                    return
                if s >= 3:
                    a_outT(c, s - 3)
                if s <= 8:
                    a_scores(c, s - 1)
                if s >= 2:
                    a_wT(c, s - 2)
                proj(1)
                if s >= 2:
                    a_pv(c, s - 2)
                if s == 9:
                    a_outT(c, 7)

            for s in range(3, 10):
                a_proj(0, s, 0)
                a_proj(0, s, 1)
                if s == 4:
                    h_outT(PAIRS - 1, 0)
                    h_outT(PAIRS - 1, 1)
            for p in range(1, PAIRS):
                for s in range(10):
                    a_slot(p - 1, s, lambda ks: a_proj(p, s, ks))
            for s in range(10):
                if s < 3:
                    a_slot(PAIRS - 1, s, lambda ks: a_proj(PAIRS, s, ks))
                else:
                    a_slot(PAIRS - 1, s, lambda ks: ga_proj(s, ks))
            ga_proj(10, 0)
            ga_proj(10, 1)

            for i, what in enumerate(M_ORDER):
                n = M_UNIT + i
                pe.wait_ge(lo_ready, n + 1)
                for cb in range(2):
                    b, cnt = mblock(2 * i + cb)
                    open_block(b, cnt)
                    if what[:2] == "gh":
                        last = feature_block(PB[b][:, :], n % 2, cb, LAT)
                    else:
                        ready, yh, yl = (yA_ready, yAh, yAl) if what[:2] == "ba" else (yH_ready, yHh, yHl)
                        for k in range(KB):
                            pe.wait_ge(ready, k + 1)
                            last = feature_block(PB[b][:, :], n % 2, cb, slice(0, TL), [k], yh, yl)
                    last.then_inc(blk_ready[b], 1)
            pe.wait_ge(scb_ready, 1)
            for u in range(GATE_UNITS):
                b, cnt = mblock(GATE_BLOCK + u // 2)
                pe.wait_ge(raw_ready[u % 2], 16 * (MOD_UNITS // 2 + O_UNIT // 2 + u // 2 + 1))
                if u % 2 == 0:
                    open_block(b, cnt)
                for k in range(KB):
                    last = nc.tensor.matmul(PB[b][:, (u % 2) * UC:(u % 2 + 1) * UC], scb[:, k, :],
                                            wraw[u % 2][:, k, :], start=(k == 0), stop=(k == KB - 1))
                last.then_inc(gate_used, 1)
            pe.wait_ge(m_ready, 8)
            for i in range(4):
                pe.wait_ge(lo_ready, O_UNIT + i + 1)
                for half in range(2):
                    b, cnt = mblock(OUT_BLOCK + 2 * i + half)
                    open_block(b, cnt)
                    for t in range(2):
                        last = token_tile(PB[b][:, t * UC:(t + 1) * UC], (O_UNIT + i) % 2, 2 * half + t,
                                          range(KB), mTh, mTl)
                    last.then_inc(blk_ready[b], 1)

        @block.scalar
        def _(act):
            link = Chain(act, act_chain)
            f = nc.scalar.activation

            def split_hi(n, cnt, extra=0):
                s = n % 2 if isinstance(n, int) else None
                act.wait_ge(raw_ready[s], 16 * (MOD_UNITS // 2 + extra + cnt + 1))
                f(wh[s][:], wraw[s][:], ACT.Copy).then_inc(hi_ready, 1)

            for dst, src in [(bmT[:], a["b_mod"][0, 0:2 * D].rearrange("(j p) -> p j", p=P)),
                             (ngT[:], a["norm_gain"][0].rearrange("(k p) -> p k", p=P)),
                             (gH[:], a["hgrn_norm_gain"][0].rearrange("(p o) -> p o", o=1)),
                             (gA[:], a["subln_gain"][0].rearrange("(p o) -> p o", o=1)),
                             (gate[:], a["b_mod"][0:1, 2 * D:3 * D].to_broadcast([P, D]))]:
                act.dma_start(dst, src, allow_slow_non_contiguous=True).then_inc(const_in, 16)
            for d, name in enumerate(("hgrn_lb_fwd", "hgrn_lb_bwd")):
                for l in range(2):
                    act.dma_start(lbraw[:, d, l, :], a[name][l].rearrange("(h p) -> p h", p=P),
                                  allow_slow_non_contiguous=True).then_inc(const_in, 16)
            act.wait_ge(const_in, 16 * 13)
            f(modT[:, 0:KB, :], scT[:], ACT.Sigmoid).then_inc(sig_c, 1)
            act.wait_ge(x_in, 32)
            for t in range(6):
                link(f(sqx[:], xt[:, t, :], ACT.Square, accum_out=ssx[:, t:t + 1]))
            act.sem_inc(ssx_ready, 1)
            act.wait_ge(lbd_ready, 1)
            f(lb[:], om[:], ACT.Sigmoid).then_inc(lb_ready, 1)
            act.wait_ge(lb_ready, 1)
            f(om[:], om[:], ACT.Sigmoid, scale=-1.0).then_inc(lb_ready, 1)
            act.wait_ge(mod_final, 1)
            for g in range(2 * KB):
                k, c = divmod(g, 2)
                n = TC if c else TL
                act.wait_ge(xT_ready, g + 1)
                if g >= 2:
                    act.wait_ge(h_split, g - 1)
                f(htmp[:, g % 2, 0:n], PB[g % 2][:, 0:n], ACT.Identity, scale=modT[:, KB + k, c:c + 1],
                  bias=modT[:, k, c:c + 1]).then_inc(xT_used, 1)
                if g in (3, 9):
                    split_hi(g // 6, 0)

            def h_evac(p, s):
                b, n = hblock(p, s)
                act.wait_ge(blk_ready[b], n + 1)
                if s < 3:
                    c = p - 1
                    if not (isinstance(c, int) and c == 0):
                        act.wait_ge(out_ready, 2 * c)
                    f(V[:, 2 * s:2 * s + 2, :], PB[b][:, :].rearrange("p (t c) -> p t c", t=2),
                      ACT.Copy).then_inc(v_ready, 1)
                    act.wait_ge(v_ready, 3 * c + s + 1)
                    act.sem_inc(blk_free[b], 1)
                    return
                if s == 3 and not (isinstance(p, int) and p == 0):
                    act.wait_ge(sig_used, 2 * p)
                if s < 9:
                    d, i = divmod(s - 3, 3)
                    if i == 2:
                        f(sig[:, :, d, 0:TC], PB[b][:, :].rearrange("p (h t) -> p h t", h=2),
                          ACT.Sigmoid).then_inc(blk_free[b], 1)
                    else:
                        f(sig[:, i, d, LAT], PB[b][:, :], ACT.Sigmoid).then_inc(blk_free[b], 1)
                else:
                    f(qs[:, s - 9, :], PB[b][:, :], ACT.Sigmoid).then_inc(qsig_ready, 1)

            def halves(ap, l, which, n=TL):
                B = 1 << l
                return ap.rearrange("p (n two b) -> p n two b", two=2, b=B)[:, :, which, :]

            def h_mix(c, st):
                l = st - 1
                for h in range(2):
                    act.wait_ge(levels_ready, 16 * c + 2 * l + h + 1)
                    act.wait_ge(scores_ready, 16 * c + 2 * l + h + 1)
                    for dst, src, side in ((mixQ, Q_, 0), (mixK, K_, 1)):
                        cols = slice(0, TL) if side == 0 else LAT
                        f(halves(dst[:, h, :], l, 1 - side), halves(src[:, h, 0, cols], l, 1 - side), ACT.Copy)
                        last = f(halves(dst[:, h, :], l, side), halves(src[:, h, 1, cols], l, side), ACT.Copy)
                    last.then_inc(mix_ready, 1)

            def h_keysT_copy(c, u):
                h, d = divmod(u, 2)
                act.wait_ge(kT_ready, 4 * c + u + 1)
                f(totE[:, h, d, 0:640], X[u % 2][:, 0:640], ACT.Copy).then_inc(kT_copied, 1)

            def h_square(c, h):
                act.wait_ge(out_ready, 2 * c + h + 1)
                if not (isinstance(c, int) and c == 0):
                    act.wait_ge(rrH_ready, 2 * c)
                for ch in range(NCH):
                    last = f(mixQ[:, h, ch * P:ch * P + P], LV[h][:, ch * P:ch * P + P], ACT.Square,
                             accum_out=ssH[:, h, ch:ch + 1])
                link(last)
                act.sem_inc(sqH_ready, 1)

            def h_outT_copy(c, h, head):
                act.wait_ge(oT_ready, 2 * c + h + 1)
                f(oTH[:, head, :], X[h][:, 0:TL], ACT.Copy, scale=gH[:, 0:1]).then_inc(oT_done, 1)

            def h_slot_core(c, s):
                if s < 7:
                    h_mix(c, s + 1)
                elif s == 8:
                    h_keysT_copy(c, 0)
                    h_keysT_copy(c, 1)
                elif s == 9:
                    h_keysT_copy(c, 2)
                    h_keysT_copy(c, 3)
                elif s == 10:
                    h_square(c, 0)
                    h_square(c, 1)

            HI_AT = {2: 1, 5: 2, 8: 3, 10: 4}

            def hi_after(base_, p, s, table):
                if s in table:
                    sl, cnt, n = unit(base_, p, table[s])
                    act.wait_ge(raw_ready[sl], 16 * (MOD_UNITS // 2 + cnt + 1))
                    f(wh[sl][:], wraw[sl][:], ACT.Copy).then_inc(hi_ready, 1)

            for s in range(3, 11):
                h_evac(0, s)
                hi_after(0, 0, s, {5: 2, 8: 3, 10: 4})
            for p in range(1, PAIRS):
                for s in range(11):
                    h_evac(p, s)
                    if s == 0 and p > 1:
                        h_outT_copy(p - 2, 0, 2 * (p - 2))
                        h_outT_copy(p - 2, 1, 2 * (p - 2) + 1)
                    h_slot_core(p - 1, s)
                    hi_after(0, p, s, HI_AT)
            for s in range(11):
                if s < 3:
                    h_evac(PAIRS, s)
                else:
                    b, n = hblock(PAIRS, s)
                    act.wait_ge(blk_ready[b], n + 1)
                    if s == 3:
                        act.wait_ge(sig_used, 2 * PAIRS)
                    f(zh[:, s - 3, :], PB[b][:, :], ACT.Sigmoid).then_inc(zsig_ready, 1)
                if s == 0:
                    h_outT_copy(PAIRS - 2, 0, HEADS - 4)
                    h_outT_copy(PAIRS - 2, 1, HEADS - 3)
                h_slot_core(PAIRS - 1, s)
                hi_after(0, PAIRS, s, {2: 1, 4: 2, 6: 3, 8: 4, 10: 5})
            h_outT_copy(PAIRS - 1, 0, HEADS - 2)
            h_outT_copy(PAIRS - 1, 1, HEADS - 1)

            act.wait_ge(onH_ready, 2 * PAIRS)
            act.wait_ge(oT_done, 2 * PAIRS)
            act.wait_ge(oTH_final, 8)
            for i in range(2):
                act.dma_start(cosg[:, i, :, :], a["cos"].rearrange("(t p) d -> p t d", p=P)).then_inc(const_in, 16)
                act.dma_start(sing[:, i, :, :], a["sin"].rearrange("(t p) d -> p t d", p=P)).then_inc(const_in, 16)
            for i, name in enumerate(("q_norm_gain", "k_norm_gain")):
                act.dma_start(gqk[:, i, :], a[name][0:1, :].to_broadcast([P, DH])).then_inc(const_in, 16)
            for i, name in enumerate(("lambda_q1", "lambda_k1", "lambda_q2", "lambda_k2")):
                act.dma_start(rtmp_lam[:, i, :], a[name][0:1, :].to_broadcast([P, DH])).then_inc(const_in, 16)
            act.wait_ge(lamd_ready, 1)
            f(lame[:], lame[:], ACT.Exp).then_inc(lame_ready, 1)

            def a_evac(p, s):
                b, n = ablock(p, s)
                act.wait_ge(blk_ready[b], n + 1)
                if s < 3:
                    if not (isinstance(p, int) and p == 1):
                        act.wait_ge(pv_ready, 8 * (p - 1))
                    f(VA[:, 2 * s:2 * s + 2, :], PB[b][:, :].rearrange("p (t c) -> p t c", t=2),
                      ACT.Copy).then_inc(va_ready, 1)
                    act.wait_ge(va_ready, 3 * (p - 1) + s + 1)
                    act.sem_inc(blk_free[b], 1)
                elif s < 5:
                    f(zA[:, 2 * p + s - 3, :], PB[b][:, :], ACT.Copy).then_inc(blk_free[b], 1)
                else:
                    i = 5 * p + s - 5
                    if not (isinstance(i, int) and i == 0):
                        act.wait_ge(qn_ready, i)
                    else:
                        act.wait_ge(tab_ready, 1)
                    f(rtmp[:, 0, :], PB[b][:, :], ACT.Copy)
                    link(f(rtmp[:, 1, :], PB[b][:, :], ACT.Square))
                    act.sem_inc(blk_free[b], 1)
                    act.sem_inc(raw_copied, 1)

            def a_qkT_copy(c, h):
                act.wait_ge(qkT_ready, 2 * c + h + 1)
                f(qT[:, h, :], SB[:, 0, :], ACT.Copy)
                f(kT[:, h, :], PX[:, 1:3, :].rearrange("p a b -> p (a b)")[:, 0:T], ACT.Copy).then_inc(qkT_copied, 1)

            def a_square(c, j):
                act.wait_ge(pv_ready, 8 * c + j + 1)
                link(f(junk[:], WB[:, 768:896], ACT.Square, accum_out=ssA[:, j:j + 1]))
                act.sem_inc(sqA_ready, 1)

            def a_outT_copy(c, j):
                h, qt = divmod(j, 4)
                act.wait_ge(oTA_ready, 8 * c + j + 1)
                f(oTA[:, 2 * c + h, qt * P:qt * P + P], WB[:, 896:1024], ACT.Copy,
                  scale=gA[:, 0:1]).then_inc(oTA_done, 1)

            def a_wT_copy(c, j):
                act.wait_ge(wT_ready, 8 * c + j + 1)
                f(WT[:], WB[:, 0:768], ACT.Copy).then_inc(wT_copied, 1)

            def a_exp(c, j):
                for m in range(2):
                    act.wait_ge(max_ready, 16 * c + 2 * j + m + 1)
                    if not (isinstance(c, int) and c == 0 and j == 0):
                        act.wait_ge(w_ready, 8 * c + j)
                    link(f(E_[:, m, :].rearrange("p (a b) -> p a b", a=2), SB[:, 2 * m:2 * m + 2, 0:384], ACT.Exp,
                           bias=nmax[:, j, m:m + 1], accum_out=esum[:, j, m:m + 1]))
                    act.sem_inc(exp_ready, 1)

            def a_slot_core(c, s):
                if s == 0:
                    a_qkT_copy(c, 0)
                    a_qkT_copy(c, 1)
                    return
                if s >= 3:
                    a_square(c, s - 3)
                    a_outT_copy(c, s - 3)
                if s >= 2:
                    a_wT_copy(c, s - 2)
                if s <= 8:
                    a_exp(c, s - 1)

            A_HI = {2: 1, 4: 2, 6: 3, 9: 4}
            for s in range(3, 10):
                a_evac(0, s)
                hi_after(A_UNIT, 0, s, {4: 2, 6: 3, 9: 4})
            for p in range(1, PAIRS):
                for s in range(10):
                    if s == 0:
                        a_evac(p, s)
                    a_slot_core(p - 1, s)
                    if s > 0:
                        a_evac(p, s)
                    if s == 9:
                        a_square(p - 1, 7)
                        a_outT_copy(p - 1, 7)
                    hi_after(A_UNIT, p, s, A_HI)

            def ga_evac(s):
                b, n = ablock(PAIRS, s)
                act.wait_ge(blk_ready[b], n + 1)
                f(ga[:, s - 3, :], PB[b][:, :], ACT.Copy).then_inc(ga_ready, 1)
                act.wait_ge(ga_ready, s - 2)
                act.sem_inc(blk_free[b], 1)

            for s in range(10):
                if s == 0:
                    a_evac(PAIRS, s)
                a_slot_core(PAIRS - 1, s)
                if 0 < s < 3:
                    a_evac(PAIRS, s)
                elif s >= 3:
                    ga_evac(s)
                if s == 9:
                    a_square(PAIRS - 1, 7)
                    a_outT_copy(PAIRS - 1, 7)
                hi_after(A_UNIT, PAIRS, s, {2: 1, 4: 2, 6: 3, 8: 4})
            ga_evac(10)

            def m_hi(i):
                sl, cnt, n = unit(M_UNIT, 0, i)
                if i >= 2:
                    b, c0 = mblock(2 * (i - 2) + 1)
                    act.wait_ge(blk_ready[b], c0 + 1)
                act.wait_ge(raw_ready[sl], 16 * (MOD_UNITS // 2 + cnt + 1))
                f(wh[sl][:], wraw[sl][:], ACT.Copy).then_inc(hi_ready, 1)

            m_hi(1)
            act.wait_ge(ga_ready, 8)
            f(ga[:], ga[:], ACT.Sigmoid).then_inc(gasig_ready, 1)
            act.wait_ge(onA_ready, 8 * PAIRS)
            act.wait_ge(oTA_done, 8 * PAIRS)
            for k in range(KB):
                f(ysig[:, k, :], zA[:, k, :], ACT.Sigmoid).then_inc(ysig_ready, 1)
            for i, what in enumerate(M_ORDER):
                if what[:2] == "gh":
                    j = int(what[2])
                    if j >= 2:
                        act.wait_ge(m_ready, 2 * (j - 1))
                    for cb in range(2):
                        b, cnt = mblock(2 * i + cb)
                        act.wait_ge(blk_ready[b], cnt + 1)
                        f(gh[:, j % 2, cb, :], PB[b][:, :], ACT.Sigmoid).then_inc(gh_ready, 1)
                        act.wait_ge(gh_ready, 2 * j + cb + 1)
                        act.sem_inc(blk_free[b], 1)
                if i + 2 < len(M_ORDER):
                    m_hi(i + 2)
            for i in range(4):
                if i < 2:
                    b, c0 = mblock(2 * (10 + i) + 1)
                    act.wait_ge(blk_ready[b], c0 + 1)
                else:
                    b, c0 = mblock(OUT_BLOCK + 2 * (i - 2) + 1)
                    act.wait_ge(blk_ready[b], c0)
                sl, cnt, n = unit(O_UNIT, 0, i)
                act.wait_ge(raw_ready[sl], 16 * (MOD_UNITS // 2 + GATE_UNITS // 2 + cnt + 1))
                f(wh[sl][:], wraw[sl][:], ACT.Copy).then_inc(hi_ready, 1)

        @block.vector
        def _(dve):
            link = Chain(dve, dve_chain)
            v = nc.vector

            def bc(ap, shape):
                return ap.to_broadcast(shape)

            dve.wait_ge(sig_c, 1)
            v.tensor_tensor(scT[:], scT[:], modT[:, 0:KB, :], ALU.mult).then_inc(sc_ready, 1)
            v.tensor_tensor(om[:], lbraw[:, :, 0, :], lbraw[:, :, 1, :], ALU.subtract).then_inc(lbd_ready, 1)
            dve.wait_ge(lb_ready, 2)
            link(v.tensor_scalar(nom[:], om[:], -1.0, None, ALU.mult))
            dve.wait_ge(rrx_ready, 1)
            for t in range(6):
                v.tensor_scalar(xt[:, t, :], xt[:, t, :], rrx[:, t:t + 1], None, ALU.mult).then_inc(xn_ready, 1)
            dve.wait_ge(mod_used, MOD_UNITS)
            link(v.tensor_tensor(modT[:], X[0][:, 0:32].rearrange("p (j c) -> p j c", c=2),
                                 bc(bmT[:].unsqueeze(2), [P, 16, 2]), ALU.add))
            link(v.tensor_scalar(modT[:, KB:, :], modT[:, KB:, :], 1.0, None, ALU.add))
            v.tensor_tensor(modT[:, KB:, :], modT[:, KB:, :], bc(ngT[:].unsqueeze(2), [P, KB, 2]),
                            ALU.mult).then_inc(mod_final, 1)
            for g in range(2 * KB):
                k, c = divmod(g, 2)
                n = TC if c else TL
                cols = CTX if c else LAT
                dve.wait_ge(xT_used, g + 1)
                link(v.tensor_copy(hTh[:, k, cols], htmp[:, g % 2, 0:n]))
                v.tensor_tensor(hTl[:, k, cols], htmp[:, g % 2, 0:n], hTh[:, k, cols].bitcast(F32),
                                ALU.subtract).then_inc(h_split, 1)

            def halves(ap, l, which):
                return ap.rearrange("p (n two b) -> p n two b", two=2, b=1 << l)[:, :, which, :]

            def h_qmul(p, i):
                b, n = hblock(p, 9 + i)
                dve.wait_ge(qsig_ready, 2 * p + i + 1)
                v.tensor_tensor(qs[:, i, :], PB[b][:, :], qs[:, i, :], ALU.mult).then_inc(q_ready, 1)
                dve.wait_ge(q_ready, 2 * p + i + 1)
                dve.sem_inc(blk_free[b], 1)


            def h_prep_gates(p):
                for h in range(2):
                    for d in range(2):
                        head = 2 * p + h
                        v.tensor_scalar(totE[:, h, d, :], sig[:, h, d, :], om[:, d, head:head + 1],
                                        lb[:, d, head:head + 1], ALU.mult, ALU.add)
                        link(v.tensor_scalar(K_[:, h, d, :], sig[:, h, d, :], nom[:, d, head:head + 1],
                                             om[:, d, head:head + 1], ALU.mult, ALU.add))

            def h_prep_queries(p):
                for h in range(2):
                    v.tensor_copy(mixQ[:, h, :], qs[:, h, :])
                    link(v.tensor_tensor(mixK[:, h, :], K_[:, h, 0, LAT], K_[:, h, 1, LAT], ALU.add))
                    dve.sem_inc(diag_ready, 1)
                    v.tensor_tensor(Q_[:, h, 0, :], qs[:, h, :], totE[:, h, 0, LAT], ALU.mult)
                    link(v.tensor_tensor(Q_[:, h, 1, :], qs[:, h, :], totE[:, h, 1, LAT], ALU.mult))
                    dve.sem_inc(levels_ready, 1)
                    dve.sem_inc(sig_used, 1)

            def tot(l, h, d):
                return (totO if l % 2 else totE)[:, h, d, 0:T >> l]

            def h_join(c, l, h):
                dve.wait_ge(mix_ready, 14 * c + 2 * l + h + 1)
                B = 1 << l
                n, nq = T // (2 * B), TL // (2 * B)
                for d in range(2):
                    tt = tot(l, h, d).rearrange("p (n two) -> p n two", two=2)
                    near, far = d, 1 - d
                    kk = halves(K_[:, h, d, :], l, near)
                    v.tensor_tensor(kk, kk, bc(tt[:, :, far:far + 1], [P, n, B]), ALU.mult)
                    qq = halves(Q_[:, h, d, :], l, far)
                    v.tensor_tensor(qq, qq, bc(tt[:, TC // (2 * B):, near:near + 1], [P, nq, B]), ALU.mult)
                    last = v.tensor_tensor(tot(l + 1, h, d), tt[:, :, 0], tt[:, :, 1], ALU.mult)
                last.then_inc(levels_ready, 1)

            def h_pick(c, st, h):
                dve.wait_ge(scores_ready, 16 * c + 2 * st + h + 1)
                if st == 0 and not (isinstance(c, int) and c == 0):
                    dve.wait_ge(oT_ready, 2 * (c - 1) + h + 1)
                v.copy_predicated(AT[:, h, :].rearrange("p (n t) -> p n t", n=NCH),
                                  bc(masks[:, st:st + 1, :], [P, NCH, CH]),
                                  LV[h].rearrange("p (n t) -> p n t", n=NCH)).then_inc(scores_used, 1)

            def h_states(c, u):
                h, d = divmod(u, 2)
                dve.wait_ge(kv_ready, 4 * c + u + 1)
                order = (0, 1, 2, 3, 4) if d == 0 else (1, 0, 5, 4, 3)
                last_tot = tot(LEVELS, h, d)
                at_chunk = [0, 0, 1, 2, 3] if d == 0 else [3, 3, 2, 1, 0]
                link(v.tensor_copy(S_[:, h, d, at_chunk[0], :], X[u % 2][:, 0:P]))
                for i in range(1, 5):
                    ins = v.scalar_tensor_tensor(S_[:, h, d, at_chunk[i], :], S_[:, h, d, at_chunk[i - 1], :],
                                                 last_tot[:, order[i]:order[i] + 1],
                                                 X[u % 2][:, i * P:i * P + P], ALU.mult, ALU.add)
                    if i < 4:
                        link(ins)
                ins.then_inc(kv_used, 1)

            def h_norm(c, h):
                dve.wait_ge(rrH_ready, 2 * c + h + 1)
                dve.wait_ge(out_ready, 2 * c + h + 1)
                v.tensor_tensor(AT[:, h, :].rearrange("p (n t) -> p n t", n=NCH),
                                LV[h].rearrange("p (n t) -> p n t", n=NCH),
                                bc(rrH[:, h, :].unsqueeze(2), [P, NCH, CH]), ALU.mult).then_inc(onH_ready, 1)

            def h_slot(c, s):
                if 1 <= s < 8:
                    h_join(c, s - 1, 0)
                    h_join(c, s - 1, 1)
                if s < 8:
                    h_pick(c, s, 0)
                    h_pick(c, s, 1)
                elif s == 9:
                    h_states(c, 0)
                    h_states(c, 1)
                elif s == 10:
                    h_states(c, 2)
                    h_states(c, 3)

            h_qmul(0, 0)
            h_qmul(0, 1)
            h_prep_gates(0)
            h_prep_queries(0)
            for p in range(1, PAIRS):
                for s in range(11):
                    h_slot(p - 1, s)
                    if s >= 9:
                        h_qmul(p, s - 9)
                h_prep_gates(p)
                h_norm(p - 1, 0)
                h_norm(p - 1, 1)
                h_prep_queries(p)
            for s in range(11):
                h_slot(PAIRS - 1, s)
                if s >= 3:
                    b, n = hblock(PAIRS, s)
                    dve.wait_ge(zsig_ready, s - 2)
                    v.tensor_tensor(zh[:, s - 3, :], PB[b][:, :], zh[:, s - 3, :], ALU.mult).then_inc(zh_ready, 1)
                    dve.wait_ge(zh_ready, s - 2)
                    dve.sem_inc(blk_free[b], 1)
            h_norm(PAIRS - 1, 0)
            h_norm(PAIRS - 1, 1)
            for head in range(HEADS):
                dve.wait_ge(oT_done, head + 1)
                v.tensor_tensor(oTH[:, head, :], oTH[:, head, :], zh[:, head, :], ALU.mult).then_inc(oTH_final, 1)

            dve.wait_ge(const_in, 16 * 23)
            link(v.tensor_scalar(gqk[:, 0, :], gqk[:, 0, :], DH ** -0.5, None, ALU.mult))
            for i in range(2):
                g = gqk[:, i:i + 1, :]
                v.tensor_tensor(cosg[:, i, :, :], cosg[:, i, :, :], bc(g, [P, 4, DH]), ALU.mult)
                for x_ in range(2):
                    for h in range(2):
                        lo = 32 * x_ + 16 * h
                        src = 32 * x_ + 16 * (1 - h)
                        v.tensor_tensor(sing[:, i, :, lo:lo + 16], sing[:, i, :, lo:lo + 16],
                                        bc(g[:, :, src:src + 16], [P, 4, 16]), ALU.mult)
            link(v.tensor_tensor(rtmp_lam[:, 0:4:2, :], rtmp_lam[:, 0:4:2, :], rtmp_lam[:, 1:4:2, :], ALU.mult))
            v.tensor_reduce(lame[:], rtmp_lam[:, 0:4:2, :], AX.X, ALU.add).then_inc(lamd_ready, 1)
            dve.wait_ge(lame_ready, 1)
            link(v.tensor_tensor(lamv[:], lame[:, 1:2], lame[:, 0:1], ALU.subtract))
            link(v.tensor_scalar(lamv[:], lamv[:], -LAM_INIT, None, ALU.add))
            v.tensor_scalar(gA[:], gA[:], 1.0 - LAM_INIT, None, ALU.mult).then_inc(tab_ready, 1)

            def a_rope(p, s):
                i = 5 * p + s - 5
                dve.wait_ge(raw_copied, i + 1)
                link_ss = v.tensor_reduce(ssn[:], rtmp[:, 1, :].rearrange("p (g d) -> p g d", d=DH), AX.X, ALU.add)
                link_ss.then_inc(ssn_ready, 1)
                dve.wait_ge(rrn_ready, i + 1)
                g3 = lambda ap: ap.rearrange("p (g d) -> p g d", d=DH)
                which = 0 if s < 7 else 1
                first = 2 * (s - 5) if s < 7 else 4 + 2 * (s - 7)
                lat = 2 * (s - 5) if s < 7 else 2 * (s - 8)
                if s == 5 and not (isinstance(p, int) and p == 0):
                    dve.wait_ge(qkT_ready, 2 * p)
                dst = qn[:, first:first + 2, :]
                if s == 7:
                    link(v.tensor_tensor(g3(rtmp[:, 2, :]), g3(rtmp[:, 0, :]), bc(rrn[:].unsqueeze(2), [P, 8, DH]),
                                         ALU.mult))
                    dve.sem_inc(u_ready, 1)
                    v.tensor_tensor(dst.rearrange("p t (g d) -> p (t g) d", d=DH), g3(rtmp[:, 2, :]),
                                    bc(gqk[:, 1:2, :], [P, 8, DH]), ALU.mult).then_inc(qn_ready, 1)
                    return
                v.tensor_tensor(g3(rtmp[:, 2, :]), g3(rtmp[:, 0, :]), bc(rrn[:].unsqueeze(2), [P, 8, DH]),
                                ALU.mult).then_inc(u_ready, 1)
                dve.wait_ge(u_ready, i + 1)
                for t in range(2):
                    uu = rtmp[:, 2, t * UC:(t + 1) * UC].rearrange("p (g a b d) -> p g a b d", a=2, b=2, d=16)
                    rr = rtmp[:, 1, t * UC:(t + 1) * UC].rearrange("p (g a b d) -> p g a b d", a=2, b=2, d=16)
                    sn = sing[:, which, lat + t, :].rearrange("p (a b d) -> p a b d", a=2, b=2)
                    for b_ in range(2):
                        last = v.tensor_tensor(rr[:, :, :, b_, :], uu[:, :, :, 1 - b_, :],
                                               bc(sn[:, :, b_, :].unsqueeze(1), [P, 4, 2, 16]), ALU.mult)
                link(last)
                dve.wait_ge(t1_ready, i + 1)
                v.tensor_tensor(dst, rtmp[:, 3, :].rearrange("p (t c) -> p t c", t=2),
                                rtmp[:, 1, :].rearrange("p (t c) -> p t c", t=2), ALU.add).then_inc(qn_ready, 1)

            def a_max(c, j):
                dve.wait_ge(s_ready, 8 * c + j + 1)
                for m in range(2):
                    v.tensor_reduce(nmax[:, j, m:m + 1], SB[:, 2 * m:2 * m + 2, 0:384], AX.XY, ALU.max,
                                    negate=True).then_inc(max_ready, 1)

            def a_weights(c, j):
                dve.wait_ge(exp_ready, 16 * c + 2 * j + 2)
                link(v.reciprocal(coef[:, j, 0:1], esum[:, j, 1:2]))
                link(v.tensor_tensor(coef[:, j, 1:2], coef[:, j, 0:1], esum[:, j, 0:1], ALU.mult))
                link(v.tensor_scalar(coef[:, j, 0:1], coef[:, j, 1:2], lamv[:, 0:1], None, ALU.mult))
                v.scalar_tensor_tensor(eA[:, j:j + 1], esum[:, j, 0:1], EPS, esum[:, j, 0:1], ALU.mult, ALU.mult)
                if not (isinstance(c, int) and c == 0 and j == 0):
                    dve.wait_ge(wT_ready, 8 * c + j)
                v.scalar_tensor_tensor(W_[:], E_[:, 1, :], coef[:, j, 0:1], E_[:, 0, :],
                                       ALU.mult, ALU.add).then_inc(w_ready, 1)

            def a_norm(c, j):
                dve.wait_ge(rrA_ready, 8 * c + j + 1)
                if not (isinstance(c, int) and c == 0 and j == 0):
                    dve.wait_ge(oTA_ready, 8 * c + j)
                v.tensor_scalar(on[:], WB[:, 768:896], rrA[:, j:j + 1], None, ALU.mult).then_inc(onA_ready, 1)

            def a_slot(c, s):
                if s >= 3:
                    a_norm(c, s - 3)
                if 1 <= s <= 8:
                    a_max(c, s - 1)
                    a_weights(c, s - 1)

            for s in range(5, 10):
                a_rope(0, s)
            for p in range(1, PAIRS):
                for s in range(10):
                    a_slot(p - 1, s)
                    if s == 9:
                        a_norm(p - 1, 7)
                    if s >= 5:
                        a_rope(p, s)
            for s in range(10):
                a_slot(PAIRS - 1, s)
            a_norm(PAIRS - 1, 7)

            dve.wait_ge(oTA_ready, 8 * PAIRS)
            dve.wait_ge(oTA_done, 8 * PAIRS)
            for k in range(KB):
                dve.wait_ge(ysig_ready, k + 1)
                link(v.tensor_tensor(zA[:, k, :], zA[:, k, :], ysig[:, k, :], ALU.mult))
                link(v.tensor_tensor(oTA[:, k, :], oTA[:, k, :], zA[:, k, :], ALU.mult))
                link(v.tensor_copy(yAh[:, k, :], oTA[:, k, :]))
                v.tensor_tensor(yAl[:, k, :], oTA[:, k, :], yAh[:, k, :].bitcast(F32),
                                ALU.subtract).then_inc(yA_ready, 1)
            for k in range(KB):
                link(v.tensor_copy(yHh[:, k, :], oTH[:, k, :]))
                v.tensor_tensor(yHl[:, k, :], oTH[:, k, :], yHh[:, k, :].bitcast(F32),
                                ALU.subtract).then_inc(yH_ready, 1)
            dve.wait_ge(gasig_ready, 1)
            for i, what in enumerate(M_ORDER):
                j = int(what[2])
                for cb in range(2):
                    k = 2 * j + cb
                    b, cnt = mblock(2 * i + cb)
                    if what[:2] == "ba":
                        dve.wait_ge(blk_ready[b], cnt + 1)
                        link(v.tensor_tensor(ga[:, k, :], PB[b][:, :], ga[:, k, :], ALU.mult))
                        dve.sem_inc(blk_free[b], 1)
                    elif what[:2] == "bh":
                        dve.wait_ge(blk_ready[b], cnt + 1)
                        dve.wait_ge(gh_ready, k + 1)
                        link(v.tensor_tensor(gh[:, j % 2, cb, :], PB[b][:, :], gh[:, j % 2, cb, :], ALU.mult))
                        dve.sem_inc(blk_free[b], 1)
                        link(v.tensor_tensor(ga[:, k, :], ga[:, k, :], gh[:, j % 2, cb, :], ALU.add))
                        link(v.tensor_copy(mTh[:, k, :], ga[:, k, :]))
                        v.tensor_tensor(mTl[:, k, :], ga[:, k, :], mTh[:, k, :].bitcast(F32),
                                        ALU.subtract).then_inc(m_ready, 1)
            b, cnt = mblock(2 * len(M_ORDER) - 1)
            dve.wait_ge(blk_ready[b], cnt + 1)
            v.tensor_copy(scb[:], bc(scT[:, :, 0:1], [P, KB, P])).then_inc(scb_ready, 1)
            for i in range(2):
                b, cnt = mblock(GATE_BLOCK + i)
                dve.wait_ge(gate_used, 2 * i + 2)
                g = gate[:, i * 512:(i + 1) * 512]
                v.tensor_tensor(g, PB[b][:, :], g, ALU.add).then_inc(gate_ready, 1)
                dve.wait_ge(gate_ready, i + 1)
                dve.sem_inc(blk_free[b], 1)
            dve.wait_ge(xb_in, 16)
            for n in range(8):
                u, half = divmod(n, 2)
                b, cnt = mblock(OUT_BLOCK + n)
                dve.wait_ge(blk_ready[b], cnt)
                c = slice(u * UC, (u + 1) * UC)
                if n >= 2:
                    dve.wait_ge(o_ready, n - 1)
                link(v.tensor_tensor(ytmp[:, n % 2, :, :], PB[b][:, :].rearrange("p (t c) -> p t c", t=2),
                                     bc(gate[:, c].unsqueeze(1), [P, 2, UC]), ALU.mult))
                dve.sem_inc(blk_free[b], 1)
                xx = xb[:, 2 * half:2 * half + 2, c]
                v.tensor_tensor(xx, xx, ytmp[:, n % 2, :, :], ALU.add).then_inc(o_ready, 1)

        @block.gpsimd
        def _(pool):
            link = Chain(pool, pool_chain)
            g = nc.gpsimd

            def split_lo(sl, n):
                pool.wait_ge(hi_ready, n + 1)
                g.tensor_tensor(wl[sl][:], wraw[sl][:], wh[sl][:].bitcast(F32), ALU.subtract).then_inc(lo_ready, 1)

            def rsqrt(dst, src, scale, eps, done):
                link(g.tensor_scalar(dst, src, scale, eps, ALU.mult, ALU.add))
                n = dst.shape[-1]
                return g.tensor_tensor(dst, dst, mhalf[:, 0:n], ALU.pow).then_inc(done, 1)

            link(g.memset(mhalf[:], -0.5))
            pool.wait_ge(ssx_ready, 1)
            rsqrt(rrx[:], ssx[:], 1.0 / D, EPS, rrx_ready)
            split_lo(0, 0)
            split_lo(1, 1)

            def h_rsqrt(c):
                for h in range(2):
                    pool.wait_ge(sqH_ready, 2 * c + h + 1)
                    rsqrt(rrH[:, h, :], ssH[:, h, :], 1.0 / P, EPS, rrH_ready)

            for p in range(PAIRS):
                for j in (2, 3, 4, 5):
                    if not (p == PAIRS - 1 and j >= 4):
                        pass
                    n = 4 * p + j
                    split_lo(n % 2, n)
                    if j == 4 and p > 0:
                        h_rsqrt(p - 1)
            for n in range(4 * PAIRS + 2, A_UNIT + 2):
                split_lo(n % 2, n)
            h_rsqrt(PAIRS - 1)

            def a_rsqrt(c, j):
                pool.wait_ge(sqA_ready, 8 * c + j + 1)
                link(g.tensor_scalar(rrA[:, j:j + 1], ssA[:, j:j + 1], 1.0 / P, None, ALU.mult))
                link(g.tensor_tensor(rrA[:, j:j + 1], rrA[:, j:j + 1], eA[:, j:j + 1], ALU.add))
                g.tensor_tensor(rrA[:, j:j + 1], rrA[:, j:j + 1], mhalf[:, 0:1], ALU.pow).then_inc(rrA_ready, 1)

            def a_rope(p, s):
                i = 5 * p + s - 5
                pool.wait_ge(ssn_ready, i + 1)
                rsqrt(rrn[:], ssn[:], 1.0 / DH, EPS, rrn_ready)
                pool.wait_ge(u_ready, i + 1)
                which = 0 if s < 7 else 1
                lat = 2 * (s - 5) if s < 7 else 2 * (s - 8)
                if s == 7:
                    return pool.sem_inc(t1_ready, 1)
                for t in range(2):
                    last = g.tensor_tensor(rtmp[:, 3, t * UC:(t + 1) * UC].rearrange("p (g d) -> p g d", d=DH),
                                           rtmp[:, 2, t * UC:(t + 1) * UC].rearrange("p (g d) -> p g d", d=DH),
                                           cosg[:, which, lat + t:lat + t + 1, :].to_broadcast([P, 4, DH]), ALU.mult)
                last.then_inc(t1_ready, 1)

            A_LO = {2: 1, 4: 2, 6: 3, 9: 4}

            def lo_after(p, s, table):
                if s in table:
                    sl, _, n = unit(A_UNIT, p, table[s])
                    split_lo(sl, n)

            for s in range(3, 10):
                if s >= 5:
                    a_rope(0, s)
                lo_after(0, s, {4: 2, 6: 3, 9: 4})
            for p in range(1, PAIRS):
                for s in range(10):
                    if s >= 3:
                        a_rsqrt(p - 1, s - 3)
                    if s == 9:
                        a_rsqrt(p - 1, 7)
                    if s >= 5:
                        a_rope(p, s)
                    lo_after(p, s, A_LO)
            for s in range(10):
                if s >= 3:
                    a_rsqrt(PAIRS - 1, s - 3)
                lo_after(PAIRS, s, {2: 1, 4: 2, 6: 3, 8: 4})
            a_rsqrt(PAIRS - 1, 7)
            for n in range(M_UNIT + 1, N_UNIT):
                split_lo(n % 2, n)


_INS = ["x", "c", "ctx", "c_ctx", "w_mod", "b_mod", "norm_gain", "w_in", "q_norm_gain", "k_norm_gain",
        "lambda_q1", "lambda_k1", "lambda_q2", "lambda_k2", "subln_gain", "hgrn_lb_fwd", "hgrn_lb_bwd",
        "hgrn_norm_gain", "w_br_attn", "w_br_hgrn", "w_out"]


def shape_constants():
    import numpy as np
    i = np.arange(CH)
    masks = np.zeros((CH, LEVELS + 1, CH), np.int32)
    masks[:, 0, :] = i[:, None] == i[None, :]
    for l in range(LEVELS):
        masks[:, l + 1, :] = ((i[:, None] >> (l + 1)) == (i[None, :] >> (l + 1))) & \
            ((i[:, None] >> l) != (i[None, :] >> l))
    row = np.repeat(np.arange(TL // GRID_W, dtype=np.float32), GRID_W)
    col = np.tile(np.arange(GRID_W, dtype=np.float32), TL // GRID_W)
    half = DH // 2
    inv = (10000.0 ** (-np.arange(0, half, 2, dtype=np.float32) / half)).astype(np.float32)
    ar, ac = row[:, None] * inv[None, :], col[:, None] * inv[None, :]
    ang = np.concatenate([ar, ar, ac, ac], axis=-1).astype(np.float32)
    sign = np.repeat(np.array([-1, 1, -1, 1], np.float32), DH // 4)
    return {"ident": np.eye(P, dtype=np.float32), "masks": masks,
            "cos": np.cos(ang).astype(np.float32), "sin": (np.sin(ang) * sign).astype(np.float32)}


def kernel(**inputs):
    import numpy as _np
    import concourse.bacc as _bacc
    from concourse import mybir as _mybir
    from concourse.bass_utils import run_bass_kernel_spmd as _run

    nc = _bacc.Bacc("TRN2", target_bir_lowering=False, num_devices=1)
    arrays, args = {}, {}
    for name, value in [(n, inputs[n]) for n in _INS] + list(shape_constants().items()):
        v = _np.ascontiguousarray(value)
        arrays[f"in_{name}_dram"] = v
        args[name] = nc.dram_tensor(f"in_{name}_dram", v.shape, _mybir.dt.from_np(v.dtype), kind="ExternalInput").ap()
    out = nc.dram_tensor("out_0_dram", (1, TL, D), _mybir.dt.float32, kind="ExternalOutput").ap()
    hybrid_layer(nc, args, out)
    r = _run(nc, [arrays], core_ids=[0])
    return r.results[0]["out_0_dram"]
```

```python
from contextlib import ExitStack

import concourse.bass as bass
from concourse import mybir

F32 = mybir.dt.float32
F32R = mybir.dt.float32r
I32 = mybir.dt.int32
ALU = mybir.AluOpType
ACT = mybir.ActivationFunctionType
AX = mybir.AxisListType

P = 128
D = 1024
KB = D // P
TC = 256
TL = 512
T = TC + TL
HEADS = 8
PAIRS = HEADS // 2
DH = 64
CH = 128
LEVELS = 7
NCH = TL // CH
UC = 256
EPS = 1e-6
GRID_W = 64
LAM_INIT = 0.8 - 0.6

COL = {"attn_k": 0, "attn_v": 1024, "hgrn_i": 2048, "hgrn_f": 3072, "hgrn_b": 4096, "attn_q": 5120,
       "hgrn_q": 6144, "attn_z": 7168, "hgrn_z": 8192, "gate_a": 9216, "gate_h": 10240}
LAT = slice(TC, T)
CTX = slice(0, TC)

A_UNIT = 4 * PAIRS + 4
M_UNIT = A_UNIT + 4 * PAIRS + 4
O_UNIT = M_UNIT + 12
N_UNIT = O_UNIT + 4
MOD_UNITS = 8
MOD_ORDER = (0, 4, 1, 5, 2, 6, 3, 7)
GATE_UNITS = 4


def unit(base, p, j):
    return (base + j) % 2, 2 * p + (base + j) // 2, 4 * p + (base + j)


def hblock(p, s):
    if isinstance(p, int) and p == 0:
        return s % 2, (s - 3) // 2 if s % 2 else (s - 4) // 2
    return s % 2, (5 * p - 1 + (s - 1) // 2 if s % 2 else 6 * p - 2 + s // 2)


A_BANK0 = 6 * PAIRS + 4
A_BANK1 = 5 * PAIRS + 4


def ablock(p, s):
    if isinstance(p, int) and p == 0:
        return s % 2, (A_BANK1 + (s - 3) // 2 if s % 2 else A_BANK0 + (s - 4) // 2)
    return s % 2, (A_BANK1 + 4 + 5 * (p - 1) + s // 2 if s % 2 else A_BANK0 + 3 + 5 * (p - 1) + s // 2)


M_BANK0 = A_BANK0 + 3 + 5 * PAIRS + 1
M_BANK1 = A_BANK1 + 4 + 5 * PAIRS


def mblock(n):
    return 1 - n % 2, (M_BANK0 if n % 2 else M_BANK1) + n // 2


M_ORDER = ["gh0", "gh1", "ba0", "bh0", "gh2", "ba1", "bh1", "gh3", "ba2", "bh2", "ba3", "bh3"]
OUT_BLOCK = 2 * len(M_ORDER)


class Chain:

    def __init__(self, eng, sem):
        self.eng, self.sem, self.n = eng, sem, 0

    def __call__(self, ins):
        self.n += 1
        ins.then_inc(self.sem, 1)
        self.eng.wait_ge(self.sem, self.n)


def hybrid_layer(nc, a, out):
    with ExitStack() as ctx:
        block = None

        def sem(name):
            return ctx.enter_context(nc.semaphore(name))

        base = (nc.sbuf_base + 63) // 64 * 64
        at = [base]

        def place(name, shape, dt=F32, offset=None):
            size = 1
            for d in shape[1:]:
                size *= d
            size *= 4
            if offset is None:
                offset = at[0]
                at[0] += (size + 31) // 32 * 32
            return nc.alloc_sbuf_tensor_at(name, shape, dt, offset=offset)

        hTh = place("hTh", [P, KB, T], F32R)
        hTl = place("hTl", [P, KB, T], F32R)
        wraw = [place(f"wraw{i}", [P, KB, UC]) for i in range(2)]
        wh = [place(f"wh{i}", [P, KB, UC], F32R) for i in range(2)]
        wl = [place(f"wl{i}", [P, KB, UC], F32R) for i in range(2)]
        ident = place("ident", [P, P])
        gate = place("gate", [P, D])
        mhalf = place("mhalf", [P, 16])
        scT = place("scT", [P, KB, 2])
        bmT = place("bmT", [P, 16])
        modT = place("modT", [P, 16, 2])
        gT = place("gT", [P, KB])
        ngT = place("ngT", [P, KB])
        lbraw = place("lbraw", [P, 2, 2, HEADS])
        lb = place("lb", [P, 2, HEADS])
        om = place("om", [P, 2, HEADS])
        nom = place("nom", [P, 2, HEADS])
        gH = place("gH", [P, 1])
        gA = place("gA", [P, 1])
        ssx = place("ssx", [P, 6])
        rrx = place("rrx", [P, 6])
        ssH = place("ssH", [P, 2, NCH])
        rrH = place("rrH", [P, 2, NCH])
        lamv = place("lamv", [P, 1])
        lame = place("lame", [P, 2])
        nmax = place("nmax", [P, 8, 2])
        esum = place("esum", [P, 8, 2])
        coef = place("coef", [P, 8, 2])
        ssA = place("ssA", [P, 8])
        eA = place("eA", [P, 8])
        rrA = place("rrA", [P, 8])
        ssn = place("ssn", [P, 8])
        rrn = place("rrn", [P, 8])
        R = (at[0] + 63) // 64 * 64
        K16 = 16384
        oTH = place("oTH", [P, HEADS, TL], offset=R)
        wmod = [place(f"wmod{u}", [P, KB, UC], offset=R + k * 8192) for u, k in
                enumerate((0, 1, 5, 7, 8, 9, 10, 11))]
        xt = place("xt", [P, 6, D], offset=R + K16)
        htmp = place("htmp", [P, 2, TL], offset=R + 3 * K16)
        sqx = place("sqx", [P, D], offset=R + 3 * K16 + 4096)
        o = R + K16
        qs = place("qs", [P, 2, TL], offset=o)
        sig = place("sig", [P, 2, 2, T], offset=o + 4096)
        zh = place("zh", [P, HEADS, TL], offset=o)
        o += K16
        K_ = place("K_", [P, 2, 2, T], offset=o); o += 12288
        Q_ = place("Q_", [P, 2, 2, TL], offset=o); o += 8192
        totE = place("totE", [P, 2, 2, T], offset=o); o += 12288
        totO = place("totO", [P, 2, 2, T // 2], offset=o); o += 6144
        mixQ = place("mixQ", [P, 2, TL], offset=o); o += 4096
        mixK = place("mixK", [P, 2, TL], offset=o); o += 4096
        V = place("V", [P, 6, UC], offset=o); o += 6144
        AT = place("AT", [P, 2, TL], offset=o); o += 4096
        S_ = place("S_", [P, 2, 2, NCH, P], offset=o); o += 8192
        masks = place("masks", [P, LEVELS + 1, CH], I32, offset=R + 6 * K16)
        ksum = place("ksum", [P, 2, TL], offset=o - 8192)
        oTA = place("oTA", [P, HEADS, TL], offset=R + K16)
        zA = place("zA", [P, HEADS, TL], offset=R + 2 * K16)
        ga = place("ga", [P, KB, TL], offset=R + 3 * K16)
        o2 = R + 3 * K16
        qn = place("qn", [P, 10, UC], offset=o2); o2 += 10240
        cosg = place("cosg", [P, 2, 4, DH], offset=o2); o2 += 2048
        sing = place("sing", [P, 2, 4, DH], offset=o2); o2 += 2048
        gqk = place("gqk", [P, 2, DH], offset=o2); o2 += 512
        rtmp = place("rtmp", [P, 4, 2 * UC], offset=o2); o2 += 8192
        rtmp_lam = place("rtmp_lam", [P, 4, DH], offset=o2 - 8192)
        o2 = (o2 + 63) // 64 * 64
        VA = place("VA", [P, 6, UC], offset=o2); o2 += 6144
        qT = place("qT", [P, 2, TL], offset=o2); o2 += 4096
        kT = place("kT", [P, 2, T], offset=o2); o2 += 6144
        E_ = place("E_", [P, 2, T], offset=o2); o2 += 6144
        W_ = place("W_", [P, T], offset=o2); o2 += 3072
        WT = place("WT", [P, T], offset=o2); o2 += 3072
        on = place("on", [P, P], offset=o2); o2 += 512
        osb = place("osb", [P, 2, P], offset=o2); o2 += 1024
        junk = place("junk", [P, P], offset=o2); o2 += 512
        yHh = place("yHh", [P, KB, TL], F32R, offset=R + 4 * K16)
        yHl = place("yHl", [P, KB, TL], F32R, offset=R)
        yAh = place("yAh", [P, KB, TL], F32R, offset=R + 5 * K16)
        ysig = place("ysig", [P, KB, TL], offset=R + 5 * K16)
        yAl = place("yAl", [P, KB, TL], F32R, offset=R + K16)
        mTh = place("mTh", [P, KB, TL], F32R, offset=R + 2 * K16)
        mTl = place("mTl", [P, KB, TL], F32R, offset=R + 3 * K16)
        gh = place("gh", [P, 2, 2, TL], offset=R + 6 * K16)
        xb = place("xb", [P, 4, D], offset=R + 4 * K16)
        ytmp = place("ytmp", [P, 2, 2, UC], offset=R + 6 * K16)

        PB = [ctx.enter_context(nc.psum_tensor(f"PB{i}", [P, 512], F32)) for i in range(2)]
        PX = ctx.enter_context(nc.psum_tensor("PX", [P, 6, 512], F32))
        LV = [PX[:, i, :] for i in range(2)]
        X = [PX[:, 2:4, :].rearrange("p a b -> p (a b)"),
             PX[:, 4:6, :].rearrange("p a b -> p (a b)")]
        SB = PX[:, 0:3, :].rearrange("p a b -> p (a b)")
        WB = PX[:, 3:5, :].rearrange("p a b -> p (a b)")
        OB = PX[:, 5, :]

        start_in = sem("start_in")
        const_in = sem("const_in")
        c_in = sem("c_in")
        mod_in = [sem(f"mod_in{u}") for u in range(MOD_UNITS)]
        x_in = sem("x_in")
        xb_in = sem("xb_in")
        raw_ready = [sem(f"raw_ready{i}") for i in range(2)]
        hi_ready = sem("hi_ready")
        lo_ready = sem("lo_ready")
        mod_used = sem("mod_used")
        gate_used = sem("gate_used")
        blk_ready = [sem(f"blk_ready{i}") for i in range(2)]
        blk_free = [sem(f"blk_free{i}") for i in range(2)]
        dve_chain = sem("dve_chain")
        act_chain = sem("act_chain")
        pool_chain = sem("pool_chain")
        sig_c = sem("sig_c")
        sc_ready = sem("sc_ready")
        mod_ready = sem("mod_ready")
        mod_final = sem("mod_final")
        ssx_ready = sem("ssx_ready")
        rrx_ready = sem("rrx_ready")
        xn_ready = sem("xn_ready")
        xT_ready = sem("xT_ready")
        xT_used = sem("xT_used")
        h_split = sem("h_split")
        lbd_ready = sem("lbd_ready")
        lb_ready = sem("lb_ready")
        qsig_ready = sem("qsig_ready")
        q_ready = sem("q_ready")
        sig_used = sem("sig_used")
        v_ready = sem("v_ready")
        diag_ready = sem("diag_ready")
        levels_ready = sem("levels_ready")
        mix_ready = sem("mix_ready")
        scores_ready = sem("scores_ready")
        scores_used = sem("scores_used")
        kT_ready = sem("kT_ready")
        kT_copied = sem("kT_copied")
        kv_ready = sem("kv_ready")
        kv_used = sem("kv_used")
        out_ready = sem("out_ready")
        sqH_ready = sem("sqH_ready")
        rrH_ready = sem("rrH_ready")
        onH_ready = sem("onH_ready")
        oT_ready = sem("oT_ready")
        oT_done = sem("oT_done")
        zsig_ready = sem("zsig_ready")
        zh_ready = sem("zh_ready")
        oTH_final = sem("oTH_final")
        lamd_ready = sem("lamd_ready")
        lame_ready = sem("lame_ready")
        tab_ready = sem("tab_ready")
        z_ready = sem("z_ready")
        va_ready = sem("va_ready")
        raw_copied = sem("raw_copied")
        ssn_ready = sem("ssn_ready")
        rrn_ready = sem("rrn_ready")
        u_ready = sem("u_ready")
        t1_ready = sem("t1_ready")
        qn_ready = sem("qn_ready")
        qkT_ready = sem("qkT_ready")
        qkT_copied = sem("qkT_copied")
        s_ready = sem("s_ready")
        s_shared = sem("s_shared")
        max_ready = sem("max_ready")
        exp_ready = sem("exp_ready")
        w_ready = sem("w_ready")
        wT_ready = sem("wT_ready")
        wT_copied = sem("wT_copied")
        pv_ready = sem("pv_ready")
        sqA_ready = sem("sqA_ready")
        rrA_ready = sem("rrA_ready")
        onA_ready = sem("onA_ready")
        oTA_ready = sem("oTA_ready")
        oTA_done = sem("oTA_done")
        ga_ready = sem("ga_ready")
        gasig_ready = sem("gasig_ready")
        ysig_ready = sem("ysig_ready")
        yH_ready = sem("yH_ready")
        yA_ready = sem("yA_ready")
        gh_ready = sem("gh_ready")
        m_ready = sem("m_ready")
        gate_in = [sem(f"gate_in{u}") for u in range(4)]
        gT_ready = sem("gT_ready")
        gate_bc = sem("gate_bc")
        gate_ready = sem("gate_ready")
        o_ready = sem("o_ready")
        out_done = sem("out_done")

        w_in = a["w_in"][0]
        w_mod = a["w_mod"][0]

        def unit_source(n):
            def cols(m, c0):
                return m[:, c0:c0 + UC].rearrange("(k p) c -> p k c", p=P)
            if n < A_UNIT:
                p, j = divmod(n, 4)
                if n >= 4 * PAIRS:
                    return cols(w_in, COL["hgrn_z"] + UC * (n - 4 * PAIRS))
                return cols(w_in, COL[("hgrn_f", "hgrn_b", "hgrn_q", "hgrn_i")[j]] + UC * p)
            if n < M_UNIT:
                n -= A_UNIT
                p, j = divmod(n, 4)
                if n >= 4 * PAIRS:
                    return cols(w_in, COL["gate_a"] + UC * (n - 4 * PAIRS))
                return cols(w_in, COL[("attn_q", "attn_k", "attn_z", "attn_v")[j]] + UC * p)
            if n < O_UNIT:
                kind, j = M_ORDER[n - M_UNIT][:2], int(M_ORDER[n - M_UNIT][2])
                if kind == "gh":
                    return cols(w_in, COL["gate_h"] + UC * j)
                return cols(a["w_br_attn"][0] if kind == "ba" else a["w_br_hgrn"][0], UC * j)
            return cols(a["w_out"][0], UC * (n - O_UNIT))

        block = ctx.enter_context(nc.Block())

        @block.sync
        def _(sp):
            sp.dma_start(xt[:, 0:2, :], a["ctx"][0].rearrange("(t p) d -> p t d", p=P)).then_inc(x_in, 16)
            sp.dma_start(xt[:, 2:6, :], a["x"][0].rearrange("(t p) d -> p t d", p=P)).then_inc(x_in, 16)

            def mod_load(u, dst, signal):
                sp.dma_start(dst[:], w_mod[:, u * UC:(u + 1) * UC].rearrange("(k p) c -> p k c", p=P)
                             ).then_inc(signal, 16)

            def unit_load(n):
                if n >= 2:
                    sp.wait_ge(lo_ready, n - 1)
                sp.dma_start(wraw[n % 2][:], unit_source(n)).then_inc(raw_ready[n % 2], 16)

            for i, u in enumerate(MOD_ORDER):
                mod_load(u, wmod[u], mod_in[u])
                if i in (3, 7):
                    unit_load(i // 4)
            sp.wait_ge(mod_used, 3)
            mod_load(8, wmod[0], gate_in[0])
            mod_load(9, wmod[1], gate_in[1])
            for n in range(2, N_UNIT):
                unit_load(n)
                if n == 4:
                    sp.wait_ge(gate_used, 2)
                    mod_load(10, wmod[0], gate_in[2])
                    mod_load(11, wmod[1], gate_in[3])
            sp.wait_ge(m_ready, 8)
            sp.dma_start(xb[:], a["x"][0].rearrange("(t p) d -> p t d", p=P)).then_inc(xb_in, 16)
            ov = out[0].rearrange("(t p) d -> p t d", p=P)
            for n in range(8):
                sp.wait_ge(o_ready, n + 1)
                u, h = divmod(n, 2)
                sp.dma_start(ov[:, 2 * h:2 * h + 2, u * UC:(u + 1) * UC],
                             xb[:, 2 * h:2 * h + 2, u * UC:(u + 1) * UC]).then_inc(out_done, 16)
            sp.wait_ge(out_done, 16 * 8)

        @block.tensor
        def _(pe):
            def mm3(dst, xh, xl, yh, yl, first, last):
                nc.tensor.matmul(dst, xh, yh, start=first, stop=False)
                nc.tensor.matmul(dst, xh, yl, start=False, stop=False)
                return nc.tensor.matmul(dst, xl, yh, start=False, stop=last)

            def feature_block(dst, s, cb, cols, ks=range(KB), yh=hTh, yl=hTl):
                c = slice(cb * P, cb * P + P)
                for k in ks:
                    last = mm3(dst, wh[s][:, k, c], wl[s][:, k, c], yh[:, k, cols], yl[:, k, cols],
                               k == 0, k == KB - 1)
                return last

            def token_tile(dst, s, t, ks=range(KB), yh=hTh, yl=hTl):
                c = slice(t * P, t * P + P)
                for k in ks:
                    last = mm3(dst, yh[:, k, c], yl[:, k, c], wh[s][:, k, :], wl[s][:, k, :],
                               k == 0, k == KB - 1)
                return last

            def open_block(b, n):
                if not (isinstance(n, int) and n == 0):
                    pe.wait_ge(blk_free[b], n)

            def h_proj(p, s):
                b, n = hblock(p, s)
                j = -1 if s < 3 else (s - 3) // 3
                ws, _, wn = unit(0, p, j)
                if s in (0, 3, 6, 9):
                    pe.wait_ge(lo_ready, wn + 1)
                open_block(b, n)
                if s < 3:
                    for i in range(2):
                        last = token_tile(PB[b][:, i * UC:(i + 1) * UC], ws, 2 * s + i)
                elif s in (5, 8):
                    for cb in range(2):
                        last = feature_block(PB[b][:, cb * UC:(cb + 1) * UC], ws, cb, CTX)
                else:
                    cb = (s - 3) % 3 if s < 9 else s - 9
                    last = feature_block(PB[b][:, :], ws, cb, LAT)
                last.then_inc(blk_ready[b], 1)

            def h_scores(c, st):
                for h in range(2):
                    if st == 0:
                        pe.wait_ge(diag_ready, 2 * c + h + 1)
                        if not (isinstance(c, int) and c == 0):
                            pe.wait_ge(onH_ready, 2 * c + h - 1)
                    else:
                        pe.wait_ge(mix_ready, 14 * c + 2 * (st - 1) + h + 1)
                        pe.wait_ge(scores_used, 16 * c + 2 * (st - 1) + h + 1)
                    for ch in range(NCH):
                        t = slice(ch * CH, ch * CH + CH)
                        kk, qq = (ksum, qs) if st == 0 else (mixK, mixQ)
                        last = nc.tensor.matmul(LV[h][:, t], kk[:, h, t], qq[:, h, t], start=True, stop=True)
                    last.then_inc(scores_ready, 1)

            ORDER = [(0, 1, 2, 3, 4), (1, 0, 5, 4, 3)]

            def h_keysT(c, u):
                h, d = divmod(u, 2)
                pe.wait_ge(levels_ready, 16 * c + 14 + h + 1)
                if u >= 2:
                    pe.wait_ge(kv_used, 4 * c + u - 1)
                elif not (isinstance(c, int) and c == 0):
                    pe.wait_ge(oT_done, 2 * c)
                else:
                    pe.wait_ge(gate_ready, 1)
                for i, ch in enumerate(ORDER[d]):
                    last = nc.tensor.transpose(X[u % 2][:, i * P:i * P + P], K_[:, h, d, ch * CH:ch * CH + CH],
                                               ident[:])
                last.then_inc(kT_ready, 1)

            def h_kv(c, u):
                h, d = divmod(u, 2)
                pe.wait_ge(kT_copied, 4 * c + u + 1)
                pe.wait_ge(v_ready, 3 * c + 3)
                for i, ch in enumerate(ORDER[d]):
                    last = nc.tensor.matmul(X[u % 2][:, i * P:i * P + P], totE[:, h, d, i * CH:i * CH + CH],
                                            V[:, ch, h * P:h * P + P], start=True, stop=True)
                last.then_inc(kv_ready, 1)

            def h_out(c, h):
                pe.wait_ge(kv_used, 4 * c + 2 * h + 2)
                pe.wait_ge(scores_used, 16 * c + 14 + h + 1)
                for ch in range(NCH):
                    t = slice(ch * CH, ch * CH + CH)
                    dst = LV[h][:, t]
                    nc.tensor.matmul(dst, AT[:, h, t], V[:, 2 + ch, h * P:h * P + P], start=True, stop=False)
                    nc.tensor.matmul(dst, Q_[:, h, 0, t], S_[:, h, 0, ch, :], start=False, stop=False)
                    last = nc.tensor.matmul(dst, Q_[:, h, 1, t], S_[:, h, 1, ch, :], start=False, stop=True)
                last.then_inc(out_ready, 1)

            def h_outT(c, h):
                pe.wait_ge(onH_ready, 2 * c + h + 1)
                pe.wait_ge(kv_used, 4 * c + 4)
                for ch in range(NCH):
                    t = slice(ch * CH, ch * CH + CH)
                    last = nc.tensor.transpose(X[h][:, t], AT[:, h, t], ident[:])
                last.then_inc(oT_ready, 1)

            def h_core(c, s):
                if s == 0:
                    return
                if s < 8:
                    if s == 1:
                        h_scores(c, 0)
                    h_scores(c, s)
                elif s == 8:
                    h_keysT(c, 0)
                    h_keysT(c, 1)
                elif s == 9:
                    h_kv(c, 0)
                    h_kv(c, 1)
                    h_keysT(c, 2)
                    h_keysT(c, 3)
                else:
                    h_kv(c, 2)
                    h_kv(c, 3)
                    h_out(c, 0)
                    h_out(c, 1)

            def mod_pair(i):
                for u in (i, i + 4):
                    pe.wait_ge(mod_in[u], 16)
                    for cb in range(2):
                        q = 4 * (u // 4) + 2 * cb
                        for k in range(KB):
                            last = nc.tensor.matmul(PX[:, 2 + i, q:q + 2], wmod[u][:, k, cb * P:cb * P + P],
                                                    scT[:, k, :], start=(k == 0), stop=(k == KB - 1))
                    last.then_inc(mod_used, 1)

            def x_transposes(i):
                for g in range(4 * i, 4 * i + 4):
                    k, c = divmod(g, 2)
                    if g >= 2:
                        pe.wait_ge(xT_used, g - 1)
                    for t0, t in enumerate(range(2) if c else range(2, 6)):
                        last = nc.tensor.transpose(LV[g % 2][:, t0 * P:t0 * P + P], xt[:, t, k * P:k * P + P],
                                                   ident[:])
                    last.then_inc(xT_ready, 1)

            def first_blocks(i):
                if i == 0:
                    pe.wait_ge(lo_ready, 1)
                for k in (2 * i, 2 * i + 1):
                    pe.wait_ge(h_split, 2 * k + 1)
                    for cb in range(2):
                        last = feature_block(PB[1 - cb][:, :], 0, cb, LAT, [k])
                        if k == KB - 1:
                            last.then_inc(blk_ready[1 - cb], 1)

            def mod_gate(u):
                pe.wait_ge(gate_in[u], 16)
                for cb in range(2):
                    for k in range(KB):
                        q = 4 * u + 2 * cb
                        last = nc.tensor.matmul(PX[:, 5, 32 + q:34 + q], wmod[u % 2][:, k, cb * P:cb * P + P],
                                                scT[:, k, :], start=(k == 0), stop=(k == KB - 1))
                last.then_inc(gate_used, 1)

            pe.wait_ge(sc_ready, 1)
            mod_pair(0)
            pe.wait_ge(start_in, 16 * 4)
            pe.wait_ge(xn_ready, 6)
            x_transposes(0)
            mod_pair(1)
            x_transposes(1)
            for i in range(2, 4):
                first_blocks(i - 2)
                mod_pair(i)
                x_transposes(i)
            first_blocks(2)
            first_blocks(3)
            pe.wait_ge(h_split, 2 * KB)
            for s in range(5, 11):
                h_proj(0, s)
                if s in (5, 8):
                    pe.wait_ge(mod_final, 4)
                    for u in range(2):
                        mod_gate(2 * (s // 8) + u)
            pe.wait_ge(gT_ready, 1)
            for k in range(KB):
                last = nc.tensor.matmul(X[1][:, k * P:k * P + P], gT[:, k:k + 1].to_broadcast([P, P]), ident[:],
                                        start=True, stop=True)
            last.then_inc(gate_bc, 1)
            for p in range(1, PAIRS):
                for s in range(11):
                    h_proj(p, s)
                    if s == 1 and p > 1:
                        h_outT(p - 2, 0)
                        h_outT(p - 2, 1)
                    h_core(p - 1, s)
            for s in range(11):
                if s < 3:
                    h_proj(PAIRS, s)
                else:
                    b, n = hblock(PAIRS, s)
                    u, cb = divmod(s - 3, 2)
                    if cb == 0:
                        pe.wait_ge(lo_ready, 4 * PAIRS + u + 1)
                    open_block(b, n)
                    feature_block(PB[b][:, :], u % 2, cb, LAT).then_inc(blk_ready[b], 1)
                if s == 1:
                    h_outT(PAIRS - 2, 0)
                    h_outT(PAIRS - 2, 1)
                h_core(PAIRS - 1, s)

            def a_proj(p, s, ks):
                b, n = ablock(p, s)
                j = -1 if s < 3 else 0 if s < 5 else 1 if s < 8 else 2
                ws, _, wn = unit(A_UNIT, p, j)
                if ks == 0:
                    if s in (0, 3, 5, 8):
                        pe.wait_ge(lo_ready, wn + 1)
                    open_block(b, n)
                if s >= 8:
                    last = feature_block(PB[b][:, :], ws, s - 8, LAT, range(4 * ks, 4 * ks + 4))
                else:
                    t = (2 * s if s < 3 else 2 + 2 * (s - 3) if s < 5 else 2 * (s - 5)) + ks
                    last = token_tile(PB[b][:, ks * UC:(ks + 1) * UC], ws, t)
                if ks == 1:
                    last.then_inc(blk_ready[b], 1)

            def ga_proj(s, ks):
                b, n = ablock(PAIRS, s)
                u, cb = divmod(s - 3, 2)
                if ks == 0:
                    if cb == 0:
                        pe.wait_ge(lo_ready, A_UNIT + 4 * PAIRS + u + 1)
                    open_block(b, n)
                last = feature_block(PB[b][:, :], u % 2, cb, LAT, range(4 * ks, 4 * ks + 4))
                if ks == 1:
                    last.then_inc(blk_ready[b], 1)

            def a_qkT(c, h):
                pe.wait_ge(qn_ready, 5 * (c + 1))
                if h == 0:
                    if not (isinstance(c, int) and c == 0):
                        pe.wait_ge(exp_ready, 16 * c)
                    else:
                        pe.wait_ge(oT_done, 2 * PAIRS)
                        pe.wait_ge(kv_used, 4 * PAIRS)
                else:
                    pe.wait_ge(qkT_copied, 2 * c + 1)
                for i in range(4):
                    nc.tensor.transpose(SB[:, i * P:i * P + P], qn[:, i, h * P:h * P + P], ident[:])
                for i in range(6):
                    last = nc.tensor.transpose(SB[:, 512 + i * P:512 + (i + 1) * P],
                                               qn[:, 4 + i, h * P:h * P + P], ident[:])
                last.then_inc(qkT_ready, 1)

            def a_scores(c, j):
                h, qt = divmod(j, 4)
                if j == 0:
                    pe.wait_ge(qkT_copied, 2 * c + 2)
                if not (isinstance(c, int) and c == 0 and j == 0):
                    pe.wait_ge(exp_ready, 16 * c + 2 * j)
                for m, k0, k1 in ((0, 512, 768), (1, 256, 768), (0, 0, 512), (1, 0, 256)):
                    if (m, k0) == (1, 0):
                        pe.wait_ge(s_shared, 8 * c + j + 1)
                    r = slice(m * DH, m * DH + DH)
                    last = nc.tensor.matmul(SB[:, m * T + k0:m * T + k1], qT[r, h, qt * P:qt * P + P],
                                            kT[r, h, k0:k1], start=True, stop=True)
                    if (m, k0) == (0, 512):
                        last.then_inc(s_shared, 1)
                last.then_inc(s_ready, 1)

            def a_wT(c, j):
                pe.wait_ge(w_ready, 8 * c + j + 1)
                if not (isinstance(c, int) and c == 0 and j == 0):
                    pe.wait_ge(wT_copied, 8 * c + j)
                for i in range(6):
                    last = nc.tensor.transpose(WB[:, i * P:i * P + P], W_[:, i * P:i * P + P], ident[:])
                last.then_inc(wT_ready, 1)

            def a_pv(c, j):
                h = j // 4
                pe.wait_ge(wT_copied, 8 * c + j + 1)
                pe.wait_ge(va_ready, 3 * c + 3)
                if not (isinstance(c, int) and c == 0 and j == 0):
                    pe.wait_ge(sqA_ready, 8 * c + j)
                    if not (isinstance(c, int) and c == 0 and j == 1):
                        pe.wait_ge(oTA_done, 8 * c + max(j - 1, 0))
                for i in range(6):
                    last = nc.tensor.matmul(OB[:, 0:128], WT[:, i * P:i * P + P], VA[:, i, h * P:h * P + P],
                                            start=(i == 0), stop=(i == 5))
                last.then_inc(pv_ready, 1)

            def a_outT(c, j):
                pe.wait_ge(onA_ready, 8 * c + j + 1)
                pe.wait_ge(sqA_ready, 8 * c + min(j + 2, 8))
                if j == 7:
                    pe.wait_ge(oTA_done, 8 * c + 7)
                nc.tensor.transpose(OB[:, 128:256], on[:], ident[:]).then_inc(oTA_ready, 1)

            def a_slot(c, s, proj):
                proj(0)
                if s <= 1 and c > 0:
                    a_outT(c - 1, 6 + s)
                if s == 0:
                    proj(1)
                    a_qkT(c, 0)
                    a_qkT(c, 1)
                    return
                if s <= 8:
                    a_scores(c, s - 1)
                if s >= 4:
                    a_outT(c, s - 4)
                if s >= 2:
                    a_wT(c, s - 2)
                proj(1)
                if s >= 2:
                    a_pv(c, s - 2)

            for s in range(3, 10):
                a_proj(0, s, 0)
                a_proj(0, s, 1)
                if s == 4:
                    h_outT(PAIRS - 1, 0)
                    h_outT(PAIRS - 1, 1)
            for p in range(1, PAIRS):
                for s in range(10):
                    a_slot(p - 1, s, lambda ks: a_proj(p, s, ks))
            for s in range(10):
                if s < 3:
                    a_slot(PAIRS - 1, s, lambda ks: a_proj(PAIRS, s, ks))
                else:
                    a_slot(PAIRS - 1, s, lambda ks: ga_proj(s, ks))
            ga_proj(10, 0)
            a_outT(PAIRS - 1, 6)
            ga_proj(10, 1)
            a_outT(PAIRS - 1, 7)

            for i, what in enumerate(M_ORDER):
                n = M_UNIT + i
                pe.wait_ge(lo_ready, n + 1)
                for cb in range(2):
                    b, cnt = mblock(2 * i + cb)
                    open_block(b, cnt)
                    if what[:2] == "gh":
                        last = feature_block(PB[b][:, :], n % 2, cb, LAT)
                    else:
                        ready, yh, yl = (yA_ready, yAh, yAl) if what[:2] == "ba" else (yH_ready, yHh, yHl)
                        for k in range(KB):
                            pe.wait_ge(ready, k + 1)
                            last = feature_block(PB[b][:, :], n % 2, cb, slice(0, TL), [k], yh, yl)
                    last.then_inc(blk_ready[b], 1)
            pe.wait_ge(m_ready, 8)
            for i in range(4):
                pe.wait_ge(lo_ready, O_UNIT + i + 1)
                for half in range(2):
                    b, cnt = mblock(OUT_BLOCK + 2 * i + half)
                    open_block(b, cnt)
                    for t in range(2):
                        last = token_tile(PB[b][:, t * UC:(t + 1) * UC], (O_UNIT + i) % 2, 2 * half + t,
                                          range(KB), mTh, mTl)
                    last.then_inc(blk_ready[b], 1)

        @block.scalar
        def _(act):
            link = Chain(act, act_chain)
            f = nc.scalar.activation

            def load(dst, src, signal=const_in):
                act.dma_start(dst, src, allow_slow_non_contiguous=True).then_inc(signal, 16)

            load(scT[:, :, 0], a["c"][0].rearrange("(k p) -> p k", p=P), c_in)
            load(scT[:, :, 1], a["c_ctx"].rearrange("(k p) -> p k", p=P), c_in)
            load(ident[:], a["ident"], start_in)
            for i in range(2):
                load(bmT[:, KB * i:KB * i + KB], a["b_mod"][0, i * D:(i + 1) * D].rearrange("(j p) -> p j", p=P),
                     start_in)
            load(ngT[:], a["norm_gain"][0].rearrange("(k p) -> p k", p=P), start_in)
            act.wait_ge(c_in, 32)
            f(modT[:, 0:KB, :], scT[:], ACT.Sigmoid).then_inc(sig_c, 1)
            act.wait_ge(x_in, 32)
            for t in range(6):
                link(f(sqx[:], xt[:, t, :], ACT.Square, accum_out=ssx[:, t:t + 1]))
            act.sem_inc(ssx_ready, 1)
            load(gH[:], a["hgrn_norm_gain"][0].rearrange("(p o) -> p o", o=1))
            load(gA[:], a["subln_gain"][0].rearrange("(p o) -> p o", o=1))
            load(gate[:], a["b_mod"][0:1, 2 * D:3 * D].to_broadcast([P, D]))
            load(masks[:], a["masks"])
            for d, name in enumerate(("hgrn_lb_fwd", "hgrn_lb_bwd")):
                for l in range(2):
                    load(lbraw[:, d, l, :], a[name][l].rearrange("(h p) -> p h", p=P))
            for g in range(2 * KB):
                k, c = divmod(g, 2)
                n = TC if c else TL
                if g % 4 == 0:
                    act.wait_ge(mod_final, g // 4 + 1)
                act.wait_ge(xT_ready, g + 1)
                if g >= 2:
                    act.wait_ge(h_split, g - 1)
                f(htmp[:, g % 2, 0:n], LV[g % 2][:, 0:n], ACT.Identity, scale=modT[:, KB + k, c:c + 1],
                  bias=modT[:, k, c:c + 1]).then_inc(xT_used, 1)
                if g in (7, 15):
                    act.wait_ge(raw_ready[g // 8], 16)
                    f(wh[g // 8][:], wraw[g // 8][:], ACT.Copy).then_inc(hi_ready, 1)
            act.wait_ge(lbd_ready, 1)
            f(lb[:], om[:], ACT.Sigmoid).then_inc(lb_ready, 1)
            act.wait_ge(lb_ready, 1)
            f(om[:], om[:], ACT.Sigmoid, scale=-1.0).then_inc(lb_ready, 1)

            def h_evac(p, s):
                b, n = hblock(p, s)
                act.wait_ge(blk_ready[b], n + 1)
                if s < 3:
                    c = p - 1
                    if not (isinstance(c, int) and c == 0):
                        act.wait_ge(out_ready, 2 * c)
                    f(V[:, 2 * s:2 * s + 2, :], PB[b][:, :].rearrange("p (t c) -> p t c", t=2),
                      ACT.Copy).then_inc(v_ready, 1)
                    act.wait_ge(v_ready, 3 * c + s + 1)
                    act.sem_inc(blk_free[b], 1)
                    return
                if s == 3 and not (isinstance(p, int) and p == 0):
                    act.wait_ge(sig_used, 2 * p)
                if s < 9:
                    d, i = divmod(s - 3, 3)
                    if i == 2:
                        f(sig[:, :, d, 0:TC], PB[b][:, :].rearrange("p (h t) -> p h t", h=2),
                          ACT.Sigmoid).then_inc(blk_free[b], 1)
                    else:
                        f(sig[:, i, d, LAT], PB[b][:, :], ACT.Sigmoid).then_inc(blk_free[b], 1)
                else:
                    if not (isinstance(p, int) and p == 0):
                        act.wait_ge(scores_ready, 16 * (p - 1) + 2)
                    f(qs[:, s - 9, :], PB[b][:, :], ACT.Sigmoid).then_inc(qsig_ready, 1)

            def halves(ap, l, which, n=TL):
                B = 1 << l
                return ap.rearrange("p (n two b) -> p n two b", two=2, b=B)[:, :, which, :]

            def h_mix(c, st):
                l = st - 1
                for h in range(2):
                    act.wait_ge(levels_ready, 16 * c + 2 * l + h + 1)
                    if l > 0:
                        act.wait_ge(scores_ready, 16 * c + 2 * l + h + 1)
                    elif not (isinstance(c, int) and c == 0):
                        act.wait_ge(scores_ready, 16 * c)
                    for dst, src, side in ((mixQ, Q_, 0), (mixK, K_, 1)):
                        cols = slice(0, TL) if side == 0 else LAT
                        f(halves(dst[:, h, :], l, 1 - side), halves(src[:, h, 0, cols], l, 1 - side), ACT.Copy)
                        last = f(halves(dst[:, h, :], l, side), halves(src[:, h, 1, cols], l, side), ACT.Copy)
                    last.then_inc(mix_ready, 1)

            def h_keysT_copy(c, u):
                h, d = divmod(u, 2)
                act.wait_ge(kT_ready, 4 * c + u + 1)
                f(totE[:, h, d, 0:640], X[u % 2][:, 0:640], ACT.Copy).then_inc(kT_copied, 1)

            def h_square(c, h):
                act.wait_ge(out_ready, 2 * c + h + 1)
                if not (isinstance(c, int) and c == 0):
                    act.wait_ge(rrH_ready, 2 * c)
                for ch in range(NCH):
                    last = f(mixQ[:, h, ch * P:ch * P + P], LV[h][:, ch * P:ch * P + P], ACT.Square,
                             accum_out=ssH[:, h, ch:ch + 1])
                link(last)
                act.sem_inc(sqH_ready, 1)

            def h_outT_copy(c, h, head):
                act.wait_ge(oT_ready, 2 * c + h + 1)
                f(oTH[:, head, :], X[h][:, 0:TL], ACT.Copy, scale=gH[:, 0:1]).then_inc(oT_done, 1)

            def h_slot_core(c, s):
                if s < 7:
                    h_mix(c, s + 1)
                elif s == 8:
                    h_keysT_copy(c, 0)
                    h_keysT_copy(c, 1)
                elif s == 9:
                    h_keysT_copy(c, 2)
                    h_keysT_copy(c, 3)
                elif s == 10:
                    h_square(c, 0)
                    h_square(c, 1)

            HI_AT = {2: 1, 5: 2, 8: 3, 10: 4}

            def hi_after(base_, p, s, table):
                if s in table:
                    sl, cnt, n = unit(base_, p, table[s])
                    act.wait_ge(raw_ready[sl], 16 * (cnt + 1))
                    f(wh[sl][:], wraw[sl][:], ACT.Copy).then_inc(hi_ready, 1)

            for s in range(3, 11):
                h_evac(0, s)
                hi_after(0, 0, s, {5: 2, 8: 3, 10: 4})
            for p in range(1, PAIRS):
                for s in range(11):
                    h_evac(p, s)
                    if s == 1 and p > 1:
                        h_outT_copy(p - 2, 0, 2 * (p - 2))
                        h_outT_copy(p - 2, 1, 2 * (p - 2) + 1)
                    h_slot_core(p - 1, s)
                    hi_after(0, p, s, HI_AT)
            for s in range(11):
                if s < 3:
                    h_evac(PAIRS, s)
                else:
                    b, n = hblock(PAIRS, s)
                    act.wait_ge(blk_ready[b], n + 1)
                    if s == 3:
                        act.wait_ge(sig_used, 2 * PAIRS)
                    f(zh[:, s - 3, :], PB[b][:, :], ACT.Sigmoid).then_inc(zsig_ready, 1)
                if s == 1:
                    h_outT_copy(PAIRS - 2, 0, HEADS - 4)
                    h_outT_copy(PAIRS - 2, 1, HEADS - 3)
                h_slot_core(PAIRS - 1, s)
                hi_after(0, PAIRS, s, {2: 1, 4: 2, 6: 3, 8: 4, 10: 5})
            h_outT_copy(PAIRS - 1, 0, HEADS - 2)
            h_outT_copy(PAIRS - 1, 1, HEADS - 1)

            act.wait_ge(onH_ready, 2 * PAIRS)
            act.wait_ge(oT_done, 2 * PAIRS)
            act.wait_ge(oTH_final, 8)
            for i in range(2):
                act.dma_start(cosg[:, i, :, :], a["cos"].rearrange("(t p) d -> p t d", p=P)).then_inc(const_in, 16)
                act.dma_start(sing[:, i, :, :], a["sin"].rearrange("(t p) d -> p t d", p=P)).then_inc(const_in, 16)
            for i, name in enumerate(("q_norm_gain", "k_norm_gain")):
                act.dma_start(gqk[:, i, :], a[name][0:1, :].to_broadcast([P, DH])).then_inc(const_in, 16)
            for i, name in enumerate(("lambda_q1", "lambda_k1", "lambda_q2", "lambda_k2")):
                act.dma_start(rtmp_lam[:, i, :], a[name][0:1, :].to_broadcast([P, DH])).then_inc(const_in, 16)
            act.wait_ge(lamd_ready, 1)
            f(lame[:], lame[:], ACT.Exp).then_inc(lame_ready, 1)

            def a_evac(p, s):
                b, n = ablock(p, s)
                act.wait_ge(blk_ready[b], n + 1)
                if s < 3:
                    if not (isinstance(p, int) and p == 1):
                        act.wait_ge(pv_ready, 8 * (p - 1))
                    f(VA[:, 2 * s:2 * s + 2, :], PB[b][:, :].rearrange("p (t c) -> p t c", t=2),
                      ACT.Copy).then_inc(va_ready, 1)
                    act.wait_ge(va_ready, 3 * (p - 1) + s + 1)
                    act.sem_inc(blk_free[b], 1)
                elif s >= 8:
                    f(zA[:, 2 * p + s - 8, :], PB[b][:, :], ACT.Copy).then_inc(blk_free[b], 1)
                else:
                    i = 5 * p + s - 3
                    if not (isinstance(i, int) and i == 0):
                        act.wait_ge(qn_ready, i)
                    else:
                        act.wait_ge(tab_ready, 1)
                    f(rtmp[:, 0, :], PB[b][:, :], ACT.Copy)
                    link(f(rtmp[:, 1, :], PB[b][:, :], ACT.Square))
                    act.sem_inc(blk_free[b], 1)
                    act.sem_inc(raw_copied, 1)

            def a_qkT_copy(c, h):
                act.wait_ge(qkT_ready, 2 * c + h + 1)
                f(qT[:, h, :], SB[:, 0:TL], ACT.Copy)
                f(kT[:, h, :], SB[:, TL:TL + T], ACT.Copy).then_inc(qkT_copied, 1)

            def a_square(c, j):
                act.wait_ge(pv_ready, 8 * c + j + 1)
                if not (isinstance(c, int) and c == 0 and j < 2):
                    act.wait_ge(onA_ready, 8 * c + j - 1)
                f(osb[:, j % 2, :], OB[:, 0:128], ACT.Copy)
                link(f(junk[:], OB[:, 0:128], ACT.Square, accum_out=ssA[:, j:j + 1]))
                act.sem_inc(sqA_ready, 1)

            def a_outT_copy(c, j):
                h, qt = divmod(j, 4)
                act.wait_ge(oTA_ready, 8 * c + j + 1)
                f(oTA[:, 2 * c + h, qt * P:qt * P + P], OB[:, 128:256], ACT.Copy,
                  scale=gA[:, 0:1]).then_inc(oTA_done, 1)

            def a_wT_copy(c, j):
                act.wait_ge(wT_ready, 8 * c + j + 1)
                f(WT[:], WB[:, 0:768], ACT.Copy).then_inc(wT_copied, 1)

            def a_exp(c, j):
                act.wait_ge(max_ready, 8 * c + j + 1)
                for m in range(2):
                    if not (isinstance(c, int) and c == 0 and j == 0):
                        act.wait_ge(w_ready, 8 * c + j)
                    link(f(E_[:, m, :], SB[:, m * T:(m + 1) * T], ACT.Exp,
                           bias=nmax[:, j, m:m + 1], accum_out=esum[:, j, m:m + 1]))
                    act.sem_inc(exp_ready, 1)

            def a_slot_core(c, s):
                if s == 0:
                    if c > 0:
                        a_outT_copy(c - 1, 6)
                    a_qkT_copy(c, 0)
                    a_qkT_copy(c, 1)
                    return
                if s == 1 and c > 0:
                    a_outT_copy(c - 1, 7)
                if s >= 3:
                    a_square(c, s - 3)
                if s >= 4:
                    a_outT_copy(c, s - 4)
                if s >= 2:
                    a_wT_copy(c, s - 2)
                if s <= 8:
                    a_exp(c, s - 1)

            A_HI = {2: 1, 4: 2, 7: 3, 9: 4}
            for s in range(3, 10):
                a_evac(0, s)
                hi_after(A_UNIT, 0, s, {4: 2, 7: 3, 9: 4})
            for p in range(1, PAIRS):
                for s in range(10):
                    if s == 0:
                        if p > 1:
                            a_square(p - 2, 7)
                        a_evac(p, s)
                    a_slot_core(p - 1, s)
                    if s > 0:
                        a_evac(p, s)
                    hi_after(A_UNIT, p, s, A_HI)

            def ga_evac(s):
                b, n = ablock(PAIRS, s)
                act.wait_ge(blk_ready[b], n + 1)
                f(ga[:, s - 3, :], PB[b][:, :], ACT.Copy).then_inc(ga_ready, 1)
                act.wait_ge(ga_ready, s - 2)
                act.sem_inc(blk_free[b], 1)

            for s in range(10):
                if s == 0:
                    a_square(PAIRS - 2, 7)
                    a_evac(PAIRS, s)
                a_slot_core(PAIRS - 1, s)
                if 0 < s < 3:
                    a_evac(PAIRS, s)
                elif s >= 3:
                    ga_evac(s)
                hi_after(A_UNIT, PAIRS, s, {2: 1, 4: 2, 6: 3, 8: 4})
            a_square(PAIRS - 1, 7)
            a_outT_copy(PAIRS - 1, 6)
            ga_evac(10)
            a_outT_copy(PAIRS - 1, 7)

            def m_hi(i):
                sl, cnt, n = unit(M_UNIT, 0, i)
                if i >= 2:
                    b, c0 = mblock(2 * (i - 2) + 1)
                    act.wait_ge(blk_ready[b], c0 + 1)
                act.wait_ge(raw_ready[sl], 16 * (cnt + 1))
                f(wh[sl][:], wraw[sl][:], ACT.Copy).then_inc(hi_ready, 1)

            m_hi(1)
            act.wait_ge(ga_ready, 8)
            f(ga[:], ga[:], ACT.Sigmoid).then_inc(gasig_ready, 1)
            act.wait_ge(onA_ready, 8 * PAIRS)
            act.wait_ge(oTA_done, 8 * PAIRS)
            for k in range(KB):
                f(ysig[:, k, :], zA[:, k, :], ACT.Sigmoid).then_inc(ysig_ready, 1)
            for i, what in enumerate(M_ORDER):
                if what[:2] == "gh":
                    j = int(what[2])
                    if j >= 2:
                        act.wait_ge(m_ready, 2 * (j - 1))
                    for cb in range(2):
                        b, cnt = mblock(2 * i + cb)
                        act.wait_ge(blk_ready[b], cnt + 1)
                        f(gh[:, j % 2, cb, :], PB[b][:, :], ACT.Sigmoid).then_inc(gh_ready, 1)
                        act.wait_ge(gh_ready, 2 * j + cb + 1)
                        act.sem_inc(blk_free[b], 1)
                if i + 2 < len(M_ORDER):
                    m_hi(i + 2)
            for i in range(4):
                b, c0 = mblock(2 * (10 + i) + 1)
                act.wait_ge(blk_ready[b], c0 + 1)
                sl, cnt, n = unit(O_UNIT, 0, i)
                act.wait_ge(raw_ready[sl], 16 * (cnt + 1))
                f(wh[sl][:], wraw[sl][:], ACT.Copy).then_inc(hi_ready, 1)

        @block.vector
        def _(dve):
            link = Chain(dve, dve_chain)
            v = nc.vector

            def bc(ap, shape):
                return ap.to_broadcast(shape)

            dve.wait_ge(sig_c, 1)
            v.tensor_tensor(scT[:], scT[:], modT[:, 0:KB, :], ALU.mult).then_inc(sc_ready, 1)
            dve.wait_ge(rrx_ready, 1)
            for t in range(6):
                v.tensor_scalar(xt[:, t, :], xt[:, t, :], rrx[:, t:t + 1], None, ALU.mult).then_inc(xn_ready, 1)
            dve.wait_ge(start_in, 16 * 4)
            for g in range(2 * KB):
                k, c = divmod(g, 2)
                n = TC if c else TL
                cols = CTX if c else LAT
                if g % 4 == 0:
                    i = g // 4
                    sh, sc = slice(2 * i, 2 * i + 2), slice(KB + 2 * i, KB + 2 * i + 2)
                    dve.wait_ge(mod_used, 2 * i + 2)
                    ps = PX[:, 2 + i, 0:8].rearrange("p (j c) -> p j c", c=2)
                    v.tensor_tensor(modT[:, sh, :], ps[:, 0:2, :], bc(bmT[:, sh].unsqueeze(2), [P, 2, 2]), ALU.add)
                    link(v.tensor_tensor(modT[:, sc, :], ps[:, 2:4, :], bc(bmT[:, sc].unsqueeze(2), [P, 2, 2]),
                                         ALU.add))
                    link(v.tensor_scalar(modT[:, sc, :], modT[:, sc, :], 1.0, None, ALU.add))
                    v.tensor_tensor(modT[:, sc, :], modT[:, sc, :], bc(ngT[:, sh].unsqueeze(2), [P, 2, 2]),
                                    ALU.mult).then_inc(mod_final, 1)
                dve.wait_ge(xT_used, g + 1)
                link(v.tensor_copy(hTh[:, k, cols], htmp[:, g % 2, 0:n]))
                v.tensor_tensor(hTl[:, k, cols], htmp[:, g % 2, 0:n], hTh[:, k, cols].bitcast(F32),
                                ALU.subtract).then_inc(h_split, 1)
            dve.wait_ge(const_in, 16 * 8)
            v.tensor_tensor(om[:], lbraw[:, :, 0, :], lbraw[:, :, 1, :], ALU.subtract).then_inc(lbd_ready, 1)
            dve.wait_ge(lb_ready, 2)
            link(v.tensor_scalar(nom[:], om[:], -1.0, None, ALU.mult))

            def halves(ap, l, which):
                return ap.rearrange("p (n two b) -> p n two b", two=2, b=1 << l)[:, :, which, :]

            def h_qmul(p, i):
                b, n = hblock(p, 9 + i)
                dve.wait_ge(qsig_ready, 2 * p + i + 1)
                v.tensor_tensor(qs[:, i, :], PB[b][:, :], qs[:, i, :], ALU.mult).then_inc(q_ready, 1)
                dve.wait_ge(q_ready, 2 * p + i + 1)
                dve.sem_inc(blk_free[b], 1)


            def h_prep_gates(p, h):
                for d in range(2):
                    head = 2 * p + h
                    v.tensor_scalar(totE[:, h, d, :], sig[:, h, d, :], om[:, d, head:head + 1],
                                    lb[:, d, head:head + 1], ALU.mult, ALU.add)
                    link(v.tensor_scalar(K_[:, h, d, :], sig[:, h, d, :], nom[:, d, head:head + 1],
                                         om[:, d, head:head + 1], ALU.mult, ALU.add))

            def h_prep_queries(p):
                for h in range(2):
                    v.tensor_tensor(ksum[:, h, :], K_[:, h, 0, LAT], K_[:, h, 1, LAT],
                                    ALU.add).then_inc(diag_ready, 1)
                    v.tensor_tensor(Q_[:, h, 0, :], qs[:, h, :], totE[:, h, 0, LAT], ALU.mult)
                    link(v.tensor_tensor(Q_[:, h, 1, :], qs[:, h, :], totE[:, h, 1, LAT], ALU.mult))
                    dve.sem_inc(levels_ready, 1)
                    dve.sem_inc(sig_used, 1)

            def tot(l, h, d):
                return (totO if l % 2 else totE)[:, h, d, 0:T >> l]

            def h_join(c, l, h):
                dve.wait_ge(mix_ready, 14 * c + 2 * l + h + 1)
                B = 1 << l
                n, nq = T // (2 * B), TL // (2 * B)
                for d in range(2):
                    tt = tot(l, h, d).rearrange("p (n two) -> p n two", two=2)
                    near, far = d, 1 - d
                    kk = halves(K_[:, h, d, :], l, near)
                    v.tensor_tensor(kk, kk, bc(tt[:, :, far:far + 1], [P, n, B]), ALU.mult)
                    qq = halves(Q_[:, h, d, :], l, far)
                    v.tensor_tensor(qq, qq, bc(tt[:, TC // (2 * B):, near:near + 1], [P, nq, B]), ALU.mult)
                    last = v.tensor_tensor(tot(l + 1, h, d), tt[:, :, 0], tt[:, :, 1], ALU.mult)
                last.then_inc(levels_ready, 1)

            def h_pick(c, st, h):
                dve.wait_ge(scores_ready, 16 * c + 2 * st + h + 1)
                if st == 0 and not (isinstance(c, int) and c == 0):
                    dve.wait_ge(oT_ready, 2 * (c - 1) + h + 1)
                v.copy_predicated(AT[:, h, :].rearrange("p (n t) -> p n t", n=NCH),
                                  bc(masks[:, st:st + 1, :], [P, NCH, CH]),
                                  LV[h].rearrange("p (n t) -> p n t", n=NCH)).then_inc(scores_used, 1)

            def h_states(c, u):
                h, d = divmod(u, 2)
                dve.wait_ge(kv_ready, 4 * c + u + 1)
                order = (0, 1, 2, 3, 4) if d == 0 else (1, 0, 5, 4, 3)
                last_tot = tot(LEVELS, h, d)
                at_chunk = [0, 0, 1, 2, 3] if d == 0 else [3, 3, 2, 1, 0]
                link(v.tensor_copy(S_[:, h, d, at_chunk[0], :], X[u % 2][:, 0:P]))
                for i in range(1, 5):
                    ins = v.scalar_tensor_tensor(S_[:, h, d, at_chunk[i], :], S_[:, h, d, at_chunk[i - 1], :],
                                                 last_tot[:, order[i]:order[i] + 1],
                                                 X[u % 2][:, i * P:i * P + P], ALU.mult, ALU.add)
                    if i < 4:
                        link(ins)
                ins.then_inc(kv_used, 1)

            def h_norm(c, h):
                dve.wait_ge(rrH_ready, 2 * c + h + 1)
                dve.wait_ge(out_ready, 2 * c + h + 1)
                v.tensor_tensor(AT[:, h, :].rearrange("p (n t) -> p n t", n=NCH),
                                LV[h].rearrange("p (n t) -> p n t", n=NCH),
                                bc(rrH[:, h, :].unsqueeze(2), [P, NCH, CH]), ALU.mult).then_inc(onH_ready, 1)

            def h_slot(c, s):
                if 1 <= s < 8:
                    h_join(c, s - 1, 0)
                    h_join(c, s - 1, 1)
                    if s == 1:
                        h_pick(c, 0, 0)
                        h_pick(c, 0, 1)
                    h_pick(c, s, 0)
                    h_pick(c, s, 1)
                elif s == 9:
                    h_states(c, 0)
                    h_states(c, 1)
                elif s == 10:
                    h_states(c, 2)
                    h_states(c, 3)

            dve.wait_ge(gate_used, 4)
            v.tensor_copy(gT[:], PX[:, 5, 32:48].rearrange("p (k c) -> p k c", c=2)[:, :, 0]).then_inc(gT_ready, 1)
            h_qmul(0, 0)
            h_qmul(0, 1)
            dve.wait_ge(gate_bc, 1)
            v.tensor_tensor(gate[:], X[1], gate[:], ALU.add).then_inc(gate_ready, 1)
            h_prep_gates(0, 0)
            h_prep_gates(0, 1)
            h_prep_queries(0)
            for p in range(1, PAIRS):
                for s in range(11):
                    h_slot(p - 1, s)
                    if s >= 9:
                        h_qmul(p, s - 9)
                h_prep_gates(p, 0)
                h_norm(p - 1, 0)
                h_norm(p - 1, 1)
                h_prep_gates(p, 1)
                h_prep_queries(p)
            for s in range(11):
                h_slot(PAIRS - 1, s)
                if s >= 3:
                    b, n = hblock(PAIRS, s)
                    dve.wait_ge(zsig_ready, s - 2)
                    v.tensor_tensor(zh[:, s - 3, :], PB[b][:, :], zh[:, s - 3, :], ALU.mult).then_inc(zh_ready, 1)
                    dve.wait_ge(zh_ready, s - 2)
                    dve.sem_inc(blk_free[b], 1)
            h_norm(PAIRS - 1, 0)
            h_norm(PAIRS - 1, 1)
            for head in range(HEADS):
                dve.wait_ge(oT_done, head + 1)
                v.tensor_tensor(oTH[:, head, :], oTH[:, head, :], zh[:, head, :], ALU.mult).then_inc(oTH_final, 1)

            dve.wait_ge(const_in, 16 * 18)
            link(v.tensor_scalar(gqk[:, 0, :], gqk[:, 0, :], DH ** -0.5, None, ALU.mult))
            for i in range(2):
                g = gqk[:, i:i + 1, :]
                v.tensor_tensor(cosg[:, i, :, :], cosg[:, i, :, :], bc(g, [P, 4, DH]), ALU.mult)
                for x_ in range(2):
                    for h in range(2):
                        lo = 32 * x_ + 16 * h
                        src = 32 * x_ + 16 * (1 - h)
                        v.tensor_tensor(sing[:, i, :, lo:lo + 16], sing[:, i, :, lo:lo + 16],
                                        bc(g[:, :, src:src + 16], [P, 4, 16]), ALU.mult)
            link(v.tensor_tensor(rtmp_lam[:, 0:4:2, :], rtmp_lam[:, 0:4:2, :], rtmp_lam[:, 1:4:2, :], ALU.mult))
            v.tensor_reduce(lame[:], rtmp_lam[:, 0:4:2, :], AX.X, ALU.add).then_inc(lamd_ready, 1)
            dve.wait_ge(lame_ready, 1)
            link(v.tensor_tensor(lamv[:], lame[:, 1:2], lame[:, 0:1], ALU.subtract))
            link(v.tensor_scalar(lamv[:], lamv[:], -LAM_INIT, None, ALU.add))
            v.tensor_scalar(gA[:], gA[:], 1.0 - LAM_INIT, None, ALU.mult).then_inc(tab_ready, 1)

            def a_rope(p, s):
                i = 5 * p + s - 3
                dve.wait_ge(raw_copied, i + 1)
                link_ss = v.tensor_reduce(ssn[:], rtmp[:, 1, :].rearrange("p (g d) -> p g d", d=DH), AX.X, ALU.add)
                link_ss.then_inc(ssn_ready, 1)
                dve.wait_ge(rrn_ready, i + 1)
                g3 = lambda ap: ap.rearrange("p (g d) -> p g d", d=DH)
                which = 0 if s < 5 else 1
                first = 2 * (s - 3) if s < 5 else 4 + 2 * (s - 5)
                lat = 2 * (s - 3) if s < 5 else 2 * (s - 6)
                if s == 3 and not (isinstance(p, int) and p == 0):
                    dve.wait_ge(qkT_ready, 2 * p)
                dst = qn[:, first:first + 2, :]
                if s == 5:
                    link(v.tensor_tensor(g3(rtmp[:, 2, :]), g3(rtmp[:, 0, :]), bc(rrn[:].unsqueeze(2), [P, 8, DH]),
                                         ALU.mult))
                    dve.sem_inc(u_ready, 1)
                    v.tensor_tensor(dst.rearrange("p t (g d) -> p (t g) d", d=DH), g3(rtmp[:, 2, :]),
                                    bc(gqk[:, 1:2, :], [P, 8, DH]), ALU.mult).then_inc(qn_ready, 1)
                    return
                v.tensor_tensor(g3(rtmp[:, 2, :]), g3(rtmp[:, 0, :]), bc(rrn[:].unsqueeze(2), [P, 8, DH]),
                                ALU.mult).then_inc(u_ready, 1)
                dve.wait_ge(u_ready, i + 1)
                for t in range(2):
                    uu = rtmp[:, 2, t * UC:(t + 1) * UC].rearrange("p (g a b d) -> p g a b d", a=2, b=2, d=16)
                    rr = rtmp[:, 1, t * UC:(t + 1) * UC].rearrange("p (g a b d) -> p g a b d", a=2, b=2, d=16)
                    sn = sing[:, which, lat + t, :].rearrange("p (a b d) -> p a b d", a=2, b=2)
                    for b_ in range(2):
                        last = v.tensor_tensor(rr[:, :, :, b_, :], uu[:, :, :, 1 - b_, :],
                                               bc(sn[:, :, b_, :].unsqueeze(1), [P, 4, 2, 16]), ALU.mult)
                link(last)
                dve.wait_ge(t1_ready, i + 1)
                v.tensor_tensor(dst, rtmp[:, 3, :].rearrange("p (t c) -> p t c", t=2),
                                rtmp[:, 1, :].rearrange("p (t c) -> p t c", t=2), ALU.add).then_inc(qn_ready, 1)

            def a_max(c, j):
                dve.wait_ge(s_ready, 8 * c + j + 1)
                v.tensor_reduce(nmax[:, j, :], SB.rearrange("p (m k) -> p m k", m=2), AX.X, ALU.max,
                                negate=True).then_inc(max_ready, 1)

            def a_weights(c, j):
                dve.wait_ge(exp_ready, 16 * c + 2 * j + 2)
                link(v.reciprocal(coef[:, j, 0:1], esum[:, j, 1:2]))
                link(v.tensor_tensor(coef[:, j, 1:2], coef[:, j, 0:1], esum[:, j, 0:1], ALU.mult))
                link(v.tensor_scalar(coef[:, j, 0:1], coef[:, j, 1:2], lamv[:, 0:1], None, ALU.mult))
                v.scalar_tensor_tensor(eA[:, j:j + 1], esum[:, j, 0:1], EPS, esum[:, j, 0:1], ALU.mult, ALU.mult)
                if not (isinstance(c, int) and c == 0 and j == 0):
                    dve.wait_ge(wT_ready, 8 * c + j)
                v.scalar_tensor_tensor(W_[:], E_[:, 1, :], coef[:, j, 0:1], E_[:, 0, :],
                                       ALU.mult, ALU.add).then_inc(w_ready, 1)

            def a_norm(c, j):
                dve.wait_ge(rrA_ready, 8 * c + j + 1)
                if not (isinstance(c, int) and c == 0 and j == 0):
                    dve.wait_ge(oTA_ready, 8 * c + j)
                v.tensor_scalar(on[:], osb[:, j % 2, :], rrA[:, j:j + 1], None, ALU.mult).then_inc(onA_ready, 1)

            def a_slot(c, s):
                if s <= 1 and c > 0:
                    a_norm(c - 1, 6 + s)
                if s >= 4:
                    a_norm(c, s - 4)
                if 1 <= s <= 8:
                    a_max(c, s - 1)
                    a_weights(c, s - 1)

            for s in range(3, 8):
                a_rope(0, s)
            for p in range(1, PAIRS):
                for s in range(10):
                    a_slot(p - 1, s)
                    if 3 <= s < 8:
                        a_rope(p, s)
            for s in range(10):
                a_slot(PAIRS - 1, s)
            a_norm(PAIRS - 1, 6)
            a_norm(PAIRS - 1, 7)

            dve.wait_ge(oTA_ready, 8 * PAIRS)
            dve.wait_ge(oTA_done, 8 * PAIRS)
            for k in range(KB):
                dve.wait_ge(ysig_ready, k + 1)
                link(v.tensor_tensor(zA[:, k, :], zA[:, k, :], ysig[:, k, :], ALU.mult))
                link(v.tensor_tensor(oTA[:, k, :], oTA[:, k, :], zA[:, k, :], ALU.mult))
                link(v.tensor_copy(yAh[:, k, :], oTA[:, k, :]))
                v.tensor_tensor(yAl[:, k, :], oTA[:, k, :], yAh[:, k, :].bitcast(F32),
                                ALU.subtract).then_inc(yA_ready, 1)
            for k in range(KB):
                link(v.tensor_copy(yHh[:, k, :], oTH[:, k, :]))
                v.tensor_tensor(yHl[:, k, :], oTH[:, k, :], yHh[:, k, :].bitcast(F32),
                                ALU.subtract).then_inc(yH_ready, 1)
            dve.wait_ge(gasig_ready, 1)
            for i, what in enumerate(M_ORDER):
                j = int(what[2])
                for cb in range(2):
                    k = 2 * j + cb
                    b, cnt = mblock(2 * i + cb)
                    if what[:2] == "ba":
                        dve.wait_ge(blk_ready[b], cnt + 1)
                        link(v.tensor_tensor(ga[:, k, :], PB[b][:, :], ga[:, k, :], ALU.mult))
                        dve.sem_inc(blk_free[b], 1)
                    elif what[:2] == "bh":
                        dve.wait_ge(blk_ready[b], cnt + 1)
                        dve.wait_ge(gh_ready, k + 1)
                        link(v.tensor_tensor(gh[:, j % 2, cb, :], PB[b][:, :], gh[:, j % 2, cb, :], ALU.mult))
                        dve.sem_inc(blk_free[b], 1)
                        link(v.tensor_tensor(ga[:, k, :], ga[:, k, :], gh[:, j % 2, cb, :], ALU.add))
                        link(v.tensor_copy(mTh[:, k, :], ga[:, k, :]))
                        v.tensor_tensor(mTl[:, k, :], ga[:, k, :], mTh[:, k, :].bitcast(F32),
                                        ALU.subtract).then_inc(m_ready, 1)
            dve.wait_ge(xb_in, 16)
            for n in range(8):
                u, half = divmod(n, 2)
                b, cnt = mblock(OUT_BLOCK + n)
                dve.wait_ge(blk_ready[b], cnt + 1)
                c = slice(u * UC, (u + 1) * UC)
                if n >= 2:
                    dve.wait_ge(o_ready, n - 1)
                link(v.tensor_tensor(ytmp[:, n % 2, :, :], PB[b][:, :].rearrange("p (t c) -> p t c", t=2),
                                     bc(gate[:, c].unsqueeze(1), [P, 2, UC]), ALU.mult))
                dve.sem_inc(blk_free[b], 1)
                xx = xb[:, 2 * half:2 * half + 2, c]
                v.tensor_tensor(xx, xx, ytmp[:, n % 2, :, :], ALU.add).then_inc(o_ready, 1)

        @block.gpsimd
        def _(pool):
            link = Chain(pool, pool_chain)
            g = nc.gpsimd

            def split_lo(sl, n):
                pool.wait_ge(hi_ready, n + 1)
                g.tensor_tensor(wl[sl][:], wraw[sl][:], wh[sl][:].bitcast(F32), ALU.subtract).then_inc(lo_ready, 1)

            def rsqrt(dst, src, scale, eps, done):
                link(g.tensor_scalar(dst, src, scale, eps, ALU.mult, ALU.add))
                n = dst.shape[-1]
                return g.tensor_tensor(dst, dst, mhalf[:, 0:n], ALU.pow).then_inc(done, 1)

            link(g.memset(mhalf[:], -0.5))
            pool.wait_ge(ssx_ready, 1)
            rsqrt(rrx[:], ssx[:], 1.0 / D, EPS, rrx_ready)
            split_lo(0, 0)
            split_lo(1, 1)

            def h_rsqrt(c):
                for h in range(2):
                    pool.wait_ge(sqH_ready, 2 * c + h + 1)
                    rsqrt(rrH[:, h, :], ssH[:, h, :], 1.0 / P, EPS, rrH_ready)

            for p in range(PAIRS):
                for j in (2, 3, 4, 5):
                    if not (p == PAIRS - 1 and j >= 4):
                        pass
                    n = 4 * p + j
                    split_lo(n % 2, n)
                    if j == 4 and p > 0:
                        h_rsqrt(p - 1)
            for n in range(4 * PAIRS + 2, A_UNIT + 2):
                split_lo(n % 2, n)
            h_rsqrt(PAIRS - 1)

            def a_rsqrt(c, j):
                pool.wait_ge(sqA_ready, 8 * c + j + 1)
                link(g.tensor_scalar(rrA[:, j:j + 1], ssA[:, j:j + 1], 1.0 / P, None, ALU.mult))
                link(g.tensor_tensor(rrA[:, j:j + 1], rrA[:, j:j + 1], eA[:, j:j + 1], ALU.add))
                g.tensor_tensor(rrA[:, j:j + 1], rrA[:, j:j + 1], mhalf[:, 0:1], ALU.pow).then_inc(rrA_ready, 1)

            def a_rope(p, s):
                i = 5 * p + s - 3
                pool.wait_ge(ssn_ready, i + 1)
                rsqrt(rrn[:], ssn[:], 1.0 / DH, EPS, rrn_ready)
                pool.wait_ge(u_ready, i + 1)
                which = 0 if s < 5 else 1
                lat = 2 * (s - 3) if s < 5 else 2 * (s - 6)
                if s == 5:
                    return pool.sem_inc(t1_ready, 1)
                for t in range(2):
                    last = g.tensor_tensor(rtmp[:, 3, t * UC:(t + 1) * UC].rearrange("p (g d) -> p g d", d=DH),
                                           rtmp[:, 2, t * UC:(t + 1) * UC].rearrange("p (g d) -> p g d", d=DH),
                                           cosg[:, which, lat + t:lat + t + 1, :].to_broadcast([P, 4, DH]), ALU.mult)
                last.then_inc(t1_ready, 1)

            A_LO = {2: 1, 4: 2, 7: 3, 9: 4}

            def lo_after(p, s, table):
                if s in table:
                    sl, _, n = unit(A_UNIT, p, table[s])
                    split_lo(sl, n)

            for s in range(3, 10):
                if s < 8:
                    a_rope(0, s)
                lo_after(0, s, {4: 2, 7: 3, 9: 4})
            for p in range(1, PAIRS):
                for s in range(10):
                    if s == 0 and p > 1:
                        a_rsqrt(p - 2, 7)
                    if s >= 3:
                        a_rsqrt(p - 1, s - 3)
                    if 3 <= s < 8:
                        a_rope(p, s)
                    lo_after(p, s, A_LO)
            for s in range(10):
                if s == 0:
                    a_rsqrt(PAIRS - 2, 7)
                if s >= 3:
                    a_rsqrt(PAIRS - 1, s - 3)
                lo_after(PAIRS, s, {2: 1, 4: 2, 6: 3, 8: 4})
            a_rsqrt(PAIRS - 1, 7)
            for n in range(M_UNIT + 1, N_UNIT):
                split_lo(n % 2, n)


_INS = ["x", "c", "ctx", "c_ctx", "w_mod", "b_mod", "norm_gain", "w_in", "q_norm_gain", "k_norm_gain",
        "lambda_q1", "lambda_k1", "lambda_q2", "lambda_k2", "subln_gain", "hgrn_lb_fwd", "hgrn_lb_bwd",
        "hgrn_norm_gain", "w_br_attn", "w_br_hgrn", "w_out"]


def shape_constants():
    import numpy as np
    i = np.arange(CH)
    masks = np.zeros((CH, LEVELS + 1, CH), np.int32)
    masks[:, 0, :] = i[:, None] == i[None, :]
    for l in range(LEVELS):
        masks[:, l + 1, :] = ((i[:, None] >> (l + 1)) == (i[None, :] >> (l + 1))) & \
            ((i[:, None] >> l) != (i[None, :] >> l))
    row = np.repeat(np.arange(TL // GRID_W, dtype=np.float32), GRID_W)
    col = np.tile(np.arange(GRID_W, dtype=np.float32), TL // GRID_W)
    half = DH // 2
    inv = (10000.0 ** (-np.arange(0, half, 2, dtype=np.float32) / half)).astype(np.float32)
    ar, ac = row[:, None] * inv[None, :], col[:, None] * inv[None, :]
    ang = np.concatenate([ar, ar, ac, ac], axis=-1).astype(np.float32)
    sign = np.repeat(np.array([-1, 1, -1, 1], np.float32), DH // 4)
    return {"ident": np.eye(P, dtype=np.float32), "masks": masks,
            "cos": np.cos(ang).astype(np.float32), "sin": (np.sin(ang) * sign).astype(np.float32)}


def kernel(**inputs):
    import numpy as _np
    import concourse.bacc as _bacc
    from concourse import mybir as _mybir
    from concourse.bass_utils import run_bass_kernel_spmd as _run

    nc = _bacc.Bacc("TRN2", target_bir_lowering=False, num_devices=1)
    arrays, args = {}, {}
    for name, value in [(n, inputs[n]) for n in _INS] + list(shape_constants().items()):
        v = _np.ascontiguousarray(value)
        arrays[f"in_{name}_dram"] = v
        args[name] = nc.dram_tensor(f"in_{name}_dram", v.shape, _mybir.dt.from_np(v.dtype), kind="ExternalInput").ap()
    out = nc.dram_tensor("out_0_dram", (1, TL, D), _mybir.dt.float32, kind="ExternalOutput").ap()
    hybrid_layer(nc, args, out)
    r = _run(nc, [arrays], core_ids=[0])
    return r.results[0]["out_0_dram"]
```

```python
from contextlib import ExitStack

import concourse.bass as bass
from concourse import mybir

F32 = mybir.dt.float32
F32R = mybir.dt.float32r
I32 = mybir.dt.int32
ALU = mybir.AluOpType
ACT = mybir.ActivationFunctionType
AX = mybir.AxisListType

P = 128
D = 1024
KB = D // P
TC = 256
TL = 512
T = TC + TL
HEADS = 8
PAIRS = HEADS // 2
DH = 64
CH = 128
LEVELS = 7
NCH = TL // CH
UC = 256
EPS = 1e-6
GRID_W = 64
LAM_INIT = 0.8 - 0.6

COL = {"attn_k": 0, "attn_v": 1024, "hgrn_i": 2048, "hgrn_f": 3072, "hgrn_b": 4096, "attn_q": 5120,
       "hgrn_q": 6144, "attn_z": 7168, "hgrn_z": 8192, "gate_a": 9216, "gate_h": 10240}
LAT = slice(TC, T)
CTX = slice(0, TC)

A_UNIT = 4 * PAIRS + 4
M_UNIT = A_UNIT + 4 * PAIRS + 4
O_UNIT = M_UNIT + 12
N_UNIT = O_UNIT + 4
MOD_ORDER = (0, 4, 1, 5, 2, 6, 3, 7)


def unit(base, p, j):
    return (base + j) % 2, 2 * p + (base + j) // 2, 4 * p + (base + j)


def hblock(p, s):
    if isinstance(p, int) and p == 0:
        return s % 2, (s - 3) // 2 if s % 2 else (s - 4) // 2
    return s % 2, (5 * p - 1 + (s - 1) // 2 if s % 2 else 6 * p - 2 + s // 2)


A_BANK0 = 6 * PAIRS + 4
A_BANK1 = 5 * PAIRS + 4


def ablock(p, s):
    if isinstance(p, int) and p == 0:
        return s % 2, (A_BANK1 + (s - 3) // 2 if s % 2 else A_BANK0 + (s - 4) // 2)
    return s % 2, (A_BANK1 + 4 + 5 * (p - 1) + s // 2 if s % 2 else A_BANK0 + 3 + 5 * (p - 1) + s // 2)


M_BANK0 = A_BANK0 + 3 + 5 * PAIRS + 1
M_BANK1 = A_BANK1 + 4 + 5 * PAIRS


def mblock(n):
    return 1 - n % 2, (M_BANK0 if n % 2 else M_BANK1) + n // 2


M_ORDER = ["gh0", "gh1", "ba0", "bh0", "gh2", "ba1", "bh1", "gh3", "ba2", "ba3", "bh2", "bh3"]
OUT_BLOCK = 2 * len(M_ORDER)


class Chain:

    def __init__(self, eng, sem):
        self.eng, self.sem, self.n = eng, sem, 0

    def __call__(self, ins):
        self.n += 1
        ins.then_inc(self.sem, 1)
        self.eng.wait_ge(self.sem, self.n)


def hybrid_layer(nc, a, out):
    with ExitStack() as ctx:
        def sem(name):
            return ctx.enter_context(nc.semaphore(name))

        base = (nc.sbuf_base + 63) // 64 * 64
        at = [base]

        def place(name, shape, dt=F32, offset=None):
            size = 1
            for d in shape[1:]:
                size *= d
            size *= 4
            if offset is None:
                offset = at[0]
                at[0] += (size + 31) // 32 * 32
            return nc.alloc_sbuf_tensor_at(name, shape, dt, offset=offset)

        hTh = place("hTh", [P, KB, T], F32R)
        hTl = place("hTl", [P, KB, T], F32R)
        wraw = [place(f"wraw{i}", [P, KB, UC]) for i in range(2)]
        wh = [place(f"wh{i}", [P, KB, UC], F32R) for i in range(2)]
        wl = [place(f"wl{i}", [P, KB, UC], F32R) for i in range(2)]
        ident = place("ident", [P, P])
        gate = place("gate", [P, D])
        mhalf = place("mhalf", [P, 16])
        scT = place("scT", [P, KB, 2])
        bmT = place("bmT", [P, 16])
        modT = place("modT", [P, 16, 2])
        ones = place("ones", [P, P])
        ngT = place("ngT", [P, KB])
        lbraw = place("lbraw", [P, 2, 2, HEADS])
        lb = place("lb", [P, 2, HEADS])
        om = place("om", [P, 2, HEADS])
        nom = place("nom", [P, 2, HEADS])
        gH = place("gH", [P, 1])
        gA = place("gA", [P, 1])
        ssx = place("ssx", [P, 6])
        rrx = place("rrx", [P, 6])
        ssH = place("ssH", [P, 2, NCH])
        rrH = place("rrH", [P, 2, NCH])
        lamv = place("lamv", [P, 1])
        lame = place("lame", [P, 2])
        nmax = place("nmax", [P, 8, 2])
        esum = place("esum", [P, 8, 2])
        coef = place("coef", [P, 8, 2])
        ssA = place("ssA", [P, 8])
        eA = place("eA", [P, 8])
        rrA = place("rrA", [P, 8])
        ssn = place("ssn", [P, 8])
        rrn = place("rrn", [P, 8])
        gqk = place("gqk", [P, 2, DH])
        lamq = place("lamq", [P, 4, DH])
        R = (at[0] + 63) // 64 * 64
        K16 = 16384
        oTH = place("oTH", [P, HEADS, TL], offset=R)
        wmod = [place(f"wmod{u}", [P, KB, UC], offset=R + k * 8192) for u, k in
                enumerate((0, 1, 5, 7, 8, 9, 10, 11))]
        xt = place("xt", [P, 6, D], offset=R + K16)
        htmp = place("htmp", [P, 2, TL], offset=R + 3 * K16)
        sqx = place("sqx", [P, D], offset=R + 3 * K16 + 4096)
        macc = {1: place("macc", [P, 2, 2, UC], offset=R + 3 * K16 + 4096)[:],
                3: gate[:].rearrange("p (u c n) -> p u c n", u=2, c=2)}
        o = R + K16
        qs = place("qs", [P, 2, TL], offset=o)
        sig = place("sig", [P, 2, 2, T], offset=o + 4096)
        zh = place("zh", [P, HEADS, TL], offset=o)
        o += K16
        K_ = place("K_", [P, 2, 2, T], offset=o); o += 12288
        Q_ = place("Q_", [P, 2, 2, TL], offset=o); o += 8192
        totE = place("totE", [P, 2, 2, T], offset=o); o += 12288
        totO = place("totO", [P, 2, 2, T // 2], offset=o); o += 6144
        mixQ = place("mixQ", [P, 2, TL], offset=o); o += 4096
        mixK = place("mixK", [P, 2, TL], offset=o); o += 4096
        V = place("V", [P, 6, UC], offset=o); o += 6144
        AT = place("AT", [P, 2, TL], offset=o); o += 4096
        gacc = place("gacc", [P, 4, UC], offset=o - 4096)
        S_ = place("S_", [P, 2, 2, NCH, P], offset=o); o += 8192
        masks = place("masks", [P, LEVELS + 1, CH], I32, offset=R + 6 * K16)
        cosg = place("cosg", [P, 2, 4, DH], offset=R + 6 * K16 + 4096)
        sing = place("sing", [P, 2, 4, DH], offset=R + 6 * K16 + 6144)
        ksum = place("ksum", [P, 2, TL], offset=o - 8192)
        oTA = place("oTA", [P, HEADS, TL], offset=R + K16)
        zA = place("zA", [P, HEADS, TL], offset=R + 2 * K16)
        ga = place("ga", [P, KB, TL], offset=R + 3 * K16)
        o2 = R + 3 * K16
        qn = place("qn", [P, 10, UC], offset=o2); o2 += 10240
        rtmp = place("rtmp", [P, 4, 2 * UC], offset=o2); o2 += 8192
        o2 = (o2 + 63) // 64 * 64
        VA = place("VA", [P, 6, UC], offset=o2); o2 += 6144
        qT = place("qT", [P, 2, TL], offset=o2); o2 += 4096
        kT = place("kT", [P, 2, T], offset=o2); o2 += 6144
        E_ = place("E_", [P, 2, T], offset=o2); o2 += 6144
        W_ = place("W_", [P, T], offset=o2); o2 += 3072
        WT = place("WT", [P, T], offset=o2); o2 += 3072
        on = place("on", [P, P], offset=o2); o2 += 512
        osb = place("osb", [P, 2, P], offset=o2); o2 += 1024
        junk = place("junk", [P, P], offset=o2); o2 += 512
        yHh = place("yHh", [P, KB, TL], F32R, offset=R + 4 * K16)
        yHl = place("yHl", [P, KB, TL], F32R, offset=R)
        yAh = place("yAh", [P, KB, TL], F32R, offset=R + 5 * K16)
        ysig = place("ysig", [P, KB, TL], offset=R + 5 * K16)
        yAl = place("yAl", [P, KB, TL], F32R, offset=R + K16)
        mTh = place("mTh", [P, KB, TL], F32R, offset=R + 2 * K16)
        mTl = place("mTl", [P, KB, TL], F32R, offset=R + 3 * K16)
        gh = place("gh", [P, 2, 2, TL], offset=R + 6 * K16)
        xb = place("xb", [P, 4, D], offset=R + 5 * K16)
        ytmp = place("ytmp", [P, 2, 2, UC], offset=R + 6 * K16)

        PB = [ctx.enter_context(nc.psum_tensor(f"PB{i}", [P, 512], F32)) for i in range(2)]
        PX = ctx.enter_context(nc.psum_tensor("PX", [P, 6, 512], F32))
        LV = [PX[:, i, :] for i in range(2)]
        X = [PX[:, 2:4, :].rearrange("p a b -> p (a b)"),
             PX[:, 4:6, :].rearrange("p a b -> p (a b)")]
        SB = PX[:, 0:3, :].rearrange("p a b -> p (a b)")
        WB = PX[:, 3:5, :].rearrange("p a b -> p (a b)")
        OB = PX[:, 5, :]

        tab_in = sem("tab_in")
        bias_in = sem("bias_in")
        start_in = sem("start_in")
        const_in = sem("const_in")
        c_in = sem("c_in")
        mod_in = [sem(f"mod_in{u}") for u in range(len(MOD_ORDER))]
        x_in = sem("x_in")
        xb_in = sem("xb_in")
        raw_ready = [sem(f"raw_ready{i}") for i in range(2)]
        hi_ready = sem("hi_ready")
        lo_ready = sem("lo_ready")
        mod_used = sem("mod_used")
        blk_ready = [sem(f"blk_ready{i}") for i in range(2)]
        blk_free = [sem(f"blk_free{i}") for i in range(2)]
        dve_chain = sem("dve_chain")
        act_chain = sem("act_chain")
        pool_chain = sem("pool_chain")
        sig_c = sem("sig_c")
        sc_ready = sem("sc_ready")
        mod_final = sem("mod_final")
        ssx_ready = sem("ssx_ready")
        rrx_ready = sem("rrx_ready")
        xn_ready = sem("xn_ready")
        xT_ready = sem("xT_ready")
        xT_used = sem("xT_used")
        h_split = sem("h_split")
        lbd_ready = sem("lbd_ready")
        lb_ready = sem("lb_ready")
        qsig_ready = sem("qsig_ready")
        q_ready = sem("q_ready")
        sig_used = sem("sig_used")
        v_ready = sem("v_ready")
        diag_ready = sem("diag_ready")
        levels_ready = sem("levels_ready")
        mix_ready = sem("mix_ready")
        scores_ready = sem("scores_ready")
        scores_used = sem("scores_used")
        kT_ready = sem("kT_ready")
        kT_copied = sem("kT_copied")
        kv_ready = sem("kv_ready")
        kv_used = sem("kv_used")
        out_ready = sem("out_ready")
        sqH_ready = sem("sqH_ready")
        rrH_ready = sem("rrH_ready")
        onH_ready = sem("onH_ready")
        oT_ready = sem("oT_ready")
        oT_done = sem("oT_done")
        zsig_ready = sem("zsig_ready")
        zh_ready = sem("zh_ready")
        oTH_final = sem("oTH_final")
        lamd_ready = sem("lamd_ready")
        lame_ready = sem("lame_ready")
        tab_ready = sem("tab_ready")
        va_ready = sem("va_ready")
        raw_copied = sem("raw_copied")
        ssn_ready = sem("ssn_ready")
        rrn_ready = sem("rrn_ready")
        u_ready = sem("u_ready")
        t1_ready = sem("t1_ready")
        qn_ready = sem("qn_ready")
        qkT_ready = sem("qkT_ready")
        qkT_copied = sem("qkT_copied")
        s_ready = sem("s_ready")
        s_shared = sem("s_shared")
        max_ready = sem("max_ready")
        exp_ready = sem("exp_ready")
        w_ready = sem("w_ready")
        wT_ready = sem("wT_ready")
        wT_copied = sem("wT_copied")
        pv_ready = sem("pv_ready")
        sqA_ready = sem("sqA_ready")
        rrA_ready = sem("rrA_ready")
        onA_ready = sem("onA_ready")
        oTA_ready = sem("oTA_ready")
        oTA_done = sem("oTA_done")
        ga_ready = sem("ga_ready")
        gasig_ready = sem("gasig_ready")
        ysig_ready = sem("ysig_ready")
        yHh_ready = sem("yHh_ready")
        yH_ready = sem("yH_ready")
        yA_ready = sem("yA_ready")
        gh_ready = sem("gh_ready")
        m_ready = sem("m_ready")
        gate_in = [sem(f"gate_in{u}") for u in range(4)]
        ones_ready = sem("ones_ready")
        macc_ready = sem("macc_ready")
        gacc_ready = sem("gacc_ready")
        gate_bc = sem("gate_bc")
        gate_ready = sem("gate_ready")
        o_ready = sem("o_ready")
        out_done = sem("out_done")

        w_in = a["w_in"][0]
        w_mod = a["w_mod"][0]

        def unit_source(n):
            def cols(m, c0):
                return m[:, c0:c0 + UC].rearrange("(k p) c -> p k c", p=P)
            if n < A_UNIT:
                p, j = divmod(n, 4)
                if n >= 4 * PAIRS:
                    return cols(w_in, COL["hgrn_z"] + UC * (n - 4 * PAIRS))
                return cols(w_in, COL[("hgrn_f", "hgrn_b", "hgrn_q", "hgrn_i")[j]] + UC * p)
            if n < M_UNIT:
                n -= A_UNIT
                p, j = divmod(n, 4)
                if n >= 4 * PAIRS:
                    return cols(w_in, COL["gate_a"] + UC * (n - 4 * PAIRS))
                return cols(w_in, COL[("attn_q", "attn_k", "attn_z", "attn_v")[j]] + UC * p)
            if n < O_UNIT:
                kind, j = M_ORDER[n - M_UNIT][:2], int(M_ORDER[n - M_UNIT][2])
                if kind == "gh":
                    return cols(w_in, COL["gate_h"] + UC * j)
                return cols(a["w_br_attn"][0] if kind == "ba" else a["w_br_hgrn"][0], UC * j)
            return cols(a["w_out"][0], UC * (n - O_UNIT))

        block = ctx.enter_context(nc.Block())

        @block.sync
        def _(sp):
            sp.dma_start(xt[:, 0:2, :], a["ctx"][0].rearrange("(t p) d -> p t d", p=P)).then_inc(x_in, 16)
            sp.dma_start(xt[:, 2:6, :], a["x"][0].rearrange("(t p) d -> p t d", p=P)).then_inc(x_in, 16)

            def mod_load(u, dst, signal):
                sp.dma_start(dst[:], w_mod[:, u * UC:(u + 1) * UC].rearrange("(k p) c -> p k c", p=P)
                             ).then_inc(signal, 16)

            def unit_load(n):
                if n >= 2:
                    sp.wait_ge(lo_ready, n - 1)
                sp.dma_start(wraw[n % 2][:], unit_source(n)).then_inc(raw_ready[n % 2], 16)

            for i, u in enumerate(MOD_ORDER):
                mod_load(u, wmod[u], mod_in[u])
                if i in (3, 7):
                    unit_load(i // 4)
            for n in range(2, N_UNIT):
                unit_load(n)
                if n == 2:
                    sp.wait_ge(mod_used, 8)
                    for u in range(4):
                        mod_load(8 + u, wmod[u], gate_in[u])
                if n == O_UNIT:
                    b, cnt = mblock(2 * M_ORDER.index("ba3") + 1)
                    sp.wait_ge(blk_ready[b], cnt + 1)
                    sp.dma_start(xb[:], a["x"][0].rearrange("(t p) d -> p t d", p=P)).then_inc(xb_in, 16)
            ov = out[0].rearrange("(t p) d -> p t d", p=P)
            for n in range(8):
                sp.wait_ge(o_ready, n + 1)
                u, h = divmod(n, 2)
                sp.dma_start(ov[:, 2 * h:2 * h + 2, u * UC:(u + 1) * UC],
                             xb[:, 2 * h:2 * h + 2, u * UC:(u + 1) * UC]).then_inc(out_done, 16)
            sp.wait_ge(out_done, 16 * 8)

        @block.tensor
        def _(pe):
            def mm3(dst, xh, xl, yh, yl, first, last):
                nc.tensor.matmul(dst, xh, yh, start=first, stop=False)
                nc.tensor.matmul(dst, xh, yl, start=False, stop=False)
                return nc.tensor.matmul(dst, xl, yh, start=False, stop=last)

            def feature_block(dst, s, cb, cols, ks=range(KB), yh=hTh, yl=hTl):
                c = slice(cb * P, cb * P + P)
                for k in ks:
                    last = mm3(dst, wh[s][:, k, c], wl[s][:, k, c], yh[:, k, cols], yl[:, k, cols],
                               k == 0, k == KB - 1)
                return last

            def token_tile(dst, s, t, ks=range(KB), yh=hTh, yl=hTl):
                c = slice(t * P, t * P + P)
                for k in ks:
                    last = mm3(dst, yh[:, k, c], yl[:, k, c], wh[s][:, k, :], wl[s][:, k, :],
                               k == 0, k == KB - 1)
                return last

            def open_block(b, n):
                if not (isinstance(n, int) and n == 0):
                    pe.wait_ge(blk_free[b], n)

            def h_proj(p, s, half=None):
                b, n = hblock(p, s)
                j = -1 if s < 3 else (s - 3) // 3
                ws, _, wn = unit(0, p, j)
                halves = (0, 1) if half is None else (half,)
                if half != 1:
                    if s in (0, 3, 6, 9):
                        pe.wait_ge(lo_ready, wn + 1)
                    open_block(b, n)
                for i in halves:
                    if s < 3:
                        last = token_tile(PB[b][:, i * UC:(i + 1) * UC], ws, 2 * s + i)
                    elif s in (5, 8):
                        last = feature_block(PB[b][:, i * UC:(i + 1) * UC], ws, i, CTX)
                    else:
                        cb = (s - 3) % 3 if s < 9 else s - 9
                        last = feature_block(PB[b][:, :], ws, cb, LAT, range(4 * i, 4 * i + 4))
                if half != 0:
                    last.then_inc(blk_ready[b], 1)

            def h_scores(c, st):
                for h in range(2):
                    if st == 0:
                        pe.wait_ge(diag_ready, 2 * c + h + 1)
                        if not (isinstance(c, int) and c == 0):
                            pe.wait_ge(onH_ready, 2 * c + h - 1)
                    else:
                        pe.wait_ge(mix_ready, 14 * c + 2 * (st - 1) + h + 1)
                        pe.wait_ge(scores_used, 16 * c + 2 * (st - 1) + h + 1)
                    for ch in range(NCH):
                        t = slice(ch * CH, ch * CH + CH)
                        kk, qq = (ksum, qs) if st == 0 else (mixK, mixQ)
                        last = nc.tensor.matmul(LV[h][:, t], kk[:, h, t], qq[:, h, t], start=True, stop=True)
                    last.then_inc(scores_ready, 1)

            ORDER = [(0, 1, 2, 3, 4), (1, 0, 5, 4, 3)]

            def h_keysT(c, u):
                h, d = divmod(u, 2)
                pe.wait_ge(levels_ready, 16 * c + 14 + h + 1)
                if u >= 2:
                    pe.wait_ge(kv_used, 4 * c + u - 1)
                elif not (isinstance(c, int) and c == 0):
                    pe.wait_ge(oT_done, 2 * c)
                else:
                    pe.wait_ge(gate_ready, 1)
                for i, ch in enumerate(ORDER[d]):
                    last = nc.tensor.transpose(X[u % 2][:, i * P:i * P + P], K_[:, h, d, ch * CH:ch * CH + CH],
                                               ident[:])
                last.then_inc(kT_ready, 1)

            def h_kv(c, u):
                h, d = divmod(u, 2)
                pe.wait_ge(kT_copied, 4 * c + u + 1)
                pe.wait_ge(v_ready, 3 * c + 3)
                for i, ch in enumerate(ORDER[d]):
                    last = nc.tensor.matmul(X[u % 2][:, i * P:i * P + P], totE[:, h, d, i * CH:i * CH + CH],
                                            V[:, ch, h * P:h * P + P], start=True, stop=True)
                last.then_inc(kv_ready, 1)

            def h_out(c, h):
                pe.wait_ge(kv_used, 4 * c + 2 * h + 2)
                pe.wait_ge(scores_used, 16 * c + 14 + h + 1)
                for ch in range(NCH):
                    t = slice(ch * CH, ch * CH + CH)
                    dst = LV[h][:, t]
                    nc.tensor.matmul(dst, AT[:, h, t], V[:, 2 + ch, h * P:h * P + P], start=True, stop=False)
                    nc.tensor.matmul(dst, Q_[:, h, 0, t], S_[:, h, 0, ch, :], start=False, stop=False)
                    last = nc.tensor.matmul(dst, Q_[:, h, 1, t], S_[:, h, 1, ch, :], start=False, stop=True)
                last.then_inc(out_ready, 1)

            def h_outT(c, h):
                pe.wait_ge(onH_ready, 2 * c + h + 1)
                pe.wait_ge(kv_used, 4 * c + 4)
                for ch in range(NCH):
                    t = slice(ch * CH, ch * CH + CH)
                    last = nc.tensor.transpose(X[h][:, t], AT[:, h, t], ident[:])
                last.then_inc(oT_ready, 1)

            def h_core(c, s):
                if s < 8:
                    h_scores(c, s)
                elif s < 10:
                    h_kv(c, 2 * (s - 8))
                    h_kv(c, 2 * (s - 8) + 1)
                else:
                    h_out(c, 1)

            def h_inner(c, s):
                if s < 10:
                    h_keysT(c, 2 * (s - 8))
                    h_keysT(c, 2 * (s - 8) + 1)
                else:
                    h_out(c, 0)

            def mod_pair(i):
                if i % 2:
                    pe.wait_ge(ones_ready, 1)
                    pe.wait_ge(macc_ready, i)
                    for u in range(2):
                        for cb in range(2):
                            for c in range(2):
                                q = 4 * u + 2 * cb + c
                                last = nc.tensor.matmul(PX[:, 2 + i, q:q + 1], macc[i][:, u, c, cb * P:cb * P + P],
                                                        ones[:, 0:1], start=True, stop=True)
                        last.then_inc(mod_used, 1)
                    return
                for u in (i, i + 4):
                    pe.wait_ge(mod_in[u], 16)
                    for cb in range(2):
                        q = 4 * (u // 4) + 2 * cb
                        for k in range(KB):
                            last = nc.tensor.matmul(PX[:, 2 + i, q:q + 2], wmod[u][:, k, cb * P:cb * P + P],
                                                    scT[:, k, :], start=(k == 0), stop=(k == KB - 1))
                    last.then_inc(mod_used, 1)

            def x_transposes(i):
                for g in range(4 * i, 4 * i + 4):
                    k, c = divmod(g, 2)
                    if g >= 2:
                        pe.wait_ge(xT_used, g - 1)
                    for t0, t in enumerate(range(2) if c else range(2, 6)):
                        last = nc.tensor.transpose(LV[g % 2][:, t0 * P:t0 * P + P], xt[:, t, k * P:k * P + P],
                                                   ident[:])
                    last.then_inc(xT_ready, 1)

            def first_blocks(i):
                if i == 0:
                    pe.wait_ge(lo_ready, 1)
                for k in (2 * i, 2 * i + 1):
                    pe.wait_ge(h_split, 2 * k + 1)
                    for cb in range(2):
                        last = feature_block(PB[1 - cb][:, :], 0, cb, LAT, [k])
                        if k == KB - 1:
                            last.then_inc(blk_ready[1 - cb], 1)

            pe.wait_ge(sc_ready, 1)
            mod_pair(0)
            mod_pair(2)
            pe.wait_ge(start_in, 16 * 4)
            pe.wait_ge(xn_ready, 6)
            x_transposes(0)
            mod_pair(1)
            x_transposes(1)
            first_blocks(0)
            x_transposes(2)
            first_blocks(1)
            mod_pair(3)
            x_transposes(3)
            first_blocks(2)
            first_blocks(3)
            pe.wait_ge(h_split, 2 * KB)
            pe.wait_ge(mod_final, 4)
            for s in range(5, 11):
                h_proj(0, s)
                if s == 9:
                    for half in range(2):
                        pe.wait_ge(gacc_ready, half + 1)
                        last = nc.tensor.matmul(X[1][:, half * 512:half * 512 + 512], ones[:],
                                                gacc[:, 2 * half:2 * half + 2, :].rearrange("p u c -> p (u c)"),
                                                start=True, stop=True)
                    last.then_inc(gate_bc, 1)
            for p in range(1, PAIRS):
                for s in range(11):
                    h_proj(p, s, 0 if s >= 8 else None)
                    if s >= 8:
                        h_inner(p - 1, s)
                        h_proj(p, s, 1)
                    if s == 0 and p > 1:
                        h_outT(p - 2, 0)
                        h_outT(p - 2, 1)
                    h_core(p - 1, s)
            for s in range(11):
                if s < 3:
                    h_proj(PAIRS, s)
                else:
                    b, n = hblock(PAIRS, s)
                    u, cb = divmod(s - 3, 2)
                    if cb == 0:
                        pe.wait_ge(lo_ready, 4 * PAIRS + u + 1)
                    open_block(b, n)
                    for half in range(2):
                        if half == 1 and s >= 8:
                            h_inner(PAIRS - 1, s)
                        last = feature_block(PB[b][:, :], u % 2, cb, LAT, range(4 * half, 4 * half + 4))
                    last.then_inc(blk_ready[b], 1)
                if s == 0:
                    h_outT(PAIRS - 2, 0)
                    h_outT(PAIRS - 2, 1)
                h_core(PAIRS - 1, s)

            def a_proj(p, s, ks):
                b, n = ablock(p, s)
                j = -1 if s < 3 else 0 if s < 5 else 1 if s < 8 else 2
                ws, _, wn = unit(A_UNIT, p, j)
                if ks == 0:
                    if s in (0, 3, 5, 8):
                        pe.wait_ge(lo_ready, wn + 1)
                    open_block(b, n)
                if s >= 8:
                    last = feature_block(PB[b][:, :], ws, s - 8, LAT, range(4 * ks, 4 * ks + 4))
                else:
                    t = (2 * s if s < 3 else 2 + 2 * (s - 3) if s < 5 else 2 * (s - 5)) + ks
                    last = token_tile(PB[b][:, ks * UC:(ks + 1) * UC], ws, t)
                if ks == 1:
                    last.then_inc(blk_ready[b], 1)

            def ga_proj(s, ks):
                b, n = ablock(PAIRS, s)
                u, cb = divmod(s - 3, 2)
                if ks == 0:
                    if cb == 0:
                        pe.wait_ge(lo_ready, A_UNIT + 4 * PAIRS + u + 1)
                    open_block(b, n)
                last = feature_block(PB[b][:, :], u % 2, cb, LAT, range(4 * ks, 4 * ks + 4))
                if ks == 1:
                    last.then_inc(blk_ready[b], 1)

            def a_qkT(c, h):
                pe.wait_ge(qn_ready, 5 * (c + 1))
                if h == 0:
                    if not (isinstance(c, int) and c == 0):
                        pe.wait_ge(exp_ready, 16 * c)
                    else:
                        pe.wait_ge(oT_done, 2 * PAIRS)
                        pe.wait_ge(kv_used, 4 * PAIRS)
                else:
                    pe.wait_ge(qkT_copied, 2 * c + 1)
                for i in range(4):
                    nc.tensor.transpose(SB[:, i * P:i * P + P], qn[:, i, h * P:h * P + P], ident[:])
                for i in range(6):
                    last = nc.tensor.transpose(SB[:, 512 + i * P:512 + (i + 1) * P],
                                               qn[:, 4 + i, h * P:h * P + P], ident[:])
                last.then_inc(qkT_ready, 1)

            def a_scores(c, j):
                h, qt = divmod(j, 4)
                if j == 0:
                    pe.wait_ge(qkT_copied, 2 * c + 2)
                if not (isinstance(c, int) and c == 0 and j == 0):
                    pe.wait_ge(exp_ready, 16 * c + 2 * j)
                for m, k0, k1 in ((0, 512, 768), (1, 256, 768), (0, 0, 512), (1, 0, 256)):
                    if (m, k0) == (1, 0):
                        pe.wait_ge(s_shared, 8 * c + j + 1)
                    r = slice(m * DH, m * DH + DH)
                    last = nc.tensor.matmul(SB[:, m * T + k0:m * T + k1], qT[r, h, qt * P:qt * P + P],
                                            kT[r, h, k0:k1], start=True, stop=True)
                    if (m, k0) == (0, 512):
                        last.then_inc(s_shared, 1)
                last.then_inc(s_ready, 1)

            def a_wT(c, j):
                pe.wait_ge(w_ready, 8 * c + j + 1)
                if not (isinstance(c, int) and c == 0 and j == 0):
                    pe.wait_ge(wT_copied, 8 * c + j)
                for i in range(6):
                    last = nc.tensor.transpose(WB[:, i * P:i * P + P], W_[:, i * P:i * P + P], ident[:])
                last.then_inc(wT_ready, 1)

            def a_pv(c, j):
                h = j // 4
                pe.wait_ge(wT_copied, 8 * c + j + 1)
                pe.wait_ge(va_ready, 3 * c + 3)
                if not (isinstance(c, int) and c == 0 and j == 0):
                    pe.wait_ge(sqA_ready, 8 * c + j)
                    if not (isinstance(c, int) and c == 0 and j == 1):
                        pe.wait_ge(oTA_done, 8 * c + max(j - 1, 0))
                for i in range(6):
                    last = nc.tensor.matmul(OB[:, 0:128], WT[:, i * P:i * P + P], VA[:, i, h * P:h * P + P],
                                            start=(i == 0), stop=(i == 5))
                last.then_inc(pv_ready, 1)

            def a_outT(c, j):
                pe.wait_ge(onA_ready, 8 * c + j + 1)
                pe.wait_ge(sqA_ready, 8 * c + min(j + 2, 8))
                if j == 7:
                    pe.wait_ge(oTA_done, 8 * c + 7)
                nc.tensor.transpose(OB[:, 128:256], on[:], ident[:]).then_inc(oTA_ready, 1)

            def a_slot(c, s, proj):
                proj(0)
                if s <= 1 and c > 0:
                    a_outT(c - 1, 6 + s)
                if s == 0:
                    proj(1)
                    a_qkT(c, 0)
                    a_qkT(c, 1)
                    return
                if s <= 8:
                    a_scores(c, s - 1)
                if s >= 4:
                    a_outT(c, s - 4)
                if s >= 2:
                    a_wT(c, s - 2)
                proj(1)
                if s >= 2:
                    a_pv(c, s - 2)

            for s in range(3, 10):
                a_proj(0, s, 0)
                a_proj(0, s, 1)
                if s == 4:
                    h_outT(PAIRS - 1, 0)
                    h_outT(PAIRS - 1, 1)
            for p in range(1, PAIRS):
                for s in range(10):
                    a_slot(p - 1, s, lambda ks: a_proj(p, s, ks))
            for s in range(10):
                if s < 3:
                    a_slot(PAIRS - 1, s, lambda ks: a_proj(PAIRS, s, ks))
                else:
                    a_slot(PAIRS - 1, s, lambda ks: ga_proj(s, ks))
            ga_proj(10, 0)
            a_outT(PAIRS - 1, 6)
            ga_proj(10, 1)
            a_outT(PAIRS - 1, 7)

            for i, what in enumerate(M_ORDER):
                n = M_UNIT + i
                pe.wait_ge(lo_ready, n + 1)
                for cb in range(2):
                    b, cnt = mblock(2 * i + cb)
                    open_block(b, cnt)
                    if what[:2] == "gh":
                        last = feature_block(PB[b][:, :], n % 2, cb, LAT)
                    else:
                        ready, yh, yl = (yA_ready, yAh, yAl) if what[:2] == "ba" else (yH_ready, yHh, yHl)
                        for k in range(KB):
                            pe.wait_ge(ready, k + 1)
                            last = feature_block(PB[b][:, :], n % 2, cb, slice(0, TL), [k], yh, yl)
                    last.then_inc(blk_ready[b], 1)
            for i in range(4):
                pe.wait_ge(lo_ready, O_UNIT + i + 1)
                for half in range(2):
                    b, cnt = mblock(OUT_BLOCK + 2 * i + half)
                    open_block(b, cnt)
                    for t in range(2):
                        for k in range(KB):
                            if (i, half, t) == (0, 0, 0):
                                pe.wait_ge(m_ready, k + 1)
                            last = token_tile(PB[b][:, t * UC:(t + 1) * UC], (O_UNIT + i) % 2, 2 * half + t,
                                              [k], mTh, mTl)
                    last.then_inc(blk_ready[b], 1)

        @block.scalar
        def _(act):
            link = Chain(act, act_chain)
            f = nc.scalar.activation

            def load(dst, src, signal=const_in):
                act.dma_start(dst, src, allow_slow_non_contiguous=True).then_inc(signal, 16)

            load(scT[:, :, 0], a["c"][0].rearrange("(k p) -> p k", p=P), c_in)
            load(scT[:, :, 1], a["c_ctx"].rearrange("(k p) -> p k", p=P), c_in)
            load(ident[:], a["ident"], start_in)
            for i in range(2):
                load(bmT[:, KB * i:KB * i + KB], a["b_mod"][0, i * D:(i + 1) * D].rearrange("(j p) -> p j", p=P),
                     start_in)
            load(ngT[:], a["norm_gain"][0].rearrange("(k p) -> p k", p=P), start_in)
            act.wait_ge(c_in, 32)
            f(modT[:, 0:KB, :], scT[:], ACT.Sigmoid).then_inc(sig_c, 1)
            act.wait_ge(x_in, 32)
            for t in range(6):
                link(f(sqx[:], xt[:, t, :], ACT.Square, accum_out=ssx[:, t:t + 1]))
            act.sem_inc(ssx_ready, 1)
            load(gH[:], a["hgrn_norm_gain"][0].rearrange("(p o) -> p o", o=1))
            load(gA[:], a["subln_gain"][0].rearrange("(p o) -> p o", o=1))
            load(masks[:], a["masks"])
            for d, name in enumerate(("hgrn_lb_fwd", "hgrn_lb_bwd")):
                for l in range(2):
                    load(lbraw[:, d, l, :], a[name][l].rearrange("(h p) -> p h", p=P))
            def first_hi(n):
                act.wait_ge(raw_ready[n], 16)
                f(wh[n][:], wraw[n][:], ACT.Copy).then_inc(hi_ready, 1)

            first_hi(0)
            for g in range(2 * KB):
                k, c = divmod(g, 2)
                n = TC if c else TL
                if g % 4 == 0:
                    act.wait_ge(mod_final, g // 4 + 1)
                act.wait_ge(xT_ready, g + 1)
                if g >= 2:
                    act.wait_ge(h_split, g - 1)
                f(htmp[:, g % 2, 0:n], LV[g % 2][:, 0:n], ACT.Identity, scale=modT[:, KB + k, c:c + 1],
                  bias=modT[:, k, c:c + 1])
                f(hTh[:, k, CTX if c else LAT], LV[g % 2][:, 0:n], ACT.Identity, scale=modT[:, KB + k, c:c + 1],
                  bias=modT[:, k, c:c + 1]).then_inc(xT_used, 1)
                if g == 11:
                    first_hi(1)
            load(gate[:], a["b_mod"][0:1, 2 * D:3 * D].to_broadcast([P, D]), bias_in)
            for i in range(2):
                act.dma_start(cosg[:, i, :, :], a["cos"].rearrange("(t p) d -> p t d", p=P)).then_inc(tab_in, 16)
                act.dma_start(sing[:, i, :, :], a["sin"].rearrange("(t p) d -> p t d", p=P)).then_inc(tab_in, 16)
            for i, name in enumerate(("q_norm_gain", "k_norm_gain")):
                act.dma_start(gqk[:, i, :], a[name][0:1, :].to_broadcast([P, DH])).then_inc(tab_in, 16)
            for i, name in enumerate(("lambda_q1", "lambda_k1", "lambda_q2", "lambda_k2")):
                act.dma_start(lamq[:, i, :], a[name][0:1, :].to_broadcast([P, DH])).then_inc(tab_in, 16)
            act.wait_ge(lbd_ready, 1)
            f(lb[:], om[:], ACT.Sigmoid).then_inc(lb_ready, 1)
            act.wait_ge(lb_ready, 1)
            f(om[:], om[:], ACT.Sigmoid, scale=-1.0).then_inc(lb_ready, 1)

            def h_evac(p, s):
                b, n = hblock(p, s)
                act.wait_ge(blk_ready[b], n + 1)
                if s < 3:
                    c = p - 1
                    if not (isinstance(c, int) and c == 0):
                        act.wait_ge(out_ready, 2 * c)
                    f(V[:, 2 * s:2 * s + 2, :], PB[b][:, :].rearrange("p (t c) -> p t c", t=2),
                      ACT.Copy).then_inc(v_ready, 1)
                    act.wait_ge(v_ready, 3 * c + s + 1)
                    act.sem_inc(blk_free[b], 1)
                    return
                if s == 3 and not (isinstance(p, int) and p == 0):
                    act.wait_ge(sig_used, 2 * p)
                if s < 9:
                    d, i = divmod(s - 3, 3)
                    if i == 2:
                        f(sig[:, :, d, 0:TC], PB[b][:, :].rearrange("p (h t) -> p h t", h=2),
                          ACT.Sigmoid).then_inc(blk_free[b], 1)
                    else:
                        f(sig[:, i, d, LAT], PB[b][:, :], ACT.Sigmoid).then_inc(blk_free[b], 1)
                else:
                    if not (isinstance(p, int) and p == 0):
                        act.wait_ge(scores_ready, 16 * (p - 1) + 2)
                    f(qs[:, s - 9, :], PB[b][:, :], ACT.Sigmoid).then_inc(qsig_ready, 1)

            def halves(ap, l, which, n=TL):
                B = 1 << l
                return ap.rearrange("p (n two b) -> p n two b", two=2, b=B)[:, :, which, :]

            def h_mix(c, st):
                l = st - 1
                for h in range(2):
                    act.wait_ge(levels_ready, 16 * c + 2 * l + h + 1)
                    if l > 0:
                        act.wait_ge(scores_ready, 16 * c + 2 * l + h + 1)
                    elif not (isinstance(c, int) and c == 0):
                        act.wait_ge(scores_ready, 16 * c)
                    for dst, src, side in ((mixQ, Q_, 0), (mixK, K_, 1)):
                        cols = slice(0, TL) if side == 0 else LAT
                        f(halves(dst[:, h, :], l, 1 - side), halves(src[:, h, 0, cols], l, 1 - side), ACT.Copy)
                        last = f(halves(dst[:, h, :], l, side), halves(src[:, h, 1, cols], l, side), ACT.Copy)
                    last.then_inc(mix_ready, 1)

            def h_keysT_copy(c, u):
                h, d = divmod(u, 2)
                act.wait_ge(kT_ready, 4 * c + u + 1)
                f(totE[:, h, d, 0:640], X[u % 2][:, 0:640], ACT.Copy).then_inc(kT_copied, 1)

            def h_square(c, h):
                act.wait_ge(out_ready, 2 * c + h + 1)
                if not (isinstance(c, int) and c == 0):
                    act.wait_ge(rrH_ready, 2 * c)
                for ch in range(NCH):
                    last = f(mixQ[:, h, ch * P:ch * P + P], LV[h][:, ch * P:ch * P + P], ACT.Square,
                             accum_out=ssH[:, h, ch:ch + 1])
                link(last)
                act.sem_inc(sqH_ready, 1)

            def h_outT_copy(c, h, head):
                act.wait_ge(oT_ready, 2 * c + h + 1)
                f(oTH[:, head, :], X[h][:, 0:TL], ACT.Copy, scale=gH[:, 0:1]).then_inc(oT_done, 1)

            def h_inner(c, s):
                if s in (8, 9):
                    h_keysT_copy(c, 2 * (s - 8))
                    h_keysT_copy(c, 2 * (s - 8) + 1)
                elif s == 10:
                    h_square(c, 0)

            def h_slot_core(c, s):
                if s < 7:
                    h_mix(c, s + 1)
                elif s == 10:
                    h_square(c, 1)

            HI_AT = {2: 1, 5: 2, 8: 3, 10: 4}

            def hi_after(base_, p, s, table):
                if s in table:
                    sl, cnt, n = unit(base_, p, table[s])
                    act.wait_ge(raw_ready[sl], 16 * (cnt + 1))
                    f(wh[sl][:], wraw[sl][:], ACT.Copy).then_inc(hi_ready, 1)

            for s in range(3, 11):
                h_evac(0, s)
                hi_after(0, 0, s, {5: 2, 8: 3, 10: 4})
            for p in range(1, PAIRS):
                for s in range(11):
                    h_inner(p - 1, s)
                    h_evac(p, s)
                    if s == 1 and p > 1:
                        h_outT_copy(p - 2, 0, 2 * (p - 2))
                        h_outT_copy(p - 2, 1, 2 * (p - 2) + 1)
                    h_slot_core(p - 1, s)
                    hi_after(0, p, s, HI_AT)
            for s in range(11):
                h_inner(PAIRS - 1, s)
                if s < 3:
                    h_evac(PAIRS, s)
                else:
                    b, n = hblock(PAIRS, s)
                    act.wait_ge(blk_ready[b], n + 1)
                    if s == 3:
                        act.wait_ge(sig_used, 2 * PAIRS)
                    f(zh[:, s - 3, :], PB[b][:, :], ACT.Sigmoid).then_inc(zsig_ready, 1)
                if s == 1:
                    h_outT_copy(PAIRS - 2, 0, HEADS - 4)
                    h_outT_copy(PAIRS - 2, 1, HEADS - 3)
                h_slot_core(PAIRS - 1, s)
                hi_after(0, PAIRS, s, {2: 1, 4: 2, 6: 3, 8: 4, 10: 5})

            act.wait_ge(lamd_ready, 1)
            f(lame[:], lame[:], ACT.Exp).then_inc(lame_ready, 1)

            def a_evac(p, s):
                b, n = ablock(p, s)
                act.wait_ge(blk_ready[b], n + 1)
                if s < 3:
                    if not (isinstance(p, int) and p == 1):
                        act.wait_ge(pv_ready, 8 * (p - 1))
                    f(VA[:, 2 * s:2 * s + 2, :], PB[b][:, :].rearrange("p (t c) -> p t c", t=2),
                      ACT.Copy).then_inc(va_ready, 1)
                    act.wait_ge(va_ready, 3 * (p - 1) + s + 1)
                    act.sem_inc(blk_free[b], 1)
                elif s >= 8:
                    f(zA[:, 2 * p + s - 8, :], PB[b][:, :], ACT.Copy).then_inc(blk_free[b], 1)
                else:
                    i = 5 * p + s - 3
                    if not (isinstance(i, int) and i == 0):
                        act.wait_ge(qn_ready, i)
                    f(rtmp[:, 0, :], PB[b][:, :], ACT.Copy)
                    link(f(rtmp[:, 1, :], PB[b][:, :], ACT.Square))
                    act.sem_inc(blk_free[b], 1)
                    act.sem_inc(raw_copied, 1)

            def a_qkT_copy(c, h):
                act.wait_ge(qkT_ready, 2 * c + h + 1)
                f(qT[:, h, :], SB[:, 0:TL], ACT.Copy)
                f(kT[:, h, :], SB[:, TL:TL + T], ACT.Copy).then_inc(qkT_copied, 1)

            def a_square(c, j):
                act.wait_ge(pv_ready, 8 * c + j + 1)
                if not (isinstance(c, int) and c == 0 and j < 2):
                    act.wait_ge(onA_ready, 8 * c + j - 1)
                f(osb[:, j % 2, :], OB[:, 0:128], ACT.Copy)
                link(f(junk[:], OB[:, 0:128], ACT.Square, accum_out=ssA[:, j:j + 1]))
                act.sem_inc(sqA_ready, 1)

            def a_outT_copy(c, j):
                h, qt = divmod(j, 4)
                act.wait_ge(oTA_ready, 8 * c + j + 1)
                f(oTA[:, 2 * c + h, qt * P:qt * P + P], OB[:, 128:256], ACT.Copy,
                  scale=gA[:, 0:1]).then_inc(oTA_done, 1)

            def a_wT_copy(c, j):
                act.wait_ge(wT_ready, 8 * c + j + 1)
                f(WT[:], WB[:, 0:768], ACT.Copy).then_inc(wT_copied, 1)

            def a_exp(c, j):
                act.wait_ge(max_ready, 8 * c + j + 1)
                for m in range(2):
                    if not (isinstance(c, int) and c == 0 and j == 0):
                        act.wait_ge(w_ready, 8 * c + j)
                    link(f(E_[:, m, :], SB[:, m * T:(m + 1) * T], ACT.Exp,
                           bias=nmax[:, j, m:m + 1], accum_out=esum[:, j, m:m + 1]))
                    act.sem_inc(exp_ready, 1)

            def a_slot_core(c, s):
                if s == 0:
                    if c > 0:
                        a_outT_copy(c - 1, 6)
                    a_qkT_copy(c, 0)
                    a_qkT_copy(c, 1)
                    return
                if s == 1 and c > 0:
                    a_outT_copy(c - 1, 7)
                if s >= 3:
                    a_square(c, s - 3)
                if s >= 4:
                    a_outT_copy(c, s - 4)
                if s >= 2:
                    a_wT_copy(c, s - 2)
                if s <= 8:
                    a_exp(c, s - 1)

            A_HI = {2: 1, 4: 2, 7: 3, 9: 4}
            for s in range(3, 10):
                if s == 7:
                    b, n = ablock(0, 7)
                    act.wait_ge(blk_ready[b], n + 1)
                    hi_after(A_UNIT, 0, s, {7: 3})
                a_evac(0, s)
                if s == 3:
                    h_outT_copy(PAIRS - 1, 0, HEADS - 2)
                    h_outT_copy(PAIRS - 1, 1, HEADS - 1)
                hi_after(A_UNIT, 0, s, {4: 2, 9: 4})
            for p in range(1, PAIRS):
                for s in range(10):
                    if s == 0:
                        if p > 1:
                            a_square(p - 2, 7)
                        a_evac(p, s)
                    a_slot_core(p - 1, s)
                    if s > 0:
                        a_evac(p, s)
                    hi_after(A_UNIT, p, s, A_HI)

            def ga_evac(s):
                b, n = ablock(PAIRS, s)
                act.wait_ge(blk_ready[b], n + 1)
                f(ga[:, s - 3, :], PB[b][:, :], ACT.Copy).then_inc(ga_ready, 1)
                act.wait_ge(ga_ready, s - 2)
                act.sem_inc(blk_free[b], 1)

            for s in range(10):
                if s == 0:
                    a_square(PAIRS - 2, 7)
                    a_evac(PAIRS, s)
                a_slot_core(PAIRS - 1, s)
                if 0 < s < 3:
                    a_evac(PAIRS, s)
                elif s >= 3:
                    ga_evac(s)
                hi_after(A_UNIT, PAIRS, s, {2: 1, 4: 2, 6: 3, 8: 4})
            a_square(PAIRS - 1, 7)
            a_outT_copy(PAIRS - 1, 6)
            ga_evac(10)
            a_outT_copy(PAIRS - 1, 7)

            def m_hi(i):
                sl, cnt, n = unit(M_UNIT, 0, i)
                if i >= 2:
                    b, c0 = mblock(2 * (i - 2) + 1)
                    act.wait_ge(blk_ready[b], c0 + 1)
                act.wait_ge(raw_ready[sl], 16 * (cnt + 1))
                f(wh[sl][:], wraw[sl][:], ACT.Copy).then_inc(hi_ready, 1)

            m_hi(1)
            act.wait_ge(onA_ready, 8 * PAIRS)
            act.wait_ge(oTA_done, 8 * PAIRS)
            for k in range(KB):
                f(ysig[:, k, :], zA[:, k, :], ACT.Sigmoid).then_inc(ysig_ready, 1)
            for i, what in enumerate(M_ORDER):
                if what[:2] == "gh":
                    j = int(what[2])
                    if j >= 2:
                        act.wait_ge(m_ready, 2 * (j - 1))
                    for cb in range(2):
                        b, cnt = mblock(2 * i + cb)
                        act.wait_ge(blk_ready[b], cnt + 1)
                        f(gh[:, j % 2, cb, :], PB[b][:, :], ACT.Sigmoid).then_inc(gh_ready, 1)
                        act.wait_ge(gh_ready, 2 * j + cb + 1)
                        act.sem_inc(blk_free[b], 1)
                if i + 2 < len(M_ORDER):
                    m_hi(i + 2)
                if i == 0:
                    act.wait_ge(ga_ready, 8)
                    f(ga[:], ga[:], ACT.Sigmoid).then_inc(gasig_ready, 1)
                if i == 1:
                    act.wait_ge(oTH_final, 8)
                    for k in range(KB):
                        f(yHh[:, k, :], oTH[:, k, :], ACT.Copy).then_inc(yHh_ready, 1)
            for i in range(4):
                b, c0 = mblock(2 * (10 + i) + 1)
                act.wait_ge(blk_ready[b], c0 + 1)
                sl, cnt, n = unit(O_UNIT, 0, i)
                act.wait_ge(raw_ready[sl], 16 * (cnt + 1))
                f(wh[sl][:], wraw[sl][:], ACT.Copy).then_inc(hi_ready, 1)

        @block.vector
        def _(dve):
            link = Chain(dve, dve_chain)
            v = nc.vector

            def bc(ap, shape):
                return ap.to_broadcast(shape)

            dve.wait_ge(sig_c, 1)
            v.tensor_tensor(scT[:], scT[:], modT[:, 0:KB, :], ALU.mult).then_inc(sc_ready, 1)
            dve.wait_ge(rrx_ready, 1)
            for t in range(6):
                v.tensor_scalar(xt[:, t, :], xt[:, t, :], rrx[:, t:t + 1], None, ALU.mult).then_inc(xn_ready, 1)
            def mod_sums(i, us):
                for u in us:
                    dve.wait_ge(mod_in[i + 4 * u], 16)
                for k in range(KB):
                    for u in us:
                        for c in range(2):
                            dst, w = macc[i][:, u, c, :], wmod[i + 4 * u][:, k, :]
                            if k == 0:
                                last = v.tensor_scalar(dst, w, scT[:, 0, c:c + 1], None, ALU.mult)
                            else:
                                last = v.scalar_tensor_tensor(dst, w, scT[:, k, c:c + 1], dst, ALU.mult, ALU.add)
                    if k < KB - 1:
                        link(last)
                last.then_inc(macc_ready, 1)

            def mod_finish(i, used):
                sh, sc = slice(2 * i, 2 * i + 2), slice(KB + 2 * i, KB + 2 * i + 2)
                dve.wait_ge(mod_used, used)
                ps = PX[:, 2 + i, 0:8].rearrange("p (j c) -> p j c", c=2)
                v.tensor_tensor(modT[:, sh, :], ps[:, 0:2, :], bc(bmT[:, sh].unsqueeze(2), [P, 2, 2]), ALU.add)
                link(v.tensor_tensor(modT[:, sc, :], ps[:, 2:4, :], bc(bmT[:, sc].unsqueeze(2), [P, 2, 2]),
                                     ALU.add))
                link(v.tensor_scalar(modT[:, sc, :], modT[:, sc, :], 1.0, None, ALU.add))
                v.tensor_tensor(modT[:, sc, :], modT[:, sc, :], bc(ngT[:, sh].unsqueeze(2), [P, 2, 2]),
                                ALU.mult).then_inc(mod_final, 1)

            dve.wait_ge(sc_ready, 1)
            dve.wait_ge(ssx_ready, 1)
            mod_sums(1, (0, 1))
            dve.wait_ge(start_in, 16 * 4)
            mod_finish(0, 2)
            mod_sums(3, (0,))
            mod_finish(1, 6)
            mod_finish(2, 6)
            mod_sums(3, (1,))
            mod_finish(3, 8)
            dve.wait_ge(const_in, 16 * 7)
            v.tensor_tensor(om[:], lbraw[:, :, 0, :], lbraw[:, :, 1, :], ALU.subtract).then_inc(lbd_ready, 1)
            dve.wait_ge(lb_ready, 2)
            link(v.tensor_scalar(nom[:], om[:], -1.0, None, ALU.mult))

            def halves(ap, l, which):
                return ap.rearrange("p (n two b) -> p n two b", two=2, b=1 << l)[:, :, which, :]

            def h_qmul(p, i):
                b, n = hblock(p, 9 + i)
                dve.wait_ge(qsig_ready, 2 * p + i + 1)
                v.tensor_tensor(qs[:, i, :], PB[b][:, :], qs[:, i, :], ALU.mult).then_inc(q_ready, 1)
                dve.wait_ge(q_ready, 2 * p + i + 1)
                dve.sem_inc(blk_free[b], 1)

            def h_prep_gates(p, h):
                b, n = hblock(p, 8)
                dve.wait_ge(blk_free[b], n + 1)
                for d in range(2):
                    head = 2 * p + h
                    v.tensor_scalar(totE[:, h, d, :], sig[:, h, d, :], om[:, d, head:head + 1],
                                    lb[:, d, head:head + 1], ALU.mult, ALU.add)
                    link(v.tensor_scalar(K_[:, h, d, :], sig[:, h, d, :], nom[:, d, head:head + 1],
                                         om[:, d, head:head + 1], ALU.mult, ALU.add))

            def h_prep_queries(p):
                for h in range(2):
                    v.tensor_tensor(ksum[:, h, :], K_[:, h, 0, LAT], K_[:, h, 1, LAT],
                                    ALU.add).then_inc(diag_ready, 1)
                    v.tensor_tensor(Q_[:, h, 0, :], qs[:, h, :], totE[:, h, 0, LAT], ALU.mult)
                    link(v.tensor_tensor(Q_[:, h, 1, :], qs[:, h, :], totE[:, h, 1, LAT], ALU.mult))
                    dve.sem_inc(levels_ready, 1)
                    dve.sem_inc(sig_used, 1)

            def tot(l, h, d):
                return (totO if l % 2 else totE)[:, h, d, 0:T >> l]

            def h_join(c, l, h):
                dve.wait_ge(mix_ready, 14 * c + 2 * l + h + 1)
                B = 1 << l
                n, nq = T // (2 * B), TL // (2 * B)
                for d in range(2):
                    tt = tot(l, h, d).rearrange("p (n two) -> p n two", two=2)
                    near, far = d, 1 - d
                    kk = halves(K_[:, h, d, :], l, near)
                    v.tensor_tensor(kk, kk, bc(tt[:, :, far:far + 1], [P, n, B]), ALU.mult)
                    qq = halves(Q_[:, h, d, :], l, far)
                    v.tensor_tensor(qq, qq, bc(tt[:, TC // (2 * B):, near:near + 1], [P, nq, B]), ALU.mult)
                    last = v.tensor_tensor(tot(l + 1, h, d), tt[:, :, 0], tt[:, :, 1], ALU.mult)
                last.then_inc(levels_ready, 1)

            def h_pick(c, st, h):
                dve.wait_ge(scores_ready, 16 * c + 2 * st + h + 1)
                if st == 0 and not (isinstance(c, int) and c == 0):
                    dve.wait_ge(oT_ready, 2 * (c - 1) + h + 1)
                v.copy_predicated(AT[:, h, :].rearrange("p (n t) -> p n t", n=NCH),
                                  bc(masks[:, st:st + 1, :], [P, NCH, CH]),
                                  LV[h].rearrange("p (n t) -> p n t", n=NCH)).then_inc(scores_used, 1)

            def h_states(c, u):
                h, d = divmod(u, 2)
                dve.wait_ge(kv_ready, 4 * c + u + 1)
                order = (0, 1, 2, 3, 4) if d == 0 else (1, 0, 5, 4, 3)
                last_tot = tot(LEVELS, h, d)
                at_chunk = [0, 0, 1, 2, 3] if d == 0 else [3, 3, 2, 1, 0]
                link(v.tensor_copy(S_[:, h, d, at_chunk[0], :], X[u % 2][:, 0:P]))
                for i in range(1, 5):
                    ins = v.scalar_tensor_tensor(S_[:, h, d, at_chunk[i], :], S_[:, h, d, at_chunk[i - 1], :],
                                                 last_tot[:, order[i]:order[i] + 1],
                                                 X[u % 2][:, i * P:i * P + P], ALU.mult, ALU.add)
                    if i < 4:
                        link(ins)
                ins.then_inc(kv_used, 1)

            def h_norm(c, h):
                dve.wait_ge(rrH_ready, 2 * c + h + 1)
                dve.wait_ge(out_ready, 2 * c + h + 1)
                v.tensor_tensor(AT[:, h, :].rearrange("p (n t) -> p n t", n=NCH),
                                LV[h].rearrange("p (n t) -> p n t", n=NCH),
                                bc(rrH[:, h, :].unsqueeze(2), [P, NCH, CH]), ALU.mult).then_inc(onH_ready, 1)

            def h_slot(c, s):
                if 1 <= s < 8:
                    if s == 1:
                        h_pick(c, 0, 0)
                        h_pick(c, 0, 1)
                    h_join(c, s - 1, 0)
                    h_join(c, s - 1, 1)
                    h_pick(c, s, 0)
                    h_pick(c, s, 1)
                elif s in (8, 9):
                    h_states(c, 2 * (s - 8))
                    h_states(c, 2 * (s - 8) + 1)

            dve.wait_ge(tab_in, 16 * 10)
            link(v.tensor_scalar(gqk[:, 0, :], gqk[:, 0, :], DH ** -0.5, None, ALU.mult))
            for i in range(2):
                g = gqk[:, i:i + 1, :]
                v.tensor_tensor(cosg[:, i, :, :], cosg[:, i, :, :], bc(g, [P, 4, DH]), ALU.mult)
                for x_ in range(2):
                    for h in range(2):
                        lo = 32 * x_ + 16 * h
                        src = 32 * x_ + 16 * (1 - h)
                        v.tensor_tensor(sing[:, i, :, lo:lo + 16], sing[:, i, :, lo:lo + 16],
                                        bc(g[:, :, src:src + 16], [P, 4, 16]), ALU.mult)
            link(v.tensor_tensor(lamq[:, 0:4:2, :], lamq[:, 0:4:2, :], lamq[:, 1:4:2, :], ALU.mult))
            v.tensor_reduce(lame[:], lamq[:, 0:4:2, :], AX.X, ALU.add).then_inc(lamd_ready, 1)
            for half in range(2):
                for u in (2 * half, 2 * half + 1):
                    dve.wait_ge(gate_in[u], 16)
                for k in range(KB):
                    for u in (2 * half, 2 * half + 1):
                        if k == 0:
                            last = v.tensor_scalar(gacc[:, u, :], wmod[u][:, 0, :], scT[:, 0, 0:1], None, ALU.mult)
                        else:
                            last = v.scalar_tensor_tensor(gacc[:, u, :], wmod[u][:, k, :], scT[:, k, 0:1],
                                                          gacc[:, u, :], ALU.mult, ALU.add)
                    if k < KB - 1:
                        link(last)
                last.then_inc(gacc_ready, 1)
            h_prep_gates(0, 0)
            h_prep_gates(0, 1)
            h_qmul(0, 0)
            h_qmul(0, 1)
            h_prep_queries(0)
            dve.wait_ge(bias_in, 16)
            dve.wait_ge(gate_bc, 1)
            v.tensor_tensor(gate[:], X[1], gate[:], ALU.add).then_inc(gate_ready, 1)
            for p in range(1, PAIRS):
                for s in range(11):
                    if s == 9:
                        h_qmul(p, 0)
                    h_slot(p - 1, s)
                    if s == 10:
                        h_prep_gates(p, 0)
                        h_prep_gates(p, 1)
                        h_qmul(p, 1)
                h_norm(p - 1, 0)
                h_norm(p - 1, 1)
                h_prep_queries(p)
            for s in range(11):
                if s != 9:
                    h_slot(PAIRS - 1, s)
                if s >= 3:
                    b, n = hblock(PAIRS, s)
                    dve.wait_ge(zsig_ready, s - 2)
                    v.tensor_tensor(zh[:, s - 3, :], PB[b][:, :], zh[:, s - 3, :], ALU.mult).then_inc(zh_ready, 1)
                    dve.wait_ge(zh_ready, s - 2)
                    dve.sem_inc(blk_free[b], 1)
                if s == 9:
                    h_slot(PAIRS - 1, s)
            h_norm(PAIRS - 1, 0)
            h_norm(PAIRS - 1, 1)
            dve.wait_ge(lame_ready, 1)
            link(v.tensor_tensor(lamv[:], lame[:, 1:2], lame[:, 0:1], ALU.subtract))
            link(v.tensor_scalar(lamv[:], lamv[:], -LAM_INIT, None, ALU.add))
            v.tensor_scalar(gA[:], gA[:], 1.0 - LAM_INIT, None, ALU.mult).then_inc(tab_ready, 1)

            def a_rope(p, s):
                i = 5 * p + s - 3
                dve.wait_ge(raw_copied, i + 1)
                v.tensor_reduce(ssn[:], rtmp[:, 1, :].rearrange("p (g d) -> p g d", d=DH), AX.X,
                                ALU.add).then_inc(ssn_ready, 1)
                dve.wait_ge(rrn_ready, i + 1)
                g3 = lambda ap: ap.rearrange("p (g d) -> p g d", d=DH)
                which = 0 if s < 5 else 1
                first = 2 * (s - 3) if s < 5 else 4 + 2 * (s - 5)
                lat = 2 * (s - 3) if s < 5 else 2 * (s - 6)
                if s == 3 and not (isinstance(p, int) and p == 0):
                    dve.wait_ge(qkT_ready, 2 * p)
                dst = qn[:, first:first + 2, :]
                if s == 5:
                    link(v.tensor_tensor(g3(rtmp[:, 2, :]), g3(rtmp[:, 0, :]), bc(rrn[:].unsqueeze(2), [P, 8, DH]),
                                         ALU.mult))
                    dve.sem_inc(u_ready, 1)
                    v.tensor_tensor(dst.rearrange("p t (g d) -> p (t g) d", d=DH), g3(rtmp[:, 2, :]),
                                    bc(gqk[:, 1:2, :], [P, 8, DH]), ALU.mult).then_inc(qn_ready, 1)
                    return
                v.tensor_tensor(g3(rtmp[:, 2, :]), g3(rtmp[:, 0, :]), bc(rrn[:].unsqueeze(2), [P, 8, DH]),
                                ALU.mult).then_inc(u_ready, 1)
                dve.wait_ge(u_ready, i + 1)
                for t in range(2):
                    uu = rtmp[:, 2, t * UC:(t + 1) * UC].rearrange("p (g a b d) -> p g a b d", a=2, b=2, d=16)
                    rr = rtmp[:, 1, t * UC:(t + 1) * UC].rearrange("p (g a b d) -> p g a b d", a=2, b=2, d=16)
                    sn = sing[:, which, lat + t, :].rearrange("p (a b d) -> p a b d", a=2, b=2)
                    for b_ in range(2):
                        last = v.tensor_tensor(rr[:, :, :, b_, :], uu[:, :, :, 1 - b_, :],
                                               bc(sn[:, :, b_, :].unsqueeze(1), [P, 4, 2, 16]), ALU.mult)
                link(last)
                dve.wait_ge(t1_ready, i + 1)
                v.tensor_tensor(dst, rtmp[:, 3, :].rearrange("p (t c) -> p t c", t=2),
                                rtmp[:, 1, :].rearrange("p (t c) -> p t c", t=2), ALU.add).then_inc(qn_ready, 1)

            def a_max(c, j):
                dve.wait_ge(s_ready, 8 * c + j + 1)
                v.tensor_reduce(nmax[:, j, :], SB.rearrange("p (m k) -> p m k", m=2), AX.X, ALU.max,
                                negate=True).then_inc(max_ready, 1)

            def a_weights(c, j):
                dve.wait_ge(exp_ready, 16 * c + 2 * j + 2)
                link(v.reciprocal(coef[:, j, 0:1], esum[:, j, 1:2]))
                link(v.tensor_tensor(coef[:, j, 1:2], coef[:, j, 0:1], esum[:, j, 0:1], ALU.mult))
                link(v.tensor_scalar(coef[:, j, 0:1], coef[:, j, 1:2], lamv[:, 0:1], None, ALU.mult))
                v.scalar_tensor_tensor(eA[:, j:j + 1], esum[:, j, 0:1], EPS, esum[:, j, 0:1], ALU.mult, ALU.mult)
                if not (isinstance(c, int) and c == 0 and j == 0):
                    dve.wait_ge(wT_ready, 8 * c + j)
                v.scalar_tensor_tensor(W_[:], E_[:, 1, :], coef[:, j, 0:1], E_[:, 0, :],
                                       ALU.mult, ALU.add).then_inc(w_ready, 1)

            def a_norm(c, j):
                dve.wait_ge(rrA_ready, 8 * c + j + 1)
                if not (isinstance(c, int) and c == 0 and j == 0):
                    dve.wait_ge(oTA_ready, 8 * c + j)
                v.tensor_scalar(on[:], osb[:, j % 2, :], rrA[:, j:j + 1], None, ALU.mult).then_inc(onA_ready, 1)

            def a_slot(c, s):
                if s == 0 and c > 0:
                    a_norm(c - 1, 7)
                if 1 <= s <= 8:
                    a_max(c, s - 1)
                    a_weights(c, s - 1)
                if s >= 3:
                    a_norm(c, s - 3)

            for s in range(3, 8):
                if s == 7:
                    sl, _, n = unit(A_UNIT, 0, 3)
                    dve.wait_ge(hi_ready, n + 1)
                    v.tensor_tensor(wl[sl][:], wraw[sl][:], wh[sl][:].bitcast(F32),
                                    ALU.subtract).then_inc(lo_ready, 1)
                a_rope(0, s)
            for head in range(HEADS):
                dve.wait_ge(oT_done, head + 1)
                v.tensor_tensor(oTH[:, head, :], oTH[:, head, :], zh[:, head, :], ALU.mult).then_inc(oTH_final, 1)
            for p in range(1, PAIRS):
                for s in range(10):
                    a_slot(p - 1, s)
                    if 3 <= s < 8:
                        a_rope(p, s)
            for s in range(10):
                a_slot(PAIRS - 1, s)
            a_norm(PAIRS - 1, 7)

            dve.wait_ge(oTA_ready, 8 * PAIRS)
            dve.wait_ge(oTA_done, 8 * PAIRS)
            for k in range(KB):
                dve.wait_ge(ysig_ready, k + 1)
                link(v.tensor_tensor(zA[:, k, :], zA[:, k, :], ysig[:, k, :], ALU.mult))
                link(v.tensor_tensor(oTA[:, k, :], oTA[:, k, :], zA[:, k, :], ALU.mult))
                link(v.tensor_copy(yAh[:, k, :], oTA[:, k, :]))
                v.tensor_tensor(yAl[:, k, :], oTA[:, k, :], yAh[:, k, :].bitcast(F32),
                                ALU.subtract).then_inc(yA_ready, 1)
            for k in range(KB):
                dve.wait_ge(yHh_ready, k + 1)
                v.tensor_tensor(yHl[:, k, :], oTH[:, k, :], yHh[:, k, :].bitcast(F32),
                                ALU.subtract).then_inc(yH_ready, 1)
            dve.wait_ge(gasig_ready, 1)
            for i, what in enumerate(M_ORDER):
                j = int(what[2])
                for cb in range(2):
                    k = 2 * j + cb
                    b, cnt = mblock(2 * i + cb)
                    if what[:2] == "ba":
                        dve.wait_ge(blk_ready[b], cnt + 1)
                        link(v.tensor_tensor(ga[:, k, :], PB[b][:, :], ga[:, k, :], ALU.mult))
                        dve.sem_inc(blk_free[b], 1)
                    elif what[:2] == "bh":
                        dve.wait_ge(blk_ready[b], cnt + 1)
                        dve.wait_ge(gh_ready, k + 1)
                        link(v.tensor_tensor(gh[:, j % 2, cb, :], PB[b][:, :], gh[:, j % 2, cb, :], ALU.mult))
                        dve.sem_inc(blk_free[b], 1)
                        link(v.tensor_tensor(ga[:, k, :], ga[:, k, :], gh[:, j % 2, cb, :], ALU.add))
                        link(v.tensor_copy(mTh[:, k, :], ga[:, k, :]))
                        v.tensor_tensor(mTl[:, k, :], ga[:, k, :], mTh[:, k, :].bitcast(F32),
                                        ALU.subtract).then_inc(m_ready, 1)
            dve.wait_ge(xb_in, 16)
            for n in range(8):
                u, half = divmod(n, 2)
                b, cnt = mblock(OUT_BLOCK + n)
                dve.wait_ge(blk_ready[b], cnt + 1)
                c = slice(u * UC, (u + 1) * UC)
                if n >= 2:
                    dve.wait_ge(o_ready, n - 1)
                link(v.tensor_tensor(ytmp[:, n % 2, :, :], PB[b][:, :].rearrange("p (t c) -> p t c", t=2),
                                     bc(gate[:, c].unsqueeze(1), [P, 2, UC]), ALU.mult))
                dve.sem_inc(blk_free[b], 1)
                xx = xb[:, 2 * half:2 * half + 2, c]
                v.tensor_tensor(xx, xx, ytmp[:, n % 2, :, :], ALU.add).then_inc(o_ready, 1)

        @block.gpsimd
        def _(pool):
            link = Chain(pool, pool_chain)
            g = nc.gpsimd

            def split_lo(sl, n):
                pool.wait_ge(hi_ready, n + 1)
                g.tensor_tensor(wl[sl][:], wraw[sl][:], wh[sl][:].bitcast(F32), ALU.subtract).then_inc(lo_ready, 1)

            def rsqrt(dst, src, scale, eps, done):
                link(g.tensor_scalar(dst, src, scale, eps, ALU.mult, ALU.add))
                n = dst.shape[-1]
                return g.tensor_tensor(dst, dst, mhalf[:, 0:n], ALU.pow).then_inc(done, 1)

            link(g.memset(mhalf[:], -0.5))
            g.memset(ones[:], 1.0).then_inc(ones_ready, 1)
            pool.wait_ge(ssx_ready, 1)
            rsqrt(rrx[:], ssx[:], 1.0 / D, EPS, rrx_ready)
            split_lo(0, 0)
            for g_ in range(2 * KB):
                k, c = divmod(g_, 2)
                cols = CTX if c else LAT
                pool.wait_ge(xT_used, g_ + 1)
                g.tensor_tensor(hTl[:, k, cols], htmp[:, g_ % 2, 0:TC if c else TL], hTh[:, k, cols].bitcast(F32),
                                ALU.subtract).then_inc(h_split, 1)
                if g_ == 11:
                    split_lo(1, 1)

            def h_rsqrt(c):
                for h in range(2):
                    pool.wait_ge(sqH_ready, 2 * c + h + 1)
                    rsqrt(rrH[:, h, :], ssH[:, h, :], 1.0 / P, EPS, rrH_ready)

            for p in range(PAIRS):
                for j in (2, 3, 4, 5):
                    if j == 4 and p > 0:
                        h_rsqrt(p - 1)
                    n = 4 * p + j
                    split_lo(n % 2, n)
            for n in range(4 * PAIRS + 2, A_UNIT + 2):
                if n == A_UNIT + 1:
                    h_rsqrt(PAIRS - 1)
                split_lo(n % 2, n)

            def a_rsqrt(c, j):
                pool.wait_ge(sqA_ready, 8 * c + j + 1)
                link(g.tensor_scalar(rrA[:, j:j + 1], ssA[:, j:j + 1], 1.0 / P, None, ALU.mult))
                link(g.tensor_tensor(rrA[:, j:j + 1], rrA[:, j:j + 1], eA[:, j:j + 1], ALU.add))
                g.tensor_tensor(rrA[:, j:j + 1], rrA[:, j:j + 1], mhalf[:, 0:1], ALU.pow).then_inc(rrA_ready, 1)

            def a_rope(p, s):
                i = 5 * p + s - 3
                pool.wait_ge(ssn_ready, i + 1)
                rsqrt(rrn[:], ssn[:], 1.0 / DH, EPS, rrn_ready)
                pool.wait_ge(u_ready, i + 1)
                which = 0 if s < 5 else 1
                lat = 2 * (s - 3) if s < 5 else 2 * (s - 6)
                if s == 5:
                    return pool.sem_inc(t1_ready, 1)
                for t in range(2):
                    last = g.tensor_tensor(rtmp[:, 3, t * UC:(t + 1) * UC].rearrange("p (g d) -> p g d", d=DH),
                                           rtmp[:, 2, t * UC:(t + 1) * UC].rearrange("p (g d) -> p g d", d=DH),
                                           cosg[:, which, lat + t:lat + t + 1, :].to_broadcast([P, 4, DH]), ALU.mult)
                last.then_inc(t1_ready, 1)

            A_LO = {2: 1, 4: 2, 7: 3, 9: 4}

            def lo_after(p, s, table):
                if s in table:
                    sl, _, n = unit(A_UNIT, p, table[s])
                    split_lo(sl, n)

            for s in range(3, 10):
                if s < 8:
                    a_rope(0, s)
                lo_after(0, s, {4: 2, 9: 4})
            for p in range(1, PAIRS):
                for s in range(10):
                    if s == 0 and p > 1:
                        a_rsqrt(p - 2, 7)
                    if s >= 3:
                        a_rsqrt(p - 1, s - 3)
                    if 3 <= s < 8:
                        a_rope(p, s)
                    lo_after(p, s, A_LO)
            for s in range(10):
                if s == 0:
                    a_rsqrt(PAIRS - 2, 7)
                if s >= 3:
                    a_rsqrt(PAIRS - 1, s - 3)
                lo_after(PAIRS, s, {2: 1, 4: 2, 6: 3, 8: 4})
            a_rsqrt(PAIRS - 1, 7)
            for n in range(M_UNIT + 1, N_UNIT):
                split_lo(n % 2, n)


_INS = ["x", "c", "ctx", "c_ctx", "w_mod", "b_mod", "norm_gain", "w_in", "q_norm_gain", "k_norm_gain",
        "lambda_q1", "lambda_k1", "lambda_q2", "lambda_k2", "subln_gain", "hgrn_lb_fwd", "hgrn_lb_bwd",
        "hgrn_norm_gain", "w_br_attn", "w_br_hgrn", "w_out"]


def shape_constants():
    import numpy as np
    i = np.arange(CH)
    masks = np.zeros((CH, LEVELS + 1, CH), np.int32)
    masks[:, 0, :] = i[:, None] == i[None, :]
    for l in range(LEVELS):
        masks[:, l + 1, :] = ((i[:, None] >> (l + 1)) == (i[None, :] >> (l + 1))) & \
            ((i[:, None] >> l) != (i[None, :] >> l))
    row = np.repeat(np.arange(TL // GRID_W, dtype=np.float32), GRID_W)
    col = np.tile(np.arange(GRID_W, dtype=np.float32), TL // GRID_W)
    half = DH // 2
    inv = (10000.0 ** (-np.arange(0, half, 2, dtype=np.float32) / half)).astype(np.float32)
    ar, ac = row[:, None] * inv[None, :], col[:, None] * inv[None, :]
    ang = np.concatenate([ar, ar, ac, ac], axis=-1).astype(np.float32)
    sign = np.repeat(np.array([-1, 1, -1, 1], np.float32), DH // 4)
    return {"ident": np.eye(P, dtype=np.float32), "masks": masks,
            "cos": np.cos(ang).astype(np.float32), "sin": (np.sin(ang) * sign).astype(np.float32)}


def kernel(**inputs):
    import numpy as _np
    import concourse.bacc as _bacc
    from concourse import mybir as _mybir
    from concourse.bass_utils import run_bass_kernel_spmd as _run

    nc = _bacc.Bacc("TRN2", target_bir_lowering=False, num_devices=1)
    arrays, args = {}, {}
    for name, value in [(n, inputs[n]) for n in _INS] + list(shape_constants().items()):
        v = _np.ascontiguousarray(value)
        arrays[f"in_{name}_dram"] = v
        args[name] = nc.dram_tensor(f"in_{name}_dram", v.shape, _mybir.dt.from_np(v.dtype), kind="ExternalInput").ap()
    out = nc.dram_tensor("out_0_dram", (1, TL, D), _mybir.dt.float32, kind="ExternalOutput").ap()
    hybrid_layer(nc, args, out)
    r = _run(nc, [arrays], core_ids=[0])
    return r.results[0]["out_0_dram"]
```
